# Optimizing a Trainium2 kernel written in Bass

```python
import jax, jax.numpy as jnp
from jax import lax
import numpy as np

D_MODEL = 1024
BATCH = 1
SEQ = 512
DEPTH = 2
DEC_BATCH = 8
DEC_SEQ = 1
PAST_LEN = 4096
PAGE_SIZE = 128

D_MIX = D_MODEL
POOL_WIDTH = D_MIX // 4
POOL_WINDOWS = (2, 4, 8, 16)
POOL_GROUPS = len(POOL_WINDOWS)
POOL_GROUP_DIM = POOL_WIDTH // POOL_GROUPS
POOL_STATE = max(POOL_WINDOWS) - 1
MLSTM_WIDTH = D_MIX // 2
MLSTM_HEADS = 4
MLSTM_HEAD_DIM = MLSTM_WIDTH // MLSTM_HEADS
MLSTM_CHUNK = 128
GMLP_WIDTH = D_MIX // 4
GMLP_GROUPS = 4
GMLP_GROUP_DIM = GMLP_WIDTH // GMLP_GROUPS
GMLP_CHUNK = 128
D_IN = POOL_WIDTH + 4 * MLSTM_WIDTH + 2 * MLSTM_HEADS + 2 * GMLP_WIDTH
D_FF = 2816
N_EXPERTS = 8
TOP_K = 2
D_FF_EXPERT = 1408
PLE_DIM = 256
N_DENSE = (DEPTH + 1) // 2
N_MOE = DEPTH // 2
RMS_EPS = 1e-6

kernel_name = "hybrid_pool_mlstm_gmlp_decoder_step"

def _rms_norm(x, w):
    xf = x.astype(jnp.float32)
    y = xf * lax.rsqrt(jnp.mean(xf * xf, axis=-1, keepdims=True) + RMS_EPS)
    return (y * w.astype(jnp.float32)).astype(x.dtype)

def _pool_mixer(u_prev, u, start_pos, pool_w, pool_scale):
    B, L, _ = u.shape
    n_prev = u_prev.shape[1]
    ext = jnp.concatenate([u_prev.astype(u.dtype), u], axis=1)
    L_ext = ext.shape[1]
    pos = start_pos - n_prev + jnp.arange(L_ext)
    ext_f = ext.astype(jnp.float32)
    cs = jnp.cumsum(ext_f, axis=1)
    outs = []
    for g, w in enumerate(POOL_WINDOWS):
        sl = slice(g * POOL_GROUP_DIM, (g + 1) * POOL_GROUP_DIM)
        csg = cs[..., sl]
        shifted = jnp.pad(csg, ((0, 0), (w, 0), (0, 0)))[:, :L_ext]
        cnt = jnp.minimum(w, pos + 1).astype(jnp.float32)
        outs.append((csg - shifted) / cnt[None, :, None] - ext_f[..., sl])
    pooled = jnp.stack(outs, axis=2)[:, n_prev:]
    y = jnp.einsum('blgc,gcd->blgd', pooled, pool_w.astype(jnp.float32)).reshape(B, L, POOL_WIDTH)
    y = y * pool_scale.astype(jnp.float32)
    return y.astype(u.dtype), ext[:, -POOL_STATE:]

def _mlstm_chunk(carry, xs):
    C, n, m = carry
    q, k, v, ig, lf = xs
    c = q.shape[1]
    b = jnp.cumsum(lf, axis=1)
    causal = jnp.tril(jnp.ones((c, c), dtype=bool))
    dmat = b[:, :, None, :] - b[:, None, :, :] + ig[:, None, :, :]
    dmat = jnp.where(causal[None, :, :, None], dmat, -jnp.inf)
    g = b + m[:, None, :]
    m_t = jnp.maximum(g, jnp.max(dmat, axis=2))
    wts = jnp.exp(dmat - m_t[:, :, None, :]) * jnp.einsum('bthd,bshd->btsh', q, k)
    inter = jnp.exp(g - m_t)
    num = inter[..., None] * jnp.einsum('bthk,bhkv->bthv', q, C) + jnp.einsum('btsh,bshv->bthv', wts, v)
    den = inter * jnp.einsum('bthk,bhk->bth', q, n) + jnp.sum(wts, axis=2)
    h = num / jnp.maximum(jnp.abs(den), jnp.exp(-m_t))[..., None]
    m_new = m_t[:, -1]
    decay = jnp.exp(b[:, -1] + m - m_new)
    w_s = jnp.exp(b[:, -1:] - b + ig - m_new[:, None])
    C_new = decay[..., None, None] * C + jnp.einsum('bsh,bshk,bshv->bhkv', w_s, k, v)
    n_new = decay[..., None] * n + jnp.einsum('bsh,bshk->bhk', w_s, k)
    return (C_new, n_new, m_new), h

def _mlstm(q, k, v, ig, lf, C, n, m):
    B, L, H, Dh = q.shape
    c = MLSTM_CHUNK if L % MLSTM_CHUNK == 0 else L
    nc = L // c

    def to_chunks(a):
        return jnp.moveaxis(a.reshape((B, nc, c) + a.shape[2:]), 1, 0)

    (C, n, m), h = lax.scan(_mlstm_chunk, (C, n, m), tuple(to_chunks(a) for a in (q, k, v, ig, lf)))
    h = jnp.moveaxis(h, 0, 1).reshape(B, L, H, Dh)
    return h, C, n, m

def _gmlp(u, v, norm_w, ws, bs):
    B, L, _ = u.shape
    vn = _rms_norm(v.reshape(B, L, GMLP_GROUPS, GMLP_GROUP_DIM), norm_w.reshape(GMLP_GROUPS, GMLP_GROUP_DIM))
    c = min(GMLP_CHUNK, L)
    vc = vn.reshape(B, L // c, c, GMLP_GROUPS, GMLP_GROUP_DIM)
    wm = jnp.tril(ws[:, :c, :c])
    mixed = jnp.einsum('gts,bnsgd->bntgd', wm, vc) + bs[:, :c].T[None, None, :, :, None]
    y = u.reshape(B, L // c, c, GMLP_GROUPS, GMLP_GROUP_DIM) * mixed
    return y.reshape(B, L, GMLP_WIDTH).astype(u.dtype), vn.reshape(B, L, GMLP_WIDTH)

def _swiglu(h, wg, wu, wd):
    return (jax.nn.silu(h @ wg) * (h @ wu)) @ wd

def _moe(h, router_w, router_b, wg, wu, wd):
    logits = (h @ router_w).astype(jnp.float32) + router_b.astype(jnp.float32)
    probs = jax.nn.softmax(logits, axis=-1)
    top_p, top_i = lax.top_k(probs, TOP_K)
    top_p = top_p / jnp.sum(top_p, axis=-1, keepdims=True)
    gates = jnp.sum(jax.nn.one_hot(top_i, N_EXPERTS, dtype=jnp.float32) * top_p[..., None], axis=-2)
    y = jnp.zeros(h.shape, jnp.float32)
    for e in range(N_EXPERTS):
        y = y + gates[..., e:e + 1] * _swiglu(h, wg[e], wu[e], wd[e]).astype(jnp.float32)
    return y.astype(h.dtype)

def _mixer(h, i, W, pool_prev, C, n, m, start_pos):
    B, L, _ = h.shape
    z = h @ W['w_in'][i]
    sizes = [POOL_WIDTH, MLSTM_WIDTH, MLSTM_WIDTH, MLSTM_WIDTH, MLSTM_WIDTH,
             MLSTM_HEADS, MLSTM_HEADS, GMLP_WIDTH, GMLP_WIDTH]
    cuts = [int(s) for s in np.cumsum(sizes)[:-1]]
    u_pool, q, k, v, o, ig, fg, gu, gv = jnp.split(z, cuts, axis=-1)
    y_pool, pool_new = _pool_mixer(pool_prev, u_pool, start_pos, W['pool_w'][i], W['pool_scale'][i])
    f32 = jnp.float32
    shp = (B, L, MLSTM_HEADS, MLSTM_HEAD_DIM)
    qh = q.astype(f32).reshape(shp)
    kh = k.astype(f32).reshape(shp) * (MLSTM_HEAD_DIM ** -0.5)
    vh = v.astype(f32).reshape(shp)
    ig_t = ig.astype(f32) + W['mlstm_b_i'][i].astype(f32)
    lf_t = jax.nn.log_sigmoid(fg.astype(f32) + W['mlstm_b_f'][i].astype(f32))
    hm, C_new, n_new, m_new = _mlstm(qh, kh, vh, ig_t, lf_t, C.astype(f32), n.astype(f32), m.astype(f32))
    hm = _rms_norm(hm, W['mlstm_norm_w'][i].reshape(MLSTM_HEADS, MLSTM_HEAD_DIM)).reshape(B, L, MLSTM_WIDTH)
    y_m = (jax.nn.sigmoid(o.astype(f32)) * hm).astype(h.dtype)
    y_g, gv_rows = _gmlp(gu, gv, W['gmlp_norm_w'][i], W['gmlp_ws'][i], W['gmlp_bs'][i])
    out = jnp.concatenate([y_pool, y_m, y_g], axis=-1) @ W['w_out'][i]
    return out, pool_new, C_new, n_new, m_new, gv_rows

def _trunk(x, p, pool_prev, C0, n0, m0, start_pos, W):
    pools, Cs, ns, ms, gvs = [], [], [], [], []
    for i in range(DEPTH):
        h = _rms_norm(x, W['norm_mix_pre'][i])
        mix, pool_new, C_new, n_new, m_new, gv_rows = _mixer(h, i, W, pool_prev[i], C0[i], n0[i], m0[i], start_pos)
        x = x + _rms_norm(mix, W['norm_mix_post'][i])
        h = _rms_norm(x, W['norm_ffn_pre'][i])
        if i % 2 == 0:
            j = i // 2
            f = _swiglu(h, W['ffn_w_gate'][j], W['ffn_w_up'][j], W['ffn_w_down'][j])
        else:
            j = i // 2
            f = _moe(h, W['moe_router_w'][j], W['moe_router_b'][j], W['moe_w_gate'][j], W['moe_w_up'][j], W['moe_w_down'][j])
        x = x + _rms_norm(f, W['norm_ffn_post'][i])
        gate = jax.nn.sigmoid(_rms_norm(x, W['norm_ple'][i]) @ W['ple_w_gate'][i])
        x = x + gate * (p[i].astype(x.dtype) @ W['ple_w_proj'][i])
        pools.append(pool_new); Cs.append(C_new); ns.append(n_new); ms.append(m_new); gvs.append(gv_rows)
    return x, jnp.stack(pools), jnp.stack(Cs), jnp.stack(ns), jnp.stack(ms), jnp.stack(gvs)

def setup_inputs(seed: int = 0) -> dict:
    key = jax.random.key(seed)
    ks = iter(jax.random.split(key, 64))
    nrm = lambda shape, s=1.0: jax.random.normal(next(ks), shape, jnp.float32) * s
    gain = lambda shape: 1.0 + nrm(shape, 0.1)
    H, Dh = MLSTM_HEADS, MLSTM_HEAD_DIM
    return {
        'x_prompt': nrm((BATCH, SEQ, D_MODEL)),
        'x_sample': nrm((DEC_BATCH, DEC_SEQ, D_MODEL)),
        'state_pool': nrm((DEPTH, DEC_BATCH, POOL_STATE, POOL_WIDTH)),
        'state_mlstm_C': nrm((DEPTH, DEC_BATCH, H, Dh, Dh), 0.1),
        'state_mlstm_n': nrm((DEPTH, DEC_BATCH, H, Dh), 0.3),
        'state_mlstm_m': nrm((DEPTH, DEC_BATCH, H), 0.5),
        'p_prompt': nrm((DEPTH, BATCH, SEQ, PLE_DIM)),
        'p_sample': nrm((DEPTH, DEC_BATCH, DEC_SEQ, PLE_DIM)),
        'norm_mix_pre': gain((DEPTH, D_MODEL)),
        'norm_mix_post': gain((DEPTH, D_MODEL)),
        'norm_ffn_pre': gain((DEPTH, D_MODEL)),
        'norm_ffn_post': gain((DEPTH, D_MODEL)),
        'norm_ple': gain((DEPTH, D_MODEL)),
        'w_in': nrm((DEPTH, D_MODEL, D_IN), D_MODEL ** -0.5),
        'pool_w': nrm((DEPTH, POOL_GROUPS, POOL_GROUP_DIM, POOL_GROUP_DIM), POOL_GROUP_DIM ** -0.5),
        'pool_scale': gain((DEPTH, POOL_WIDTH)),
        'mlstm_b_i': nrm((DEPTH, H), 0.1),
        'mlstm_b_f': jnp.linspace(3.0, 6.0, H, dtype=jnp.float32)[None, :] + nrm((DEPTH, H), 0.1),
        'mlstm_norm_w': gain((DEPTH, MLSTM_WIDTH)),
        'gmlp_norm_w': gain((DEPTH, GMLP_WIDTH)),
        'gmlp_ws': nrm((DEPTH, GMLP_GROUPS, GMLP_CHUNK, GMLP_CHUNK), 0.5 * GMLP_CHUNK ** -0.5),
        'gmlp_bs': 1.0 + nrm((DEPTH, GMLP_GROUPS, GMLP_CHUNK), 0.1),
        'w_out': nrm((DEPTH, D_MIX, D_MODEL), D_MIX ** -0.5),
        'ffn_w_gate': nrm((N_DENSE, D_MODEL, D_FF), D_MODEL ** -0.5),
        'ffn_w_up': nrm((N_DENSE, D_MODEL, D_FF), D_MODEL ** -0.5),
        'ffn_w_down': nrm((N_DENSE, D_FF, D_MODEL), D_FF ** -0.5),
        'moe_router_w': nrm((N_MOE, D_MODEL, N_EXPERTS), D_MODEL ** -0.5),
        'moe_router_b': nrm((N_MOE, N_EXPERTS), 0.01),
        'moe_w_gate': nrm((N_MOE, N_EXPERTS, D_MODEL, D_FF_EXPERT), D_MODEL ** -0.5),
        'moe_w_up': nrm((N_MOE, N_EXPERTS, D_MODEL, D_FF_EXPERT), D_MODEL ** -0.5),
        'moe_w_down': nrm((N_MOE, N_EXPERTS, D_FF_EXPERT, D_MODEL), D_FF_EXPERT ** -0.5),
        'ple_w_gate': nrm((DEPTH, D_MODEL, D_MODEL), D_MODEL ** -0.5),
        'ple_w_proj': nrm((DEPTH, PLE_DIM, D_MODEL), PLE_DIM ** -0.5),
    }

def reference(x_prompt, x_sample, state_pool, state_mlstm_C, state_mlstm_n, state_mlstm_m, p_prompt, p_sample,
              norm_mix_pre, norm_mix_post, norm_ffn_pre, norm_ffn_post, norm_ple, w_in, pool_w, pool_scale,
              mlstm_b_i, mlstm_b_f, mlstm_norm_w, gmlp_norm_w, gmlp_ws, gmlp_bs, w_out,
              ffn_w_gate, ffn_w_up, ffn_w_down, moe_router_w, moe_router_b, moe_w_gate, moe_w_up, moe_w_down,
              ple_w_gate, ple_w_proj):
    W = dict(norm_mix_pre=norm_mix_pre, norm_mix_post=norm_mix_post, norm_ffn_pre=norm_ffn_pre,
             norm_ffn_post=norm_ffn_post, norm_ple=norm_ple, w_in=w_in, pool_w=pool_w, pool_scale=pool_scale,
             mlstm_b_i=mlstm_b_i, mlstm_b_f=mlstm_b_f, mlstm_norm_w=mlstm_norm_w, gmlp_norm_w=gmlp_norm_w,
             gmlp_ws=gmlp_ws, gmlp_bs=gmlp_bs, w_out=w_out, ffn_w_gate=ffn_w_gate, ffn_w_up=ffn_w_up,
             ffn_w_down=ffn_w_down, moe_router_w=moe_router_w, moe_router_b=moe_router_b,
             moe_w_gate=moe_w_gate, moe_w_up=moe_w_up, moe_w_down=moe_w_down,
             ple_w_gate=ple_w_gate, ple_w_proj=ple_w_proj)
    H, Dh = MLSTM_HEADS, MLSTM_HEAD_DIM
    B = x_prompt.shape[0]
    pool0 = jnp.zeros((DEPTH, B, 0, POOL_WIDTH), x_prompt.dtype)
    C0 = jnp.zeros((DEPTH, B, H, Dh, Dh), jnp.float32)
    n0 = jnp.zeros((DEPTH, B, H, Dh), jnp.float32)
    m0 = jnp.zeros((DEPTH, B, H), jnp.float32)
    y_prompt, pool_p, C_p, n_p, m_p, _gv_p = _trunk(x_prompt, p_prompt, pool0, C0, n0, m0, 0, W)
    y_sample, pool_s, C_s, n_s, m_s, gv_s = _trunk(x_sample, p_sample, state_pool, state_mlstm_C,
                                                  state_mlstm_n, state_mlstm_m, PAST_LEN, W)
    return (y_prompt, y_sample, pool_p, C_p, n_p, m_p, pool_s, C_s, n_s, m_s, gv_s)


_drawn_inputs = setup_inputs


def setup_inputs(seed=0):
    import zlib

    import numpy as np

    out = dict(_drawn_inputs(seed))
    spreads = {}
    factors = {}
    for name, (base, spread) in spreads.items():
        noise = np.random.default_rng([zlib.crc32(name.encode()), seed]).standard_normal(out[name].shape)
        drawn = base * np.exp(spread * noise) if base else spread * noise
        out[name] = __import__('jax').numpy.asarray(drawn.astype(out[name].dtype))
    for name, factor in factors.items():
        out[name] = (out[name] * factor).astype(out[name].dtype)
    return out
```

```python
import concourse.bass as bass
from concourse import mybir
from contextlib import ExitStack

f32 = mybir.dt.float32
f32r = mybir.dt.float32r
u32 = mybir.dt.uint32
ACT = mybir.ActivationFunctionType
ALU = mybir.AluOpType
AXX = mybir.AxisListType.X

P = 128
DEPTH, DM, SEQ, NB = 2, 1024, 512, 8
TOK = SEQ + NB
HALF = TOK // 2
DC = DM // P
TT = SEQ // P
H, DH = 4, 128
NE, FS = 8, 1408
FCH = FS // P
KMAX = FCH
EPS = 1e-6
QS = float(DH) ** -0.5
PLE = 256
WINDOWS = (2, 4, 8, 16)
PST = 15
D_IN = 2824
GATE_COL = 2304
GW = 36
Z_POOL, Z_Q, Z_K, Z_V, Z_O, Z_GU, Z_GV = 0, 2, 6, 10, 14, 18, 20
WIN_P, WOUT_P, GU_P, DOWN_P, PLE_P = 11, 4, 11, 4, 8
SLICES = (2, NE)


def win_base(L):
    return 0 if L == 0 else ple_base(0) + PLE_P


def wout_base(L):
    return win_base(L) + WIN_P


def ffn_base(L):
    return wout_base(L) + WOUT_P


def ple_base(L):
    return ffn_base(L) + SLICES[L] * (GU_P + DOWN_P)


LAST_PAIR = ple_base(DEPTH - 1) + PLE_P - 1
MIX_PRE, MIX_POST, FFN_PRE, FFN_POST, PLE_PRE = range(5)
R_F, R_IG, R_EM, R_G, R_M, R_A = range(6)
C_ID, C_BLK, C_TRI, C_ONE, C_MEAN, C_MEANH, C_INVW, C_RC = 0, 128, 256, 384, 385, 386, 387, 389
NCONST = C_RC + 2 * 16


def build(nc, A, O):
    ctx = ExitStack()
    with ctx:
        def sb(name, shape, dt=f32):
            return ctx.enter_context(nc.sbuf_tensor(name, shape, dt))

        def sem(name):
            return ctx.enter_context(nc.semaphore(name))

        x = sb("x", [P, DC, TOK])
        zreg = sb("zreg", [P, 23 * TOK])
        z = zreg[:, :].rearrange("p (c t) -> p c t", t=TOK)
        acc = z[:, 0:8]
        sq = z[:, 8:12]
        ht = z[:, 12:14]
        rn = z[:, 14]
        sg = z[:, 15]
        gt = z[:, 16]
        ut = z[:, 17:19]
        p_tok = zreg[:, 19 * TOK:19 * TOK + 5 * PLE].rearrange("p (t c) -> p t c", c=PLE)
        gb = z[:, 22]
        x_tok = zreg[:, 0:5 * DM].rearrange("p (t c) -> p t c", c=DM)
        y_tok = zreg[:, 0:2 * DM].rearrange("p (t c) -> p t c", c=DM)
        with nc.sbuf_tensor("h_hi", [P, DC, TOK], f32r) as h_hi, \
                nc.sbuf_tensor("h_lo", [P, DC, TOK], f32r) as h_lo:
            pass
        ra = sb("region_a", [P, 2 * DC * TOK])
        with nc.sbuf_tensor("gu_hi", [P, FCH, TOK], f32r) as gu_hi, \
                nc.sbuf_tensor("gu_lo", [P, FCH, TOK], f32r) as gu_lo:
            pass
        y_hi = sb("y_hi", [P, DC, TOK], f32r)
        y_lo = sb("y_lo", [P, DC, TOK], f32r)
        rb = sb("region_b", [P, 2 * (FCH - DC) * TOK])
        EXT = PST + SEQ
        with nc.sbuf_tensor("p_hi", [P, 2, TOK], f32r) as p_hi, \
                nc.sbuf_tensor("p_lo", [P, 2, TOK], f32r) as p_lo:
            pass
        rc = sb("region_c", [P, 2, 2, EXT])
        wst = sb("wst", [P, 2, KMAX * P])
        whi = sb("whi", [P, 2, KMAX * P], f32r)
        wlo = sb("wlo", [P, 2, KMAX * P], f32r)
        rows = sb("rows", [H, 6, TOK])
        const = sb("const", [P, NCONST])
        cols = sb("cols", [P, 96])
        colrows = sb("colrows", [96, P])
        gwf = sb("gwf", [P, DC * GW + 92])
        gwh = sb("gwh", [P, DC * GW + 92], f32r)
        gwl = sb("gwl", [P, DC * GW + 92], f32r)
        bdw = sb("bdw", [P, 2, P])
        gate_b = sb("gate_b", [H, 2, DEPTH])
        sg_b = sb("sg_b", [P, 2, DEPTH, 2])
        bsr = sb("bsr", [4, DEPTH, P])
        m0 = sb("m0", [H, DEPTH, NB])
        tsm = sb("tsm", [H, NB])
        epsc = sb("epsc", [P, 1])
        rwf = sb("rwf", [P, DC, NE])
        rwh = sb("rwh", [P, DC, NE], f32r)
        rwl = sb("rwl", [P, DC, NE], f32r)
        rbias = sb("rbias", [P, NE])
        lg = sb("lg", [P, 5, NE])
        top = sb("top", [P, 5, 8])
        topi = sb("topi", [P, 5, 8], u32)
        topf = sb("topf", [P, 5, 8])
        gwt = sb("gwt", [P, 5, 2])
        gatet = sb("gatet", [P, 5, NE])
        gtmp = sb("gtmp", [P, 5, NE])
        iota8 = sb("iota8", [P, NE])
        grow = sb("grow", [NE, TOK])

        def view(region, at, *shape):
            n = 1
            for s in shape:
                n *= s
            v = region[:, at:at + n]
            if len(shape) == 2:
                v = v.rearrange("p (a b) -> p a b", b=shape[1])
            if len(shape) == 3:
                v = v.rearrange("p (a b c) -> p a b c", b=shape[1], c=shape[2])
            return v, at + n

        vtok, a = view(ra, 0, TT, 129)
        ktok, a = view(ra, a, TT, P)
        kw, a = view(ra, a, TT, P)
        E, a = view(ra, a, 2, SEQ)
        W, a = view(ra, a, 2, SEQ)
        a_nd = a
        num, a = view(ra, a, H, TOK)
        D, a = view(ra, a, H, TOK)
        Cout, a = view(ra, a, 129)
        acol, a = view(ra, a, TT, H)
        kws, a = view(ra, a, H, NB)
        dcs, a = view(ra, a, H, 3, NB)
        nT, a = view(ra, a, NB, H)
        nn, a = view(ra, a, NB, H)
        qn, a = view(ra, a, H, NB)
        assert a <= 2 * DC * TOK
        wsr, a = view(ra, a_nd, 4, P)
        wmT, a = view(ra, a, 4, P)
        vnt, a = view(ra, a, 2, TT, P)
        assert a <= a_nd + H * TOK
        gsq, a = view(ra, a_nd + H * TOK, 2, TOK)
        gr, a = view(ra, a, 2, TOK)
        Cb, a = view(rb, 0, 3, H, P)
        Ct, a = view(rb, a, H, P)
        vs, a = view(rb, a, H, P)
        us, a = view(rb, a, 2, P)
        nst, a = view(rb, a, P)
        nout, a = view(rb, a, P)
        assert a <= 2 * (FCH - DC) * TOK
        pst = Ct[:, :, :].rearrange("p a b -> p (a b)")[:, 0:256]
        gvo = Ct[:, :, :].rearrange("p a b -> p (a b)")[:, 256:512]
        hs1, hs2 = E[:, :, :].rearrange("p a b -> p (a b)"), W[:, :, :].rearrange("p a b -> p (a b)")

        ident = const[:, C_ID:C_ID + P]
        blk = const[:, C_BLK:C_BLK + P]
        tri = const[:, C_TRI:C_TRI + P]
        one = const[:, C_ONE:C_ONE + 1]

        def bcol(c):
            return const[:, c:c + 1].to_broadcast([P, P])

        def pick(k, n, m=P):
            return const[0:k, n:n + 1].to_broadcast([k, m])

        def two(ap):
            return ap.rearrange("p (a b) -> p a b", b=HALF)

        lin = ctx.enter_context(nc.psum_tensor("lin", [P, 4, 512], f32))
        aux = ctx.enter_context(nc.psum_tensor("aux", [P, 4, 512], f32))

        staged = [sem("staged0"), sem("staged1")]
        hi_done, lo_done = sem("hi_done"), sem("lo_done")
        pe_slab = sem("pe_slab")
        pair_free = [sem("pair_free0"), sem("pair_free1")]
        x_in, c_in, w_small = sem("x_in"), sem("c_in"), sem("w_small")
        setup_pool = sem("setup_pool")
        cols_t, cols_ok = sem("cols_t"), sem("cols_ok")
        x_t, x_ok, xs_t = sem("x_t"), sem("x_ok"), sem("xs_t")
        sq_ready, sq_used, stats = sem("sq_ready"), sem("sq_used"), sem("stats")
        r_ready = sem("r_ready")
        ht_ready, h_hi_ok, h_ready = sem("ht_ready"), sem("h_hi_ok"), sem("h_ready")
        ut_ready, x_upd, ple_x = sem("ut_ready"), sem("x_upd"), sem("ple_x")
        gw_in, gw_ok, gw_lo = sem("gw_in"), sem("gw_ok"), sem("gw_lo")
        gates = sem("gates")
        gate_l1, gate_lf, gate_scan, gate_g, gate_em = (sem(s) for s in
                                                        ("gate_l1", "gate_lf", "gate_scan", "gate_g", "gate_em"))
        lay_in = sem("lay_in")
        pw_zero = sem("pw_zero")
        m_out = sem("m_out")
        pool_win, pool_t, pool_v, pool_y = sem("pool_win"), sem("pool_t"), sem("pool_v"), sem("pool_y")
        pool_mm, pool_e = sem("pool_mm"), sem("pool_e")
        g_sq, g_mean, g_r, g_vn, g_t, g_ev, g_wm, g_wt, g_mix, g_y = (
            sem(s) for s in ("g_sq", "g_mean", "g_r", "g_vn", "g_t", "g_ev", "g_wm", "g_wt", "g_mix", "g_y"))
        acol_t, acol_ok = sem("acol_t"), sem("acol_ok")
        st_t, st_ev, st_k, st_den, st_de, st_dd = (sem(s) for s in ("st_t", "st_ev", "st_k", "st_den", "st_de", "st_dd"))
        C_in = [sem(f"C_in{i}") for i in range(3)]
        C_st = sem("C_st")
        vb_ready, ct_ready, cn_ready, cq_done = sem("vb_ready"), sem("ct_ready"), sem("cn_ready"), sem("cq_done")
        st_num = sem("st_num")
        kv_t, kv_ev, gb_ready, e_ready, e_mask, s_ready, w_ready, w_used = (
            sem(s) for s in ("kv_t", "kv_ev", "gb_ready", "e_ready", "e_mask", "s_ready", "w_ready", "w_used"))
        nd_ready, nd_ev, nd_max, kw_ready, c_ready, c_ev, c_out = (
            sem(s) for s in ("nd_ready", "nd_ev", "nd_max", "kw_ready", "c_ready", "c_ev", "c_out"))
        hq, hm, hd2, ha, hr, hy, hy2 = (sem(s) for s in ("hq", "hm", "hd2", "ha", "hr", "hy", "hy2"))
        sig_o, y_hi_ok, y_ok = sem("sig_o"), sem("y_hi_ok"), sem("y_ok")
        p_in, p_t, p_hi_ok, p_ok = sem("p_in"), sem("p_t"), sem("p_hi_ok"), sem("p_ok")
        gt_ready, gu_hi_ok, gu_ok = sem("gt_ready"), sem("gu_hi_ok"), sem("gu_ok")
        acc0 = sem("acc0")
        rw_ok, rw_lo, rt_lg, rt_max, rt_e, rt_gate, rt_t, rt_row, gb_mm, gb_ok = (
            sem(s) for s in ("rw_ok", "rw_lo", "rt_lg", "rt_max", "rt_e", "rt_gate", "rt_t", "rt_row", "gb_mm", "gb_ok"))
        yt_t, yt_ev, out_st = sem("yt_t"), sem("yt_ev"), sem("out_st")
        y_st = [sem("y_st0"), sem("y_st1")]
        ctx.enter_context(nc.allow_non_contiguous_dma(reason="per-head rows and state columns are a few words each"))
        block = ctx.enter_context(nc.Block())

        def kcs(phase):
            return {"win": (8, 8), "wout": (8, 8), "gu": (8, 8), "down": (11, 11), "ple": (8, 2)}[phase]

        def phases(L):
            yield "win", win_base(L), WIN_P, 8
            yield "wout", wout_base(L), WOUT_P, 8

        @block.sync
        def _(sp):
            tokp = A["x_prompt"][0].rearrange("(t p) c -> p t c", p=P)
            for t in range(TT):
                sp.dma_start(x_tok[:, t, :], tokp[:, t, :]).then_inc(x_in, 16)
            sp.dma_start(x_tok[0:NB, TT, :], A["x_sample"][:, 0, :]).then_inc(x_in, 16)

            def load(q, s, src, kc, n):
                if not (isinstance(q, int) and q == 0):
                    sp.wait_ge(hi_done, q * 2 + (s - 1))
                    sp.wait_ge(lo_done, q * 2 + (s - 1))
                sp.dma_start(wst[:, s, 0:kc * n].rearrange("p (k n) -> p k n", n=n), src).then_inc(staged[s], 16)

            def cut(w, c):
                return w.rearrange("(k p) n -> p k n", p=P)[:, :, bass.ds(c, P)]

            for L in range(DEPTH):
                w_in = A["w_in"][L]
                b = win_base(L)
                if L == 0:
                    for s in range(2):
                        load(0, s, cut(w_in, s * P), DC, P)
                with sp.Fori(1 if L == 0 else 0, Z_GU // 2) as i:
                    for s in range(2):
                        load(i + b, s, cut(w_in, i * 2 * P + s * P), DC, P)
                for i in range(Z_GU // 2, WIN_P):
                    for s in range(2):
                        load(i + b, s, cut(w_in, (2 * i + s) * P + 2 * H), DC, P)
                with sp.Fori(0, WOUT_P) as i:
                    for s in range(2):
                        load(i + wout_base(L), s, cut(A["w_out"][L], i * 2 * P + s * P), DC, P)
                if L == 0:
                    for e in range(SLICES[0]):
                        with sp.Fori(0, GU_P) as i:
                            for s, w in enumerate(("ffn_w_gate", "ffn_w_up")):
                                load(i + ffn_base(0) + e * (GU_P + DOWN_P), s, cut(A[w][0], i * P + e * FS), DC, P)
                        with sp.Fori(0, DOWN_P) as i:
                            for s in range(2):
                                load(i + ffn_base(0) + e * (GU_P + DOWN_P) + GU_P, s,
                                     cut(A["ffn_w_down"][0, e * FS:(e + 1) * FS], i * 2 * P + s * P), FCH, P)
                else:
                    with sp.Fori(0, NE) as e:
                        def expert(w):
                            return A[w][0][bass.ds(e, 1)].rearrange("a (k p) n -> p (a k) n", p=P)
                        with sp.Fori(0, GU_P) as i:
                            for s, w in enumerate(("moe_w_gate", "moe_w_up")):
                                load(i + (e * (GU_P + DOWN_P) + ffn_base(1)), s,
                                     expert(w)[:, :, bass.ds(i * P, P)], DC, P)
                        with sp.Fori(0, DOWN_P) as i:
                            for s in range(2):
                                load(i + (e * (GU_P + DOWN_P) + (ffn_base(1) + GU_P)), s,
                                     expert("moe_w_down")[:, :, bass.ds(i * 2 * P + s * P, P)], FCH, P)
                with sp.Fori(0, PLE_P) as i:
                    load(i + ple_base(L), 0, cut(A["ple_w_gate"][L], i * P), DC, P)
                    load(i + ple_base(L), 1, cut(A["ple_w_proj"][L], i * P), 2, P)
            for t in range(TT + 1):
                sp.wait_ge(yt_ev, t + 1)
                if t < TT:
                    sp.dma_start(O["y_prompt"][0, t * P:(t + 1) * P, :], y_tok[:, t % 2, :]).then_inc(y_st[t % 2], 16)
                else:
                    sp.dma_start(O["y_sample"][:, 0, :], y_tok[0:NB, t % 2, :]).then_inc(y_st[t % 2], 16)
            sp.wait_ge(y_st[0], 16 * 3)
            sp.wait_ge(y_st[1], 16 * 2)

        @block.gpsimd
        def _(pool):
            pool.dma_start(const[:, :], A["shape_constants"]).then_inc(c_in, 16)
            for n, w in enumerate(("norm_mix_pre", "norm_mix_post", "norm_ffn_pre", "norm_ffn_post", "norm_ple")):
                pool.dma_start(colrows[16 * n:16 * n + 16, :],
                               A[w].rearrange("l (c p) -> (l c) p", p=P)).then_inc(c_in, 16)
            pool.dma_start(colrows[80:84, :], A["pool_scale"].rearrange("l (c p) -> (l c) p", p=P)).then_inc(c_in, 16)
            pool.dma_start(colrows[84:92, :], A["mlstm_norm_w"].rearrange("l (c p) -> (l c) p", p=P)).then_inc(c_in, 16)
            pool.dma_start(colrows[92:96, :], A["gmlp_norm_w"].rearrange("l (c p) -> (l c) p", p=P)).then_inc(c_in, 16)
            nsmall = 0
            small = [(gate_b[:, 0, :], A["mlstm_b_i"].rearrange("l h -> h l")),
                     (gate_b[:, 1, :], A["mlstm_b_f"].rearrange("l h -> h l")),
                     (rbias[:, :], A["moe_router_b"][0].partition_broadcast(P)),
                     (bsr[:, :, :], A["gmlp_bs"].rearrange("l g t -> g l t")),
                     (rwf[:, :, :], A["moe_router_w"][0].rearrange("(k p) n -> p k n", p=P))]
            for L in range(DEPTH):
                small.append((m0[:, L, :], A["state_mlstm_m"][L].rearrange("b h -> h b")))
                for g in range(4):
                    at = slice(64 * (g % 2), 64 * (g % 2) + 64)
                    small.append((sg_b[at, 0, L, g // 2:g // 2 + 1], A["gmlp_ws"][L, g, 0, 0:1].partition_broadcast(64)))
                    small.append((sg_b[at, 1, L, g // 2:g // 2 + 1], A["gmlp_bs"][L, g, 0:1].partition_broadcast(64)))
            for dst, src in small:
                pool.dma_start(dst, src).then_inc(w_small, 16)
                nsmall += 16
            pool.memset(gwf[:, :], 0.0)
            pool.memset(epsc[:, :], EPS)
            pool.memset(bdw[:, :, :], 0.0)
            pool.iota(topi[:, 0, :], pattern=[[1, NE]], base=0, channel_multiplier=0)
            pool.drain()
            pool.tensor_copy(iota8[:, :], topi[:, 0, :]).then_inc(setup_pool, 1)
            pool.wait_ge(w_small, nsmall)

            def add_x(N):
                for c in range(DC):
                    pool.wait_ge(ut_ready, N * DC + c + 1)
                    pool.tensor_tensor(x[:, c], x[:, c], ut[:, c % 2], ALU.add).then_inc(x_upd, 1)

            for L in range(DEPTH):
                if L:
                    pool.wait_ge(h_ready, DC * 3 * L)
                pool.wait_ge(setup_pool, 1)
                gsrc = A["w_in"][L].rearrange("(k p) n -> p k n", p=P)
                gdst = gwf[:, 0:DC * GW].rearrange("p (k n) -> p k n", n=GW)
                pool.dma_start(gdst[:, :, 0:H], gsrc[:, :, GATE_COL:GATE_COL + H]).then_inc(gw_in, 16)
                pool.dma_start(gdst[:, :, 32:32 + H], gsrc[:, :, GATE_COL + H:GATE_COL + 2 * H]).then_inc(gw_in, 16)
                for g in range(4):
                    o = 64 * (g % 2)
                    pool.dma_start(bdw[o:o + 64, g // 2, o:o + 64], A["pool_w"][L, g]).then_inc(lay_in, 16)
                if L:
                    pool.wait_ge(pair_free[1], ple_base(0) + 1)
                pool.dma_start(pst[0:NB * PST, :], A["state_pool"][L].rearrange("b r c -> (b r) c")).then_inc(lay_in, 16)
                pool.dma_start(nst[0:NB * H, :], A["state_mlstm_n"][L].rearrange("b h k -> (b h) k")).then_inc(lay_in, 16)
                pool.dma_start(O["new_pool_sample"][L, :, 0:PST - 1, :], A["state_pool"][L, :, 1:PST, :]).then_inc(out_st, 16)
                pool.wait_ge(gate_l1, L + 1)
                pool.tensor_scalar(rows[:, R_F], rows[:, R_F], 0.0, None, ALU.min)
                pool.drain()
                pool.tensor_tensor(rows[:, R_F], rows[:, R_F], rows[:, R_EM], ALU.subtract)
                pool.drain()
                pool.memset(rows[:, R_A], 0.0)
                pool.tensor_tensor(tsm[:, :], rows[:, R_F, SEQ:TOK], m0[:, L, :], ALU.add).then_inc(gate_lf, 1)
                pool.wait_ge(pair_free[1], win_base(L) + WIN_P)
                pool.dma_start(wsr[:, :, :], A["gmlp_ws"][L].rearrange("g t s -> t g s")).then_inc(lay_in, 16)
                for b in range(3):
                    pool.dma_start(Cb[:, b], A["state_mlstm_C"][L, b].rearrange("h k v -> k h v")).then_inc(C_in[b], 16)
                pool.memset(rc[:, :, :, 0:PST], 0.0)
                pool.tensor_copy(rc[:, 0, :, PST:EXT], z[:, Z_POOL:Z_POOL + 2, 0:SEQ])
                pool.drain()
                src = 0
                for g, w in enumerate(WINDOWS):
                    sh = w // 2
                    lo = 64 if g % 2 else 0
                    j = g // 2
                    pool.tensor_tensor(rc[:, 1 - src, :, PST:EXT], rc[:, src, :, PST:EXT],
                                       rc[:, src, :, PST - sh:EXT - sh], ALU.add)
                    pool.drain()
                    src = 1 - src
                    s_ = rc[lo:lo + 64, src, j, PST:EXT]
                    zz = z[lo:lo + 64, Z_POOL + j, 0:SEQ]
                    pool.tensor_tensor(gsq[lo:lo + 64, j, 0:16], s_[:, 0:16],
                                       const[lo:lo + 64, C_RC + 16 * j:C_RC + 16 * j + 16], ALU.mult)
                    pool.tensor_scalar(gsq[lo:lo + 64, j, 16:SEQ], s_[:, 16:SEQ],
                                       const[lo:lo + 64, C_INVW + j:C_INVW + j + 1], None, ALU.mult)
                    pool.drain()
                    ins = pool.tensor_tensor(gsq[lo:lo + 64, j, 0:SEQ], gsq[lo:lo + 64, j, 0:SEQ], zz, ALU.subtract)
                    if g < 3:
                        pool.drain()
                ins.then_inc(pool_win, 1)
                pool.wait_ge(gate_scan, L + 1)
                pool.tensor_tensor(rows[:, R_A, 0:SEQ], rows[:, R_IG, 0:SEQ], rows[:, R_G, 0:SEQ], ALU.subtract)
                pool.tensor_tensor(rows[:, R_A, SEQ:TOK], rows[:, R_IG, SEQ:TOK], rows[:, R_M, SEQ:TOK], ALU.subtract)
                pool.drain()
                pool.tensor_tensor(rows[:, R_G, 0:SEQ], rows[:, R_G, 0:SEQ], rows[:, R_M, 0:SEQ], ALU.subtract)
                pool.tensor_tensor(rows[:, R_G, SEQ:TOK], tsm[:, :], rows[:, R_M, SEQ:TOK],
                                   ALU.subtract).then_inc(gate_g, 1)
                pool.wait_ge(gate_g, L + 1)
                pool.dma_start(O["new_m_prompt"][L].rearrange("a h -> h a"), rows[:, R_M, SEQ - 1:SEQ]).then_inc(m_out, 16)
                pool.dma_start(O["new_m_sample"][L].rearrange("b h -> h b"), rows[:, R_M, SEQ:TOK]).then_inc(m_out, 16)
                pool.wait_ge(pool_e, 2 * L + 2)
                pool.dma_start(O["new_pool_sample"][L, :, PST - 1, :], us[0:NB, :, :].rearrange("p a b -> p (a b)")).then_inc(out_st, 16)
                pool.dma_start(O["new_pool_prompt"][L, 0], us[32:32 + PST, :, :].rearrange("p a b -> p (a b)")).then_inc(out_st, 16)
                pool.wait_ge(g_ev, 3 * L + 3)
                pool.dma_start(O["new_gmlp_v_sample"][L, :, 0, :], gvo[0:NB, :]).then_inc(out_st, 16)
                for b in range(NB):
                    pool.wait_ge(cn_ready, NB * L + b + 1)
                    pool.dma_start(O["new_C_sample"][L, b].rearrange("h k v -> k h v"), Cb[:, b % 3]).then_inc(C_st, 16)
                    if b + 3 < NB:
                        pool.wait_ge(C_st, 16 * (NB * L + b + 1))
                        pool.wait_ge(cq_done, NB * L + b + 1)
                        pool.dma_start(Cb[:, b % 3], A["state_mlstm_C"][L, b + 3].rearrange("h k v -> k h v")).then_inc(C_in[b % 3], 16)
                pool.wait_ge(st_de, 2 * L + 2)
                pool.dma_start(O["new_n_sample"][L].rearrange("b h k -> (b h) k"), nout[0:NB * H, :]).then_inc(out_st, 16)
                for h in range(H):
                    hn = H * L + h
                    for i in range(TT):
                        n = TT * hn + i
                        w = SEQ - P * i
                        pool.wait_ge(e_ready, n + 1)
                        pool.affine_select(out=E[:, i % 2, 0:P], in_=E[:, i % 2, 0:P], compare_op=ALU.is_ge, fill=0.0,
                                           base=0, pattern=[[1, P]], channel_multiplier=-1).then_inc(e_mask, 1)
                        pool.wait_ge(kv_ev, hn + 1)
                        if i == 3:
                            pool.wait_ge(e_mask, n + 1)
                        if i == 0 and h:
                            pool.wait_ge(c_ready, hn)
                        pool.tensor_scalar(kw[:, i], ktok[:, i], E[:, i % 2, w - 1:w], None, ALU.mult).then_inc(kw_ready, 1)
                    pool.wait_ge(c_ev, hn + 1)
                    pool.dma_start(O["new_C_prompt"][L, 0, h], Cout[:, 0:P]).then_inc(c_out, 16)
                    pool.dma_start(O["new_n_prompt"][L, 0, h].rearrange("(k a) -> k a", a=1), Cout[:, P:P + 1]).then_inc(c_out, 16)
                for h in range(H):
                    hn = H * L + h
                    if h == 0:
                        pool.wait_ge(st_dd, L + 1)
                        pool.wait_ge(nd_max, H * (L + 1))
                    pool.tensor_tensor(D[:, h], D[:, h], D[:, h], ALU.mult).then_inc(hd2, 1)
                pool.wait_ge(sig_o, L + 1)
                for h in range(H):
                    hn = H * L + h
                    pool.wait_ge(hy, hn + 1)
                    pool.tensor_tensor(z[:, Z_O + h], num[:, h], z[:, Z_O + h], ALU.mult).then_inc(hy2, 1)
                pool.wait_ge(y_ok, L + 1)
                pool.dma_start(p_tok[:, 0:TT, :], A["p_prompt"][L, 0].rearrange("(t p) c -> p t c", p=P)).then_inc(p_in, 16)
                pool.dma_start(p_tok[0:NB, TT, :], A["p_sample"][L, :, 0, :]).then_inc(p_in, 16)
                add_x(2 * L)
                pool.wait_ge(r_ready, 5 * L + 3)
                pool.memset(acc[:, :, :], 0.0).then_inc(acc0, 1)
                add_x(2 * L + 1)
            pool.wait_ge(out_st, 16 * 5 * DEPTH)
            pool.wait_ge(m_out, 16 * 2 * DEPTH)
            pool.wait_ge(c_out, 16 * 2 * H * DEPTH)
            pool.wait_ge(C_st, 16 * NB * DEPTH)

        @block.tensor
        def _(pe):
            def mm(out, lhsT, rhs, start=True, stop=True):
                return nc.tensor.matmul(out, lhsT, rhs, start=start, stop=stop)

            pe.wait_ge(c_in, 16 * 9)
            nc.tensor.transpose(aux[:, 3, 0:96], colrows[0:96, :], ident[0:96, 0:96]).then_inc(cols_t, 1)
            pe.wait_ge(x_in, 16 * 5)
            for c in range(DC):
                if c >= 3:
                    pe.wait_ge(x_ok, c - 2)
                for t in range(TT):
                    last = nc.tensor.transpose(aux[:, c % 3, t * P:(t + 1) * P], x_tok[:, t, c * P:(c + 1) * P], ident)
                last.then_inc(x_t, 1)
            for c in range(DC):
                last = nc.tensor.transpose(lin[:, 0, c * NB:(c + 1) * NB], x_tok[0:NB, TT, c * P:(c + 1) * P], ident[0:NB, 0:NB])
            last.then_inc(xs_t, 1)

            def norm(N):
                for c in range(DC):
                    pe.wait_ge(sq_ready, N * DC + c + 1)
                    for a in range(2):
                        last = mm(aux[:, a, 0:HALF], bcol(C_MEAN), two(sq[:, c % 4])[:, a], c == 0, c == DC - 1)
                    last.then_inc(sq_used, 1)

            def slab(q, s, kc, rhs_hi, rhs_lo):
                pe.wait_ge(lo_done, q * 2 + (s + 1))
                if not (isinstance(q, int) and q == 0):
                    pe.wait_ge(pair_free[s], q)
                for k in range(kc):
                    whk, wlk = whi[:, s, k * P:(k + 1) * P], wlo[:, s, k * P:(k + 1) * P]
                    st, en = k == 0, k == kc - 1
                    for a in range(2):
                        o = lin[:, 2 * s + a, 0:HALF]
                        mm(o, whk, two(rhs_hi[:, k])[:, a], st, False)
                        mm(o, whk, two(rhs_lo[:, k])[:, a], False, False)
                    for a in range(2):
                        last = mm(lin[:, 2 * s + a, 0:HALF], wlk, two(rhs_hi[:, k])[:, a], False, en)
                last.then_inc(pe_slab, 1)

            def stream(base, pairs, kc, rhs):
                first = 1 if base == 0 else 0
                for q in range(first):
                    for s in range(2):
                        slab(0, s, kc[s], *rhs[s])
                with pe.Fori(first, pairs) as i:
                    for s in range(2):
                        slab(i + base, s, kc[s], *rhs[s])

            hh, yy, gg, pp = (h_hi, h_lo), (y_hi, y_lo), (gu_hi, gu_lo), (p_hi, p_lo)
            for L in range(DEPTH):
                norm(5 * L)
                pe.wait_ge(gw_lo, L + 1)
                for k in range(DC):
                    pe.wait_ge(h_ready, DC * 3 * L + k + 1)
                    gk = slice(k * GW, k * GW + P)
                    for a in range(2):
                        o = aux[:, 2 + a, 0:HALF]
                        mm(o, gwh[:, gk], two(h_hi[:, k])[:, a], k == 0, False)
                        mm(o, gwh[:, gk], two(h_lo[:, k])[:, a], False, False)
                        last = mm(o, gwl[:, gk], two(h_hi[:, k])[:, a], False, k == DC - 1)
                last.then_inc(gates, 1)
                stream(win_base(L), WIN_P, kcs("win"), (hh, hh))

                pe.wait_ge(pair_free[1], win_base(L) + WIN_P)
                pe.wait_ge(lay_in, 16 * 7 * (L + 1))
                for j in range(2):
                    nc.tensor.transpose(aux[0:NB, 0, j * P:(j + 1) * P], z[:, Z_POOL + j, SEQ:TOK], ident)
                    nc.tensor.transpose(aux[0:PST, 1, j * P:(j + 1) * P], z[:, Z_POOL + j, SEQ - PST:SEQ], ident)
                    last = nc.tensor.transpose(aux[:, 2, j * P:j * P + NB * PST], pst[0:NB * PST, j * P:(j + 1) * P],
                                               ident[0:NB * PST, 0:NB * PST])
                last.then_inc(pool_t, 1)
                for g in range(4):
                    last = nc.tensor.transpose(lin[:, 0, g * P:(g + 1) * P], wsr[:, g, :], ident)
                last.then_inc(g_wt, 1)
                for j in range(2):
                    n = 2 * L + j
                    pe.wait_ge(g_sq, n + 1)
                    for a in range(2):
                        last = mm(lin[:, 2 + a, 0:HALF], blk, two(gr[:, j])[:, a])
                    last.then_inc(g_mean, 1)
                    if j == 0:
                        pe.wait_ge(g_r, n + 1)
                pe.wait_ge(pool_v, L + 1)
                pe.wait_ge(pool_e, 2 * L + 2)
                for j in range(2):
                    for a in range(2):
                        last = mm(aux[:, 2 * j + a, 0:HALF], bdw[:, j, :], two(gsq[:, j])[:, a])
                last.then_inc(pool_mm, 1)
                for j in range(2):
                    pe.wait_ge(g_vn, 2 * L + 2)
                    for i in range(TT):
                        last = nc.tensor.transpose(lin[:, 2 + j, i * P:(i + 1) * P], z[:, Z_GV + j, i * P:(i + 1) * P], ident)
                    last.then_inc(g_t, 1)
                pe.wait_ge(g_wm, L + 1)
                for j in range(2):
                    last = nc.tensor.transpose(lin[0:NB, 0, j * P:(j + 1) * P], z[:, Z_GV + j, SEQ:TOK], ident)
                last.then_inc(g_t, 1)
                pe.wait_ge(pool_y, L + 1)
                pe.wait_ge(g_ev, 3 * L + 2)
                for j in range(2):
                    for i in range(TT):
                        for g in range(2):
                            o = aux[64 * g:64 * g + 64, j, i * P:(i + 1) * P]
                            mm(o, vnt[:, j, i, 64 * g:64 * g + 64], wmT[:, 2 * j + g, :], True, False)
                            last = mm(o, pick(4, 2 * j + g, 64), bsr[:, L, :], False, True)
                    last.then_inc(g_mix, 1)
                pe.wait_ge(gate_em, L + 1)
                pe.wait_ge(g_y, L + 1)
                for i in range(TT):
                    last = nc.tensor.transpose(aux[:, 0, i * H:(i + 1) * H], rows[:, R_A, i * P:(i + 1) * P], ident[0:H, 0:H])
                last.then_inc(acol_t, 1)
                for h in range(H):
                    nc.tensor.transpose(aux[0:NB, 1, h * P:(h + 1) * P], z[:, Z_V + h, SEQ:TOK], ident)
                    for n, r in enumerate((R_EM, R_G, R_A)):
                        mm(aux[:, 2, (3 * h + n) * NB:(3 * h + n + 1) * NB], pick(H, h), rows[:, r, SEQ:TOK])
                nc.tensor.transpose(aux[:, 3, 0:NB * H], nst[0:NB * H, :], ident[0:NB * H, 0:NB * H]).then_inc(st_t, 1)
                pe.wait_ge(st_k, L + 1)
                mm(aux[:, 3, 0:H * NB], bcol(C_ONE), qn.rearrange("p h b -> p (h b)"))
                nc.tensor.transpose(aux[0:NB * H, 2, 0:P], nn.rearrange("p b h -> p (b h)"), ident).then_inc(st_den, 1)
                for b in range(NB):
                    n = NB * L + b
                    if b >= 2:
                        pe.wait_ge(ct_ready, n - 1)
                    elif b == 0:
                        pe.wait_ge(g_ev, 3 * L + 3)
                    mm(lin[:, b % 2, :], pick(NB, b), vs[0:NB].rearrange("p h v -> p (h v)")).then_inc(vb_ready, 1)
                    if b >= 1:
                        pe.wait_ge(cn_ready, n)
                        for h in range(H):
                            last = mm(lin[:, 2, h * NB + b - 1:h * NB + b], Cb[:, (b - 1) % 3, h], z[:, Z_Q + h, SEQ + b - 1:SEQ + b])
                        last.then_inc(cq_done, 1)
                pe.wait_ge(cn_ready, NB * (L + 1))
                for h in range(H):
                    last = mm(lin[:, 2, h * NB + NB - 1:h * NB + NB], Cb[:, (NB - 1) % 3, h], z[:, Z_Q + h, TOK - 1:TOK])
                last.then_inc(cq_done, 1)
                pe.wait_ge(st_num, L + 1)
                for h in range(H):
                    hn = H * L + h
                    if h:
                        pe.wait_ge(nd_max, hn)
                        pe.wait_ge(nd_ev, hn)
                        pe.wait_ge(c_ev, hn)
                    else:
                        pe.wait_ge(st_dd, L + 1)
                        pe.wait_ge(acol_ok, L + 1)
                    for i in range(TT):
                        nc.tensor.transpose(aux[:, 0, i * P:(i + 1) * P], z[:, Z_V + h, i * P:(i + 1) * P], ident)
                        last = nc.tensor.transpose(aux[:, 1, i * P:(i + 1) * P], z[:, Z_K + h, i * P:(i + 1) * P], ident)
                    last.then_inc(kv_t, 1)
                    mm(aux[:, 2, :], pick(H, h), rows[:, R_G, 0:SEQ])
                    mm(aux[:, 3, :], pick(H, h), rows[:, R_EM, 0:SEQ]).then_inc(gb_ready, 1)
                    for i in range(TT):
                        mm(lin[:, i, 0:SEQ - i * P], z[:, Z_K + h, i * P:(i + 1) * P], z[:, Z_Q + h, i * P:SEQ]).then_inc(s_ready, 1)
                    pe.wait_ge(kv_ev, hn + 1)
                    for i in range(TT):
                        n = TT * hn + i
                        pe.wait_ge(w_ready, n + 1)
                        w = SEQ - i * P
                        mm(aux[:, 0, i * P:SEQ], vtok[:, i, 0:P], W[:, i % 2, 0:w], i == 0, i == TT - 1)
                        mm(aux[:, 1, i * P:SEQ], bcol(C_ONE), W[:, i % 2, 0:w], i == 0, i == TT - 1).then_inc(w_used, 1)
                    pe.wait_ge(e_ready, TT * (hn + 1))
                    pe.wait_ge(kw_ready, TT * (hn + 1))
                    for i in range(TT):
                        last = mm(aux[:, 2, 0:P + 1], kw[:, i], vtok[:, i, :], i == 0, i == TT - 1)
                    last.then_inc(c_ready, 1)
                for h in range(H):
                    hn = H * L + h
                    pe.wait_ge(hq, hn + 1)
                    if h == 0:
                        pe.wait_ge(nd_max, H * (L + 1))
                    for a in range(2):
                        last = mm(aux[:, a, 0:HALF], bcol(C_MEANH), two(hs1[:, 0:TOK])[:, a])
                    last.then_inc(hm, 1)
                pe.wait_ge(y_ok, L + 1)
                stream(wout_base(L), WOUT_P, kcs("wout"), (yy, yy))
                pe.wait_ge(p_in, 32 * (L + 1))
                for j in range(2):
                    if j == 1:
                        pe.wait_ge(p_ok, 2 * L + 1)
                    for t in range(TT):
                        nc.tensor.transpose(aux[:, 2, t * P:(t + 1) * P], p_tok[:, t, j * P:(j + 1) * P], ident)
                    nc.tensor.transpose(aux[:, 3, 0:NB], p_tok[0:NB, TT, j * P:(j + 1) * P], ident[0:NB, 0:NB]).then_inc(p_t, 1)
                norm(5 * L + 1)
                norm(5 * L + 2)
                pe.wait_ge(h_ready, DC * (3 * L + 2))
                if L:
                    pe.wait_ge(rw_lo, 1)
                    for t in range(5):
                        at = t * P if t < TT else TOK - P
                        for k in range(DC):
                            o = aux[:, 2, t * NE:(t + 1) * NE]
                            mm(o, h_hi[:, k, at:at + P], rwh[:, k], k == 0, False)
                            mm(o, h_lo[:, k, at:at + P], rwh[:, k], False, False)
                            last = mm(o, h_hi[:, k, at:at + P], rwl[:, k], False, k == DC - 1)
                    last.then_inc(rt_lg, 1)
                    pe.wait_ge(rt_gate, 1)
                    for t in range(TT):
                        nc.tensor.transpose(aux[0:NE, 3, t * P:(t + 1) * P], gatet[:, t], ident)
                    nc.tensor.transpose(aux[0:NE, 2, 0:P], gatet[:, TT], ident).then_inc(rt_t, 1)
                    pe.wait_ge(rt_row, 1)
                for e in range(SLICES[L]):
                    if L:
                        if e:
                            pe.wait_ge(gb_ok, e)
                        for a in range(2):
                            last = mm(aux[:, 2 + a, 0:HALF], pick(NE, e), two(grow[:, :])[:, a])
                        last.then_inc(gb_mm, 1)
                    b = ffn_base(L) + e * (GU_P + DOWN_P)
                    stream(b, GU_P, kcs("gu"), (hh, hh))
                    pe.wait_ge(gu_ok, GU_P * (SLICES[0] * L + e + 1))
                    stream(b + GU_P, DOWN_P, kcs("down"), (gg, gg))
                norm(5 * L + 3)
                norm(5 * L + 4)
                pe.wait_ge(h_ready, DC * (3 * L + 3))
                stream(ple_base(L), PLE_P, kcs("ple"), (hh, pp))
            pe.wait_ge(pair_free[1], LAST_PAIR + 1)
            pe.wait_ge(ple_x, DC * DEPTH)
            for t in range(TT + 1):
                n = P if t < TT else NB
                if t:
                    pe.wait_ge(yt_ev, t)
                for c in range(DC):
                    last = nc.tensor.transpose(lin[0:n, c // 4, (c % 4) * P:(c % 4 + 1) * P], x[:, c, t * P:t * P + n], ident)
                last.then_inc(yt_t, 1)

        @block.scalar
        def _(act):
            def cp(out, in_, **k):
                return nc.scalar.activation(out, in_, ACT.Copy, **k)

            def split(q, s, kc):
                act.wait_ge(staged[s], q * 16 + 16)
                if not (isinstance(q, int) and q == 0):
                    act.wait_ge(pe_slab, q * 2 + (s - 1))
                cp(whi[:, s, 0:kc * P], wst[:, s, 0:kc * P]).then_inc(hi_done, 1)

            def stream(base, pairs, kc, after, take):
                def pair(q, i, nxt):
                    split(q, 1, kc[1])
                    take(0, q, i)
                    if nxt:
                        split(q + 1, 0, nxt)
                    take(1, q, i)
                first = 1 if base == 0 else 0
                if first:
                    pair(0, 0, kc[0])
                with act.Fori(first, pairs - 1) as i:
                    pair(i + base, i, kc[0])
                pair(base + pairs - 1, pairs - 1, after)

            act.wait_ge(setup_pool, 1)
            act.wait_ge(cols_t, 1)
            cp(cols[:, :], aux[:, 3, 0:96]).then_inc(cols_ok, 1)
            split(0, 0, DC)
            for c in range(DC):
                act.wait_ge(x_t, c + 1)
                cp(x[:, c, 0:SEQ], aux[:, c % 3, :]).then_inc(x_ok, 1)
            act.wait_ge(xs_t, 1)
            cp(x[:, :, SEQ:TOK], lin[:, 0, 0:DC * NB].rearrange("p (c b) -> p c b", b=NB)).then_inc(x_ok, 1)
            act.wait_ge(x_ok, DC + 1)

            def norm(N, src, ready):
                for c in range(DC):
                    if ready is not None:
                        act.wait_ge(ready[0], ready[1] + c + 1)
                    if N or c >= 4:
                        act.wait_ge(sq_used, N * DC + max(c - 3, 0))
                    nc.scalar.activation(sq[:, c % 4], src[:, c], ACT.Square).then_inc(sq_ready, 1)
                act.wait_ge(sq_used, (N + 1) * DC)
                nc.scalar.activation(two(rn), aux[:, 0:2, 0:HALF], ACT.Ln, bias=epsc[:, :])
                act.drain()
                nc.scalar.activation(rn, rn, ACT.Exp, scale=-0.5).then_inc(r_ready, 1)

            def round_h(N):
                for c in range(DC):
                    act.wait_ge(ht_ready, N * DC + c + 1)
                    cp(h_hi[:, c], ht[:, c % 2]).then_inc(h_hi_ok, 1)

            def rsqrt(out, in_, eps=True):
                if eps:
                    nc.scalar.activation(out, in_, ACT.Ln, bias=epsc[:, :])
                else:
                    nc.scalar.activation(out, in_, ACT.Ln)
                act.drain()
                return nc.scalar.activation(out, out, ACT.Exp, scale=-0.5)

            for L in range(DEPTH):
                act.wait_ge(gw_in, 32 * (L + 1))
                cp(gwh[:, :], gwf[:, :]).then_inc(gw_ok, 1)
                norm(5 * L, x, (ple_x, DC * (L - 1)) if L else None)
                round_h(3 * L)
                act.wait_ge(gates, L + 1)
                if L == 0:
                    act.wait_ge(w_small, 16 * 23)
                nc.scalar.activation(two(rows[:, R_IG]), aux[0:H, 2:4, 0:HALF], ACT.Identity, bias=gate_b[:, 0, L:L + 1])
                cp(two(rows[:, R_F]), aux[32:32 + H, 2:4, 0:HALF])
                act.drain()
                nc.scalar.activation(rows[:, R_F], rows[:, R_F], ACT.Identity, bias=gate_b[:, 1, L:L + 1])
                act.drain()
                nc.scalar.activation(rows[:, R_EM], rows[:, R_F], ACT.Abs)
                act.drain()
                nc.scalar.activation(rows[:, R_EM], rows[:, R_EM], ACT.Exp, scale=-1.0)
                act.drain()
                nc.scalar.activation(rows[:, R_EM], rows[:, R_EM], ACT.Ln, bias=one[0:H]).then_inc(gate_l1, 1)

                def take_z(s, q, i):
                    act.wait_ge(pe_slab, q * 2 + (s + 1))
                    cp(z[:, bass.ds(i * 2 + s, 1)].rearrange("p a (b c) -> p (a b) c", c=HALF),
                       lin[:, 2 * s:2 * s + 2, 0:HALF]).then_inc(pair_free[s], 1)
                stream(win_base(L), WIN_P, kcs("win"), kcs("wout")[0], take_z)
                act.wait_ge(pair_free[0], wout_base(L))
                act.wait_ge(pair_free[1], wout_base(L))
                nc.scalar.activation(z[:, Z_O:Z_O + H], z[:, Z_O:Z_O + H], ACT.Sigmoid).then_inc(sig_o, 1)
                act.wait_ge(pool_t, L + 1)
                if L:
                    act.wait_ge(out_st, 16 * 5 * L)
                cp(us[0:NB], aux[0:NB, 0, 0:2 * P].rearrange("p (a b) -> p a b", b=P)).then_inc(pool_e, 1)
                cp(us[32:32 + PST], aux[0:PST, 1, 0:2 * P].rearrange("p (a b) -> p a b", b=P)).then_inc(pool_e, 1)
                for j in range(2):
                    nc.scalar.activation(gr[:, j], z[:, Z_GV + j], ACT.Square).then_inc(g_sq, 1)
                for j in range(2):
                    act.wait_ge(g_mean, 2 * L + j + 1)
                    rsqrt(two(gr[:, j]), lin[:, 2:4, 0:HALF]).then_inc(g_r, 1)
                act.wait_ge(pool_mm, L + 1)
                for j in range(2):
                    ins = cp(two(z[:, Z_POOL + j]), aux[:, 2 * j:2 * j + 2, 0:HALF], scale=cols[:, 80 + 2 * L + j:81 + 2 * L + j])
                ins.then_inc(pool_y, 1)
                for j in range(2):
                    act.wait_ge(g_t, 3 * L + j + 1)
                    cp(vnt[:, j], lin[:, 2 + j, :].rearrange("p (i d) -> p i d", d=P)).then_inc(g_ev, 1)
                act.wait_ge(g_t, 3 * L + 3)
                cp(gvo[0:NB, :], lin[0:NB, 0, 0:2 * P]).then_inc(g_ev, 1)
                act.wait_ge(gate_g, L + 1)
                nc.scalar.activation(rows[:, R_EM], rows[:, R_M], ACT.Exp, scale=-1.0)
                nc.scalar.activation(rows[:, R_G, SEQ:TOK], rows[:, R_G, SEQ:TOK], ACT.Exp)
                nc.scalar.activation(rows[:, R_A, SEQ:TOK], rows[:, R_A, SEQ:TOK], ACT.Exp).then_inc(gate_em, 1)
                act.wait_ge(acol_t, L + 1)
                cp(acol[:, :, :], aux[:, 0, 0:TT * H].rearrange("p (i h) -> p i h", h=H)).then_inc(acol_ok, 1)
                act.wait_ge(st_t, L + 1)
                cp(vs[0:NB], aux[0:NB, 1, :].rearrange("p (h v) -> p h v", v=P))
                cp(dcs[:, :, :, :], aux[:, 2, 0:H * 3 * NB].rearrange("p (h n b) -> p h n b", n=3, b=NB))
                cp(nT[:, :, :], aux[:, 3, 0:NB * H].rearrange("p (b h) -> p b h", h=H)).then_inc(st_ev, 1)
                act.wait_ge(st_den, L + 1)
                nc.scalar.activation(D[:, :, SEQ:TOK], aux[:, 3, 0:H * NB].rearrange("p (h b) -> p h b", b=NB), ACT.Abs).then_inc(st_de, 1)
                cp(nout[0:NB * H, :], aux[0:NB * H, 2, 0:P]).then_inc(st_de, 1)
                act.wait_ge(out_st, 16 * (5 * L + 4))
                for b in range(NB):
                    n = NB * L + b
                    act.wait_ge(vb_ready, n + 1)
                    if b:
                        act.wait_ge(cn_ready, n)
                    for h in range(H):
                        ins = cp(Ct[:, h], lin[:, b % 2, h * P:(h + 1) * P], scale=kws[:, h, b:b + 1])
                    ins.then_inc(ct_ready, 1)
                act.wait_ge(cq_done, NB * (L + 1))
                cp(num[:, :, SEQ:TOK], lin[:, 2, 0:H * NB].rearrange("p (h b) -> p h b", b=NB)).then_inc(st_num, 1)
                for h in range(H):
                    hn = H * L + h
                    act.wait_ge(kv_t, hn + 1)
                    if h:
                        act.wait_ge(c_ready, hn)
                        act.wait_ge(kw_ready, TT * hn)
                    cp(vtok[:, :, 0:P], aux[:, 0, :].rearrange("p (i d) -> p i d", d=P))
                    if h == 0:
                        cp(vtok[:, :, P:P + 1], one.to_broadcast([P, TT]).rearrange("p (i a) -> p i a", a=1))
                    cp(ktok[:, :, :], aux[:, 1, :].rearrange("p (i d) -> p i d", d=P), scale=QS).then_inc(kv_ev, 1)
                    act.wait_ge(gb_ready, hn + 1)
                    for i in range(TT):
                        n = TT * hn + i
                        if n >= 2:
                            act.wait_ge(w_ready, n - 1)
                            act.wait_ge(kw_ready, n - 1)
                        nc.scalar.activation(E[:, i % 2, 0:SEQ - i * P], aux[:, 2, i * P:SEQ], ACT.Exp,
                                             bias=acol[:, i, h:h + 1]).then_inc(e_ready, 1)
                    act.wait_ge(w_used, TT * (hn + 1))
                    cp(num[:, h, 0:SEQ], aux[:, 0, :])
                    nc.scalar.activation(D[:, h, 0:SEQ], aux[:, 1, :], ACT.Abs).then_inc(nd_ev, 1)
                    act.wait_ge(c_ready, hn + 1)
                    if h:
                        act.wait_ge(c_out, 32 * hn)
                    elif L:
                        act.wait_ge(c_out, 32 * H * L)
                    cp(Cout[:, :], aux[:, 2, 0:P + 1]).then_inc(c_ev, 1)
                act.wait_ge(st_num, L + 1)
                act.wait_ge(nd_ev, H * (L + 1))
                for h in range(H):
                    hn = H * L + h
                    nc.scalar.activation(hs1[:, 0:TOK], num[:, h], ACT.Square).then_inc(hq, 1)
                    act.wait_ge(ha, hn + 1)
                    if h:
                        act.wait_ge(hy, hn)
                    rsqrt(hs2[:, 0:TOK], hs1[:, 0:TOK], False).then_inc(hr, 1)
                act.wait_ge(hy2, H * (L + 1))
                act.wait_ge(g_y, L + 1)
                cp(y_hi[:, 0:2], z[:, Z_POOL:Z_POOL + 2])
                cp(y_hi[:, 2:6], z[:, Z_O:Z_O + H])
                cp(y_hi[:, 6:8], z[:, Z_GU:Z_GU + 2]).then_inc(y_hi_ok, 1)

                act.wait_ge(y_ok, L + 1)
                stream(wout_base(L), WOUT_P, kcs("wout"), kcs("gu")[0], take_z)
                for j in range(2):
                    act.wait_ge(p_t, 2 * L + j + 1)
                    cp(p_hi[:, j, 0:SEQ], aux[:, 2, :])
                    cp(p_hi[:, j, SEQ:TOK], aux[:, 3, 0:NB]).then_inc(p_hi_ok, 1)
                act.wait_ge(pair_free[0], ffn_base(L))
                act.wait_ge(pair_free[1], ffn_base(L))
                norm(5 * L + 1, acc, None)
                norm(5 * L + 2, x, (x_upd, DC * 2 * L))
                round_h(3 * L + 1)
                if L:
                    act.wait_ge(rt_max, 1)
                    nc.scalar.activation(gwt[:, :, 1], gwt[:, :, 1], ACT.Sigmoid).then_inc(rt_e, 1)
                    act.wait_ge(rt_t, 1)
                    cp(grow[:, 0:SEQ], aux[0:NE, 3, :])
                    act.drain()
                    cp(grow[:, TOK - P:TOK], aux[0:NE, 2, 0:P]).then_inc(rt_row, 1)
                for e in range(SLICES[L]):
                    b = ffn_base(L) + e * (GU_P + DOWN_P)
                    done = GU_P * (SLICES[0] * L + e)
                    if L:
                        act.wait_ge(gb_mm, e + 1)
                        if e:
                            act.wait_ge(gu_ok, done)
                        cp(two(gb), aux[:, 2:4, 0:HALF]).then_inc(gb_ok, 1)

                    def take_gu(s, q, i):
                        if s == 0:
                            act.wait_ge(pe_slab, q * 2 + 1)
                            nc.scalar.activation(two(sg), lin[:, 0:2, 0:HALF], ACT.Silu).then_inc(pair_free[0], 1)
                        else:
                            if L:
                                act.wait_ge(gt_ready, i + (GU_P * e + 1))
                            else:
                                act.wait_ge(pair_free[1], q + 1)
                            cp(gu_hi[:, bass.ds(i, 1)].rearrange("p a t -> p (a t)"), gt).then_inc(gu_hi_ok, 1)
                    stream(b, GU_P, kcs("gu"), kcs("down")[0], take_gu)
                    stream(b + GU_P, DOWN_P, kcs("down"), kcs("gu")[0] if e < SLICES[L] - 1 else kcs("ple")[0],
                           lambda s, q, i: None)
                act.wait_ge(pair_free[0], ple_base(L))
                act.wait_ge(pair_free[1], ple_base(L))
                norm(5 * L + 3, acc, None)
                norm(5 * L + 4, x, (x_upd, DC * (2 * L + 1)))
                round_h(3 * L + 2)

                def take_ple(s, q, i):
                    if s == 0:
                        act.wait_ge(pe_slab, q * 2 + 1)
                        if not (isinstance(i, int) and i == 0):
                            act.wait_ge(pair_free[1], q)
                        nc.scalar.activation(two(sg), lin[:, 0:2, 0:HALF], ACT.Sigmoid).then_inc(pair_free[0], 1)
                stream(ple_base(L), PLE_P, kcs("ple"), kcs("win")[0] if L < DEPTH - 1 else 0, take_ple)
            for t in range(TT + 1):
                n = P if t < TT else NB
                act.wait_ge(yt_t, t + 1)
                if t >= 2:
                    act.wait_ge(y_st[t % 2], 16 * (t // 2))
                cp(y_tok[0:n, t % 2, :], lin[0:n, 0:2, :].rearrange("p a b -> p (a b)")).then_inc(yt_ev, 1)

        @block.vector
        def _(dve):
            def tt(out, a, b, op):
                return nc.vector.tensor_tensor(out, a, b, op)

            def stt(out, a, s, b, op0, op1):
                return nc.vector.scalar_tensor_tensor(out=out, in0=a, scalar=s, in1=b, op0=op0, op1=op1)

            def split(q, s, kc):
                dve.wait_ge(hi_done, q * 2 + (s + 1))
                tt(wlo[:, s, 0:kc * P], wst[:, s, 0:kc * P], whi[:, s, 0:kc * P].bitcast(f32), ALU.subtract).then_inc(lo_done, 1)

            def stream(base, pairs, kc, after, take):
                def pair(q, i, nxt):
                    split(q, 1, kc[1])
                    take(0, q, i)
                    if nxt:
                        split(q + 1, 0, nxt)
                    take(1, q, i)
                with dve.Fori(0, pairs - 1) as i:
                    pair(i + base, i, kc[0])
                pair(base + pairs - 1, pairs - 1, after)

            def nothing(s, q, i):
                pass

            def make_h(N, w):
                def scaled(c):
                    stt(ht[:, c % 2], x[:, c], cols[:, w + c:w + c + 1], rn, ALU.mult, ALU.mult).then_inc(ht_ready, 1)
                scaled(0)
                for c in range(DC):
                    if c + 1 < DC:
                        if c:
                            dve.wait_ge(h_ready, N * DC + c)
                        scaled(c + 1)
                    dve.wait_ge(h_hi_ok, N * DC + c + 1)
                    dve.wait_ge(ht_ready, N * DC + c + 1)
                    tt(h_lo[:, c], ht[:, c % 2], h_hi[:, c].bitcast(f32), ALU.subtract).then_inc(h_ready, 1)

            def normed(N, w):
                for c in range(DC):
                    if N or c >= 2:
                        dve.wait_ge(x_upd, N * DC + max(c - 1, 0))
                    stt(ut[:, c % 2], acc[:, c], cols[:, w + c:w + c + 1], rn, ALU.mult, ALU.mult).then_inc(ut_ready, 1)

            split(0, 0, DC)
            dve.wait_ge(cols_ok, 1)
            dve.wait_ge(x_ok, DC + 1)
            for L in range(DEPTH):
                dve.wait_ge(gw_ok, L + 1)
                tt(gwl[:, :], gwf[:, :], gwh[:, :].bitcast(f32), ALU.subtract).then_inc(gw_lo, 1)
                dve.wait_ge(r_ready, 5 * L + 1)
                make_h(3 * L, 8 * L)
                stream(win_base(L), WIN_P, kcs("win"), kcs("wout")[0], nothing)
                dve.wait_ge(gate_lf, L + 1)
                nc.vector.tensor_tensor_scan(rows[:, R_G, 0:SEQ], rows[:, R_F, 0:SEQ], rows[:, R_A, 0:SEQ], 0.0, ALU.add, ALU.add)
                nc.vector.tensor_tensor_scan(rows[:, R_M, 0:SEQ], rows[:, R_F, 0:SEQ], rows[:, R_IG, 0:SEQ], 0.0, ALU.add, ALU.max)
                tt(rows[:, R_M, SEQ:TOK], tsm[:, :], rows[:, R_IG, SEQ:TOK], ALU.max).then_inc(gate_scan, 1)
                dve.wait_ge(pool_win, L + 1)
                dve.wait_ge(pool_t, L + 1)
                for g, w in enumerate(WINDOWS):
                    lo, j = 64 * (g % 2), g // 2
                    old = aux[lo:lo + 64, 2, j * P:j * P + NB * PST].rearrange("p (b r) -> p b r", r=PST)[:, :, PST - w + 1:PST]
                    nc.vector.tensor_reduce(gsq[lo:lo + 64, j, SEQ:TOK], old, AXX, ALU.add)
                dve.drain()
                tt(gsq[:, :, SEQ:TOK], gsq[:, :, SEQ:TOK], z[:, Z_POOL:Z_POOL + 2, SEQ:TOK], ALU.add)
                dve.drain()
                for j in range(2):
                    last = stt(gsq[:, j, SEQ:TOK], gsq[:, j, SEQ:TOK], const[:, C_INVW + j:C_INVW + j + 1],
                               z[:, Z_POOL + j, SEQ:TOK], ALU.mult, ALU.subtract)
                last.then_inc(pool_v, 1)
                dve.wait_ge(g_wt, L + 1)
                tt(wmT[:, :, :], lin[:, 0, :].rearrange("p (g t) -> p g t", t=P),
                   tri.rearrange("p (a t) -> p a t", a=1).to_broadcast([P, 4, P]), ALU.mult).then_inc(g_wm, 1)
                for j in range(2):
                    dve.wait_ge(g_r, 2 * L + j + 1)
                    stt(z[:, Z_GV + j], z[:, Z_GV + j], cols[:, 92 + 2 * L + j:93 + 2 * L + j], gr[:, j], ALU.mult, ALU.mult).then_inc(g_vn, 1)
                dve.wait_ge(g_vn, 2 * L + 2)
                dve.wait_ge(pool_mm, L + 1)
                for j in range(2):
                    nc.vector.tensor_scalar(gsq[:, j, SEQ:TOK], z[:, Z_GV + j, SEQ:TOK], sg_b[:, 0, L, j:j + 1],
                                            sg_b[:, 1, L, j:j + 1], ALU.mult, ALU.add)
                dve.drain()
                for j in range(2):
                    dve.wait_ge(g_mix, 2 * L + j + 1)
                    tt(z[:, Z_GU + j, 0:SEQ], z[:, Z_GU + j, 0:SEQ], aux[:, j, :], ALU.mult)
                    last = tt(z[:, Z_GU + j, SEQ:TOK], z[:, Z_GU + j, SEQ:TOK], gsq[:, j, SEQ:TOK], ALU.mult)
                last.then_inc(g_y, 1)
                dve.wait_ge(st_ev, L + 1)
                nv = nn.rearrange("p b h -> p h b")
                stt(kws[:, :, :], z[:, Z_K:Z_K + H, SEQ:TOK], QS, dcs[:, :, 2, :], ALU.mult, ALU.mult)
                tt(nv, nT.rearrange("p b h -> p h b"), dcs[:, :, 1, :], ALU.mult)
                dve.drain()
                tt(nv, nv, kws[:, :, :], ALU.add)
                dve.drain()
                tt(qn[:, :, :], z[:, Z_Q:Z_Q + H, SEQ:TOK], nv, ALU.mult).then_inc(st_k, 1)
                dve.wait_ge(st_de, 2 * L + 1)
                tt(D[:, :, SEQ:TOK], D[:, :, SEQ:TOK], dcs[:, :, 0, :], ALU.max).then_inc(st_dd, 1)
                for b in range(NB):
                    dve.wait_ge(C_in[b % 3], 16 * ((3, 3, 2)[b % 3] * L + b // 3 + 1))
                    dve.wait_ge(ct_ready, NB * L + b + 1)
                    for h in range(H):
                        last = stt(Cb[:, b % 3, h], Cb[:, b % 3, h], dcs[:, h, 1, b:b + 1], Ct[:, h], ALU.mult, ALU.add)
                    last.then_inc(cn_ready, 1)
                for h in range(H):
                    hn = H * L + h
                    for i in range(TT):
                        n = TT * hn + i
                        dve.wait_ge(e_mask, n + 1)
                        dve.wait_ge(s_ready, n + 1)
                        if n >= 2:
                            dve.wait_ge(w_used, n - 1)
                        w = SEQ - i * P
                        stt(W[:, i % 2, 0:w], lin[:, i, 0:w], QS, E[:, i % 2, 0:w], ALU.mult, ALU.mult).then_inc(w_ready, 1)
                    dve.wait_ge(nd_ev, hn + 1)
                    tt(D[:, h, 0:SEQ], D[:, h, 0:SEQ], aux[:, 3, :], ALU.max).then_inc(nd_max, 1)
                for h in range(H):
                    hn = H * L + h
                    dve.wait_ge(hm, hn + 1)
                    dve.wait_ge(hd2, hn + 1)
                    stt(two(hs1[:, 0:TOK]), two(D[:, h]), EPS, aux[:, 0:2, 0:HALF], ALU.mult, ALU.add).then_inc(ha, 1)
                    dve.wait_ge(hr, hn + 1)
                    stt(num[:, h], num[:, h], cols[:, 84 + 4 * L + h:85 + 4 * L + h], hs2[:, 0:TOK], ALU.mult, ALU.mult).then_inc(hy, 1)
                dve.wait_ge(y_hi_ok, L + 1)
                tt(y_lo[:, 0:2], z[:, Z_POOL:Z_POOL + 2], y_hi[:, 0:2].bitcast(f32), ALU.subtract)
                tt(y_lo[:, 2:6], z[:, Z_O:Z_O + H], y_hi[:, 2:6].bitcast(f32), ALU.subtract)
                tt(y_lo[:, 6:8], z[:, Z_GU:Z_GU + 2], y_hi[:, 6:8].bitcast(f32), ALU.subtract).then_inc(y_ok, 1)
                stream(wout_base(L), WOUT_P, kcs("wout"), kcs("gu")[0], nothing)
                for j in range(2):
                    dve.wait_ge(p_hi_ok, 2 * L + j + 1)
                    tt(p_lo[:, j, 0:SEQ], aux[:, 2, :], p_hi[:, j, 0:SEQ].bitcast(f32), ALU.subtract)
                    tt(p_lo[:, j, SEQ:TOK], aux[:, 3, 0:NB], p_hi[:, j, SEQ:TOK].bitcast(f32), ALU.subtract).then_inc(p_ok, 1)
                dve.wait_ge(r_ready, 5 * L + 2)
                normed(2 * L, 16 + 8 * L)
                dve.wait_ge(r_ready, 5 * L + 3)
                make_h(3 * L + 1, 32 + 8 * L)
                if L == 0:
                    nc.vector.tensor_copy(rwh[:, :, :], rwf[:, :, :])
                    dve.drain()
                    tt(rwl[:, :, :], rwf[:, :, :], rwh[:, :, :].bitcast(f32), ALU.subtract).then_inc(rw_lo, 1)
                else:
                    dve.wait_ge(rt_lg, 1)
                    tt(lg[:, :, :], aux[:, 2, 0:5 * NE].rearrange("p (t e) -> p t e", e=NE),
                       rbias[:, :].rearrange("p (a e) -> p a e", a=1).to_broadcast([P, 5, NE]), ALU.add)
                    dve.drain()
                    for t in range(5):
                        nc.vector.max(top[:, t], lg[:, t])
                    dve.drain()
                    for t in range(5):
                        nc.vector.max_index(topi[:, t], top[:, t], lg[:, t])
                    tt(gwt[:, :, 1], top[:, :, 1], top[:, :, 0], ALU.subtract).then_inc(rt_max, 1)
                    dve.drain()
                    nc.vector.tensor_copy(topf[:, :, :], topi[:, :, :])
                    dve.wait_ge(rt_e, 1)
                    nc.vector.tensor_scalar(gwt[:, :, 0], gwt[:, :, 1], -1.0, 1.0, ALU.mult, ALU.add)
                    dve.drain()
                    for t in range(5):
                        nc.vector.tensor_scalar(gtmp[:, t], iota8[:, :], topf[:, t, 0:1], gwt[:, t, 0:1], ALU.is_equal, ALU.mult)
                        nc.vector.tensor_scalar(gatet[:, t], iota8[:, :], topf[:, t, 1:2], gwt[:, t, 1:2], ALU.is_equal, ALU.mult)
                    dve.drain()
                    tt(gatet[:, :, :], gatet[:, :, :], gtmp[:, :, :], ALU.add).then_inc(rt_gate, 1)
                dve.wait_ge(acc0, L + 1)
                for e in range(SLICES[L]):
                    b = ffn_base(L) + e * (GU_P + DOWN_P)
                    done = GU_P * (SLICES[0] * L + e)
                    if L:
                        dve.wait_ge(gb_ok, e + 1)

                    def take_gu(s, q, i):
                        if s == 0:
                            return
                        dve.wait_ge(pe_slab, q * 2 + 2)
                        dve.wait_ge(pair_free[0], q + 1)
                        if L:
                            tt(two(gt), two(sg), lin[:, 2:4, 0:HALF], ALU.mult).then_inc(pair_free[1], 1)
                            dve.drain()
                            tt(gt, gt, gb, ALU.mult).then_inc(gt_ready, 1)
                        else:
                            tt(two(gt), two(sg), lin[:, 2:4, 0:HALF], ALU.mult).then_inc(pair_free[1], 1)
                        dve.wait_ge(gu_hi_ok, i + (done + 1))
                        tt(gu_lo[:, bass.ds(i, 1)].rearrange("p a t -> p (a t)"), gt,
                           gu_hi[:, bass.ds(i, 1)].rearrange("p a t -> p (a t)").bitcast(f32), ALU.subtract).then_inc(gu_ok, 1)

                    def take_down(s, q, i):
                        dve.wait_ge(pe_slab, q * 2 + (s + 1))
                        o = acc[:, bass.ds(i * 2 + s, 1)].rearrange("p a (b c) -> p (a b) c", c=HALF)
                        tt(o, o, lin[:, 2 * s:2 * s + 2, 0:HALF], ALU.add).then_inc(pair_free[s], 1)
                    stream(b, GU_P, kcs("gu"), kcs("down")[0], take_gu)
                    stream(b + GU_P, DOWN_P, kcs("down"), kcs("gu")[0] if e < SLICES[L] - 1 else kcs("ple")[0], take_down)
                dve.wait_ge(r_ready, 5 * L + 4)
                normed(2 * L + 1, 48 + 8 * L)
                dve.wait_ge(r_ready, 5 * L + 5)
                make_h(3 * L + 2, 64 + 8 * L)

                def take_ple(s, q, i):
                    if s == 0:
                        return
                    dve.wait_ge(pe_slab, q * 2 + 2)
                    dve.wait_ge(pair_free[0], q + 1)
                    tt(two(gt), two(sg), lin[:, 2:4, 0:HALF], ALU.mult).then_inc(pair_free[1], 1)
                    dve.drain()
                    xd = x[:, bass.ds(i, 1)].rearrange("p a t -> p (a t)")
                    tt(xd, xd, gt, ALU.add).then_inc(ple_x, 1)
                stream(ple_base(L), PLE_P, kcs("ple"), kcs("win")[0] if L < DEPTH - 1 else 0, take_ple)


_INS = ["x_prompt", "x_sample", "state_pool", "state_mlstm_C", "state_mlstm_n", "state_mlstm_m", "p_prompt", "p_sample",
        "norm_mix_pre", "norm_mix_post", "norm_ffn_pre", "norm_ffn_post", "norm_ple", "w_in", "pool_w", "pool_scale",
        "mlstm_b_i", "mlstm_b_f", "mlstm_norm_w", "gmlp_norm_w", "gmlp_ws", "gmlp_bs", "w_out", "ffn_w_gate",
        "ffn_w_up", "ffn_w_down", "moe_router_w", "moe_router_b", "moe_w_gate", "moe_w_up", "moe_w_down",
        "ple_w_gate", "ple_w_proj"]
_OUTS = [("y_prompt", (1, SEQ, DM)), ("y_sample", (NB, 1, DM)),
         ("new_pool_prompt", (DEPTH, 1, PST, 256)), ("new_C_prompt", (DEPTH, 1, H, DH, DH)),
         ("new_n_prompt", (DEPTH, 1, H, DH)), ("new_m_prompt", (DEPTH, 1, H)),
         ("new_pool_sample", (DEPTH, NB, PST, 256)), ("new_C_sample", (DEPTH, NB, H, DH, DH)),
         ("new_n_sample", (DEPTH, NB, H, DH)), ("new_m_sample", (DEPTH, NB, H)),
         ("new_gmlp_v_sample", (DEPTH, NB, 1, 256))]


def kernel(**inputs):
    import numpy as np
    import concourse.bacc as bacc
    from concourse import mybir as mb
    from concourse.bass_utils import run_bass_kernel_spmd

    const = np.zeros((P, NCONST), np.float32)
    const[:, C_ID:C_ID + P] = np.eye(P)
    const[:64, C_BLK:C_BLK + 64] = 1 / 64
    const[64:, C_BLK + 64:C_BLK + P] = 1 / 64
    const[:, C_TRI:C_TRI + P] = np.triu(np.ones((P, P)))
    const[:, C_ONE], const[:, C_MEAN], const[:, C_MEANH] = 1, 1 / DM, 1 / DH
    for g, w in enumerate(WINDOWS):
        rows, j = slice(64 * (g % 2), 64 * (g % 2) + 64), g // 2
        const[rows, C_INVW + j] = 1 / w
        const[rows, C_RC + 16 * j:C_RC + 16 * j + 16] = 1 / np.minimum(w, np.arange(16) + 1)

    nc = bacc.Bacc("TRN2", target_bir_lowering=False, num_devices=1)
    arrays, A, O = {}, {}, {}
    for name in _INS + ["shape_constants"]:
        a = np.ascontiguousarray(const if name == "shape_constants" else inputs[name])
        arrays[f"in_{name}"] = a
        A[name] = nc.dram_tensor(f"in_{name}", a.shape, mb.dt.from_np(a.dtype), kind="ExternalInput").ap()
    for name, shape in _OUTS:
        O[name] = nc.dram_tensor(f"out_{name}", shape, mb.dt.float32, kind="ExternalOutput").ap()
    build(nc, A, O)
    r = run_bass_kernel_spmd(nc, [arrays], core_ids=[0])
    return tuple(r.results[0][f"out_{name}"] for name, _ in _OUTS)
```

```python
import concourse.bass as bass
from concourse import mybir
from contextlib import ExitStack

f32 = mybir.dt.float32
f32r = mybir.dt.float32r
u32 = mybir.dt.uint32
ACT = mybir.ActivationFunctionType
ALU = mybir.AluOpType
AXX = mybir.AxisListType.X

P = 128
DEPTH, DM, SEQ, NB = 2, 1024, 512, 8
TOK = SEQ + NB
HALF = TOK // 2
DC = DM // P
TT = SEQ // P
H, DH = 4, 128
NE, FS = 8, 1408
FCH = FS // P
KMAX = FCH
EPS = 1e-6
QS = float(DH) ** -0.5
PLE = 256
WINDOWS = (2, 4, 8, 16)
PST = 15
D_IN = 2824
GATE_COL = 2304
GW = 36
Z_POOL, Z_Q, Z_K, Z_V, Z_O, Z_GU, Z_GV = 0, 2, 6, 10, 14, 18, 20
WIN_P, WOUT_P, GU_P, DOWN_P, PLE_P = 11, 4, 11, 4, 8
CAP = 160
CAP2 = CAP - P
NMIN = 192
NSLOT = NE * CAP
SLICES = (2, NE)


def win_base(L):
    return 0 if L == 0 else ple_base(0) + PLE_P


def wout_base(L):
    return win_base(L) + WIN_P


def ffn_base(L):
    return wout_base(L) + WOUT_P


def ple_base(L):
    return ffn_base(L) + SLICES[L] * (GU_P + DOWN_P)


LAST_PAIR = ple_base(DEPTH - 1) + PLE_P - 1
MIX_PRE, MIX_POST, FFN_PRE, FFN_POST, PLE_PRE = range(5)
R_F, R_IG, R_EM, R_G, R_M, R_A = range(6)
C_ID, C_BLK, C_TRI, C_ONE, C_MEAN, C_MEANH, C_INVW, C_RC, C_VAL = 0, 128, 256, 384, 385, 386, 387, 389, 421
NCONST = C_VAL + 5


def build(nc, A, O):
    ctx = ExitStack()
    with ctx:
        def sb(name, shape, dt=f32):
            return ctx.enter_context(nc.sbuf_tensor(name, shape, dt))

        def sem(name):
            return ctx.enter_context(nc.semaphore(name))

        x = sb("x", [P, DC, TOK])
        with nc.sbuf_tensor("z_before_xg", [P, 8 * TOK], f32), \
                nc.sbuf_tensor("xg", [P, DC, 2, CAP], f32r) as xg:
            pass
        zreg = sb("zreg", [P, 23 * TOK])
        z = zreg[:, :].rearrange("p (c t) -> p c t", t=TOK)
        acc = z[:, 0:8]
        sq = z[:, 8:12]
        ht = z[:, 12:14]
        rn = z[:, 14]
        sg = z[:, 15]
        gt = z[:, 16]
        ut = z[:, 17:19]
        p_tok = zreg[:, 19 * TOK:19 * TOK + 5 * PLE].rearrange("p (t c) -> p t c", c=PLE)
        gb = z[:, 22]
        xs = zreg[:, 17 * TOK:17 * TOK + 2 * DM].rearrange("p (a c) -> p a c", c=DM)
        x_tok = zreg[:, 0:5 * DM].rearrange("p (t c) -> p t c", c=DM)
        y_tok = zreg[:, 0:2 * DM].rearrange("p (t c) -> p t c", c=DM)
        with nc.sbuf_tensor("h_hi", [P, DC, TOK], f32r) as h_hi, \
                nc.sbuf_tensor("h_lo", [P, DC, TOK], f32r) as h_lo:
            pass
        ra = sb("region_a", [P, 2 * DC * TOK])
        with nc.sbuf_tensor("gs", [P, FCH, 2, CAP], f32r) as gs:
            pass
        with nc.sbuf_tensor("htok", [P, 5, DM], f32) as htok:
            pass
        with nc.sbuf_tensor("yrow", [P, 2, 2, DM], f32) as yrow, nc.sbuf_tensor("ctok", [P, 2, DM], f32) as ctok:
            pass
        with nc.sbuf_tensor("gu_hi", [P, FCH, TOK], f32r) as gu_hi, \
                nc.sbuf_tensor("gu_lo", [P, FCH, TOK], f32r) as gu_lo:
            pass
        y_hi = sb("y_hi", [P, DC, TOK], f32r)
        y_lo = sb("y_lo", [P, DC, TOK], f32r)
        rb = sb("region_b", [P, 2 * (FCH - DC) * TOK])
        EXT = PST + SEQ
        with nc.sbuf_tensor("p_hi", [P, 2, TOK], f32r) as p_hi, \
                nc.sbuf_tensor("p_lo", [P, 2, TOK], f32r) as p_lo:
            pass
        rc = sb("region_c", [P, 2, 2, EXT])
        wst = sb("wst", [P, 2, KMAX * P])
        whi = sb("whi", [P, 2, KMAX * P], f32r)
        wlo = sb("wlo", [P, 2, KMAX * P], f32r)
        with nc.sbuf_tensor("ys", [P, 2, DM], f32) as ys, nc.sbuf_tensor("ytb", [P, 2, CAP], f32) as ytb:
            pass
        rows = sb("rows", [H, 6, TOK])
        const = sb("const", [P, NCONST])
        cols = sb("cols", [P, 96])
        colrows = ra[0:96, 0:P]
        gwf = sb("gwf", [P, DC * GW + 92])
        gwh = sb("gwh", [P, DC * GW + 92], f32r)
        gwl = sb("gwl", [P, DC * GW + 92], f32r)
        bdw = sb("bdw", [P, 2, P])
        gate_b = sb("gate_b", [H, 2, DEPTH])
        sg_b = sb("sg_b", [P, 2, DEPTH, 2])
        bsr = sb("bsr", [4, DEPTH, P])
        m0 = sb("m0", [H, DEPTH, NB])
        tsm = sb("tsm", [H, NB])
        epsc = sb("epsc", [P, 1])
        spare = sb("spare", [P, 1])
        rwf = sb("rwf", [P, DC, NE])
        rwh = sb("rwh", [P, DC, NE], f32r)
        rwl = sb("rwl", [P, DC, NE], f32r)
        rbias = sb("rbias", [P, NE])
        lg = sb("lg", [P, 5, NE])
        top = sb("top", [P, 5, 8])
        topi = sb("topi", [P, 5, 8], u32)
        topf = sb("topf", [P, 5, 8])
        gwt = sb("gwt", [P, 5, 2])
        oh = sb("oh", [P, 2, 5, NE])
        msk = sb("msk", [P, 5, NE])
        rel = sb("rel", [P, 5, NE])
        fits = sb("fits", [P, NE])
        fitu = sb("fitu", [P, NE], u32)
        idxf = sb("idxf", [P, 5, 2])
        idxu = sb("idxu", [P, 5, 2], u32)
        pick_e = sb("pick_e", [NE, P])
        gatet = sb("gatet", [P, 5, NE])
        gtmp = sb("gtmp", [P, 5, NE])
        iota8 = sb("iota8", [P, NE])
        grow = sb("grow", [NE, TOK])

        def view(region, at, *shape):
            n = 1
            for s in shape:
                n *= s
            v = region[:, at:at + n]
            if len(shape) == 2:
                v = v.rearrange("p (a b) -> p a b", b=shape[1])
            if len(shape) == 3:
                v = v.rearrange("p (a b c) -> p a b c", b=shape[1], c=shape[2])
            return v, at + n

        vtok, a = view(ra, 0, TT, 129)
        ktok, a = view(ra, a, TT, P)
        kw, a = view(ra, a, TT, P)
        E, a = view(ra, a, 2, SEQ)
        W, a = view(ra, a, 2, SEQ)
        a_nd = a
        num, a = view(ra, a, H, TOK)
        D, a = view(ra, a, H, TOK)
        Cout, a = view(ra, a, 129)
        acol, a = view(ra, a, TT, H)
        kws, a = view(ra, a, H, NB)
        dcs, a = view(ra, a, H, 3, NB)
        nT, a = view(ra, a, NB, H)
        nn, a = view(ra, a, NB, H)
        qn, a = view(ra, a, H, NB)
        assert a <= 2 * DC * TOK
        wsr, a = view(ra, a_nd, 4, P)
        wmT, a = view(ra, a, 4, P)
        vnt, a = view(ra, a, 2, TT, P)
        assert a <= a_nd + H * TOK
        gsq, a = view(ra, a_nd + H * TOK, 2, TOK)
        gr, a = view(ra, a, 2, TOK)
        Cb, a = view(rb, 0, 3, H, P)
        Ct, a = view(rb, a, H, P)
        vs, a = view(rb, a, H, P)
        us, a = view(rb, a, 2, P)
        nst, a = view(rb, a, P)
        nout, a = view(rb, a, P)
        assert a <= 2 * (FCH - DC) * TOK
        pst = Ct[:, :, :].rearrange("p a b -> p (a b)")[:, 0:256]
        gvo = Ct[:, :, :].rearrange("p a b -> p (a b)")[:, 256:512]
        hs1, hs2 = E[:, :, :].rearrange("p a b -> p (a b)"), W[:, :, :].rearrange("p a b -> p (a b)")

        ident = const[:, C_ID:C_ID + P]
        blk = const[:, C_BLK:C_BLK + P]
        tri = const[:, C_TRI:C_TRI + P]
        one = const[:, C_ONE:C_ONE + 1]

        def bcol(c):
            return const[:, c:c + 1].to_broadcast([P, P])

        def pick(k, n, m=P):
            return const[0:k, n:n + 1].to_broadcast([k, m])

        def two(ap):
            return ap.rearrange("p (a b) -> p a b", b=HALF)

        xslot = nc.dram_tensor("xslot", ((NE + 1) * CAP, DM), f32).ap()
        yslot = nc.dram_tensor("yslot", (NSLOT + 1, DM), f32).ap()
        lin = ctx.enter_context(nc.psum_tensor("lin", [P, 4, 512], f32))
        aux = ctx.enter_context(nc.psum_tensor("aux", [P, 4, 512], f32))

        staged = [sem("staged0"), sem("staged1")]
        hi_done, lo_done = sem("hi_done"), sem("lo_done")
        pe_slab = sem("pe_slab")
        pair_free = [sem("pair_free0"), sem("pair_free1")]
        x_in, c_in, w_small = sem("x_in"), sem("c_in"), sem("w_small")
        setup_pool = sem("setup_pool")
        cols_t, cols_ok = sem("cols_t"), sem("cols_ok")
        x_t, x_ok, xs_t = sem("x_t"), sem("x_ok"), sem("xs_t")
        sq_ready, sq_used, stats = sem("sq_ready"), sem("sq_used"), sem("stats")
        r_ready = sem("r_ready")
        ht_ready, h_hi_ok, h_ready = sem("ht_ready"), sem("h_hi_ok"), sem("h_ready")
        ut_ready, x_upd, ple_x = sem("ut_ready"), sem("x_upd"), sem("ple_x")
        gw_in, gw_ok, gw_lo = sem("gw_in"), sem("gw_ok"), sem("gw_lo")
        gates = sem("gates")
        gate_l1, gate_lf, gate_scan, gate_g, gate_em = (sem(s) for s in
                                                        ("gate_l1", "gate_lf", "gate_scan", "gate_g", "gate_em"))
        lay_in = sem("lay_in")
        pw_zero = sem("pw_zero")
        m_out = sem("m_out")
        pool_win, pool_t, pool_v, pool_y = sem("pool_win"), sem("pool_t"), sem("pool_v"), sem("pool_y")
        pool_mm, pool_e = sem("pool_mm"), sem("pool_e")
        g_sq, g_mean, g_r, g_vn, g_t, g_ev, g_wm, g_wt, g_mix, g_y = (
            sem(s) for s in ("g_sq", "g_mean", "g_r", "g_vn", "g_t", "g_ev", "g_wm", "g_wt", "g_mix", "g_y"))
        acol_t, acol_ok = sem("acol_t"), sem("acol_ok")
        st_t, st_ev, st_k, st_den, st_de, st_dd = (sem(s) for s in ("st_t", "st_ev", "st_k", "st_den", "st_de", "st_dd"))
        C_in = [sem(f"C_in{i}") for i in range(3)]
        C_st = sem("C_st")
        vb_ready, ct_ready, cn_ready, cq_done = sem("vb_ready"), sem("ct_ready"), sem("cn_ready"), sem("cq_done")
        st_num = sem("st_num")
        kv_t, kv_ev, gb_ready, e_ready, e_mask, s_ready, w_ready, w_used = (
            sem(s) for s in ("kv_t", "kv_ev", "gb_ready", "e_ready", "e_mask", "s_ready", "w_ready", "w_used"))
        nd_ready, nd_ev, nd_max, kw_ready, c_ready, c_ev, c_out = (
            sem(s) for s in ("nd_ready", "nd_ev", "nd_max", "kw_ready", "c_ready", "c_ev", "c_out"))
        hq, hm, hd2, ha, hr, hy, hy2 = (sem(s) for s in ("hq", "hm", "hd2", "ha", "hr", "hy", "hy2"))
        sig_o, y_hi_ok, y_ok = sem("sig_o"), sem("y_hi_ok"), sem("y_ok")
        p_in, p_t, p_hi_ok, p_ok = sem("p_in"), sem("p_t"), sem("p_hi_ok"), sem("p_ok")
        gt_ready, gu_hi_ok, gu_ok = sem("gt_ready"), sem("gu_hi_ok"), sem("gu_ok")
        acc0 = sem("acc0")
        hx_t, hx_ok, x_zero, rt_oh, rt_cnt, rt_idx, xs_scat, xs_in, xg_t, xg_hi, xg_ok, pk = (
            sem(s) for s in ("hx_t", "hx_ok", "x_zero", "rt_oh", "rt_cnt", "rt_idx", "xs_scat", "xs_in", "xg_t", "xg_hi",
                             "xg_ok", "pk"))
        silu_ok = sem("silu_ok")
        yx_t, ys_ok, y_stored, cb_a, cb_b, cb_t, cb_acc = (
            sem(s) for s in ("yx_t", "ys_ok", "y_stored", "cb_a", "cb_b", "cb_t", "cb_acc"))
        y_back = [sem("y_back0"), sem("y_back1")]
        rw_ok, rw_lo, rt_lg, rt_max, rt_e, rt_gate, rt_t, rt_row, gb_mm, gb_ok = (
            sem(s) for s in ("rw_ok", "rw_lo", "rt_lg", "rt_max", "rt_e", "rt_gate", "rt_t", "rt_row", "gb_mm", "gb_ok"))
        yt_t, yt_ev, out_st = sem("yt_t"), sem("yt_ev"), sem("out_st")
        y_st = [sem("y_st0"), sem("y_st1")]
        ctx.enter_context(nc.allow_non_contiguous_dma(reason="per-head rows and state columns are a few words each"))
        block = ctx.enter_context(nc.Block())

        def kcs(phase):
            return {"win": (8, 8), "wout": (8, 8), "gu": (8, 8), "down": (11, 11), "ple": (8, 2)}[phase]

        @block.sync
        def _(sp):
            tokp = A["x_prompt"][0].rearrange("(t p) c -> p t c", p=P)
            for t in range(TT):
                sp.dma_start(x_tok[:, t, :], tokp[:, t, :]).then_inc(x_in, 16)
            sp.dma_start(x_tok[0:NB, TT, :], A["x_sample"][:, 0, :]).then_inc(x_in, 16)

            def load(q, s, src, kc, n):
                if not (isinstance(q, int) and q == 0):
                    sp.wait_ge(hi_done, q * 2 + (s - 1))
                    sp.wait_ge(lo_done, q * 2 + (s - 1))
                sp.dma_start(wst[:, s, 0:kc * n].rearrange("p (k n) -> p k n", n=n), src).then_inc(staged[s], 16)

            def cut(w, c):
                return w.rearrange("(k p) n -> p k n", p=P)[:, :, bass.ds(c, P)]

            for L in range(DEPTH):
                w_in = A["w_in"][L]
                b = win_base(L)
                if L == 0:
                    for s in range(2):
                        load(0, s, cut(w_in, s * P), DC, P)
                with sp.Fori(1 if L == 0 else 0, Z_GU // 2) as i:
                    for s in range(2):
                        load(i + b, s, cut(w_in, i * 2 * P + s * P), DC, P)
                for i in range(Z_GU // 2, WIN_P):
                    for s in range(2):
                        load(i + b, s, cut(w_in, (2 * i + s) * P + 2 * H), DC, P)
                with sp.Fori(0, WOUT_P) as i:
                    for s in range(2):
                        load(i + wout_base(L), s, cut(A["w_out"][L], i * 2 * P + s * P), DC, P)
                if L == 0:
                    for e in range(SLICES[0]):
                        with sp.Fori(0, GU_P) as i:
                            for s, w in enumerate(("ffn_w_gate", "ffn_w_up")):
                                load(i + ffn_base(0) + e * (GU_P + DOWN_P), s, cut(A[w][0], i * P + e * FS), DC, P)
                        with sp.Fori(0, DOWN_P) as i:
                            for s in range(2):
                                load(i + ffn_base(0) + e * (GU_P + DOWN_P) + GU_P, s,
                                     cut(A["ffn_w_down"][0, e * FS:(e + 1) * FS], i * 2 * P + s * P), FCH, P)
                else:
                    with sp.Fori(0, NE) as e:
                        def expert(w):
                            return A[w][0][bass.ds(e, 1)].rearrange("a (k p) n -> p (a k) n", p=P)
                        with sp.Fori(0, GU_P) as i:
                            for s, w in enumerate(("moe_w_gate", "moe_w_up")):
                                load(i + (e * (GU_P + DOWN_P) + ffn_base(1)), s,
                                     expert(w)[:, :, bass.ds(i * P, P)], DC, P)
                        with sp.Fori(0, DOWN_P) as i:
                            for s in range(2):
                                load(i + (e * (GU_P + DOWN_P) + (ffn_base(1) + GU_P)), s,
                                     expert("moe_w_down")[:, :, bass.ds(i * 2 * P + s * P, P)], FCH, P)
                with sp.Fori(0, PLE_P) as i:
                    load(i + ple_base(L), 0, cut(A["ple_w_gate"][L], i * P), DC, P)
                    load(i + ple_base(L), 1, cut(A["ple_w_proj"][L], i * P), 2, P)
            for t in range(TT + 1):
                sp.wait_ge(yt_ev, t + 1)
                if t < TT:
                    sp.dma_start(O["y_prompt"][0, t * P:(t + 1) * P, :], y_tok[:, t % 2, :]).then_inc(y_st[t % 2], 16)
                else:
                    sp.dma_start(O["y_sample"][:, 0, :], y_tok[0:NB, t % 2, :]).then_inc(y_st[t % 2], 16)
            sp.wait_ge(y_st[0], 16 * 3)
            sp.wait_ge(y_st[1], 16 * 2)

        @block.gpsimd
        def _(pool):
            pool.dma_start(const[:, :], A["shape_constants"]).then_inc(c_in, 16)
            for n, w in enumerate(("norm_mix_pre", "norm_mix_post", "norm_ffn_pre", "norm_ffn_post", "norm_ple")):
                pool.dma_start(colrows[16 * n:16 * n + 16, :],
                               A[w].rearrange("l (c p) -> (l c) p", p=P)).then_inc(c_in, 16)
            pool.dma_start(colrows[80:84, :], A["pool_scale"].rearrange("l (c p) -> (l c) p", p=P)).then_inc(c_in, 16)
            pool.dma_start(colrows[84:92, :], A["mlstm_norm_w"].rearrange("l (c p) -> (l c) p", p=P)).then_inc(c_in, 16)
            pool.dma_start(colrows[92:96, :], A["gmlp_norm_w"].rearrange("l (c p) -> (l c) p", p=P)).then_inc(c_in, 16)
            nsmall = 0
            small = [(gate_b[:, 0, :], A["mlstm_b_i"].rearrange("l h -> h l")),
                     (gate_b[:, 1, :], A["mlstm_b_f"].rearrange("l h -> h l")),
                     (rbias[:, :], A["moe_router_b"][0].partition_broadcast(P)),
                     (bsr[:, :, :], A["gmlp_bs"].rearrange("l g t -> g l t")),
                     (rwf[:, :, :], A["moe_router_w"][0].rearrange("(k p) n -> p k n", p=P))]
            for L in range(DEPTH):
                small.append((m0[:, L, :], A["state_mlstm_m"][L].rearrange("b h -> h b")))
                for g in range(4):
                    at = slice(64 * (g % 2), 64 * (g % 2) + 64)
                    small.append((sg_b[at, 0, L, g // 2:g // 2 + 1], A["gmlp_ws"][L, g, 0, 0:1].partition_broadcast(64)))
                    small.append((sg_b[at, 1, L, g // 2:g // 2 + 1], A["gmlp_bs"][L, g, 0:1].partition_broadcast(64)))
            for dst, src in small:
                pool.dma_start(dst, src).then_inc(w_small, 16)
                nsmall += 16
            pool.memset(gwf[:, :], 0.0)
            pool.memset(epsc[:, :], EPS)
            pool.memset(bdw[:, :, :], 0.0)
            pool.iota(topi[:, 0, :], pattern=[[1, NE]], base=0, channel_multiplier=0)
            pool.drain()
            pool.tensor_copy(iota8[:, :], topi[:, 0, :]).then_inc(setup_pool, 1)
            pool.memset(rb[:, 0:DM], 0.0)
            pool.memset(lg[:, :, :], 0.0)
            pool.drain()
            xflat = xslot.rearrange("(p r) c -> p (r c)", r=12)
            for n in range(12):
                pool.dma_start(xflat[:, n * DM:(n + 1) * DM], rb[0:(NE + 1) * CAP // 12, 0:DM]).then_inc(x_zero, 16)
            for n in range(2):
                pool.dma_start(yslot[NSLOT:NSLOT + 1, n * 512:(n + 1) * 512], rb[0:1, 0:512]).then_inc(y_stored, 16)
            pool.wait_ge(w_small, nsmall)
            pool.wait_ge(x_zero, 16 * 12)
            pool.wait_ge(y_stored, 32)

            def add_x(N):
                for c in range(DC):
                    pool.wait_ge(ut_ready, N * DC + c + 1)
                    pool.tensor_tensor(x[:, c], x[:, c], ut[:, c % 2], ALU.add).then_inc(x_upd, 1)

            for L in range(DEPTH):
                if L:
                    pool.wait_ge(h_ready, DC * 3 * L)
                pool.wait_ge(setup_pool, 1)
                gsrc = A["w_in"][L].rearrange("(k p) n -> p k n", p=P)
                gdst = gwf[:, 0:DC * GW].rearrange("p (k n) -> p k n", n=GW)
                pool.dma_start(gdst[:, :, 0:H], gsrc[:, :, GATE_COL:GATE_COL + H]).then_inc(gw_in, 16)
                pool.dma_start(gdst[:, :, 32:32 + H], gsrc[:, :, GATE_COL + H:GATE_COL + 2 * H]).then_inc(gw_in, 16)
                for g in range(4):
                    o = 64 * (g % 2)
                    pool.dma_start(bdw[o:o + 64, g // 2, o:o + 64], A["pool_w"][L, g]).then_inc(lay_in, 16)
                if L:
                    pool.wait_ge(pair_free[1], ple_base(0) + 1)
                pool.dma_start(pst[0:NB * PST, :], A["state_pool"][L].rearrange("b r c -> (b r) c")).then_inc(lay_in, 16)
                pool.dma_start(nst[0:NB * H, :], A["state_mlstm_n"][L].rearrange("b h k -> (b h) k")).then_inc(lay_in, 16)
                pool.dma_start(O["new_pool_sample"][L, :, 0:PST - 1, :], A["state_pool"][L, :, 1:PST, :]).then_inc(out_st, 16)
                pool.wait_ge(gate_l1, L + 1)
                pool.tensor_scalar(rows[:, R_F], rows[:, R_F], 0.0, None, ALU.min)
                pool.drain()
                pool.tensor_tensor(rows[:, R_F], rows[:, R_F], rows[:, R_EM], ALU.subtract)
                pool.drain()
                pool.memset(rows[:, R_A], 0.0)
                pool.tensor_tensor(tsm[:, :], rows[:, R_F, SEQ:TOK], m0[:, L, :], ALU.add).then_inc(gate_lf, 1)
                pool.wait_ge(pair_free[1], win_base(L) + WIN_P)
                pool.dma_start(wsr[:, :, :], A["gmlp_ws"][L].rearrange("g t s -> t g s")).then_inc(lay_in, 16)
                for b in range(3):
                    pool.dma_start(Cb[:, b], A["state_mlstm_C"][L, b].rearrange("h k v -> k h v")).then_inc(C_in[b], 16)
                pool.memset(rc[:, :, :, 0:PST], 0.0)
                pool.tensor_copy(rc[:, 0, :, PST:EXT], z[:, Z_POOL:Z_POOL + 2, 0:SEQ])
                pool.drain()
                src = 0
                for g, w in enumerate(WINDOWS):
                    sh = w // 2
                    lo = 64 if g % 2 else 0
                    j = g // 2
                    pool.tensor_tensor(rc[:, 1 - src, :, PST:EXT], rc[:, src, :, PST:EXT],
                                       rc[:, src, :, PST - sh:EXT - sh], ALU.add)
                    pool.drain()
                    src = 1 - src
                    s_ = rc[lo:lo + 64, src, j, PST:EXT]
                    zz = z[lo:lo + 64, Z_POOL + j, 0:SEQ]
                    pool.tensor_tensor(gsq[lo:lo + 64, j, 0:16], s_[:, 0:16],
                                       const[lo:lo + 64, C_RC + 16 * j:C_RC + 16 * j + 16], ALU.mult)
                    pool.tensor_scalar(gsq[lo:lo + 64, j, 16:SEQ], s_[:, 16:SEQ],
                                       const[lo:lo + 64, C_INVW + j:C_INVW + j + 1], None, ALU.mult)
                    pool.drain()
                    ins = pool.tensor_tensor(gsq[lo:lo + 64, j, 0:SEQ], gsq[lo:lo + 64, j, 0:SEQ], zz, ALU.subtract)
                    if g < 3:
                        pool.drain()
                ins.then_inc(pool_win, 1)
                pool.wait_ge(gate_scan, L + 1)
                pool.tensor_tensor(rows[:, R_A, 0:SEQ], rows[:, R_IG, 0:SEQ], rows[:, R_G, 0:SEQ], ALU.subtract)
                pool.tensor_tensor(rows[:, R_A, SEQ:TOK], rows[:, R_IG, SEQ:TOK], rows[:, R_M, SEQ:TOK], ALU.subtract)
                pool.drain()
                pool.tensor_tensor(rows[:, R_G, 0:SEQ], rows[:, R_G, 0:SEQ], rows[:, R_M, 0:SEQ], ALU.subtract)
                pool.tensor_tensor(rows[:, R_G, SEQ:TOK], tsm[:, :], rows[:, R_M, SEQ:TOK],
                                   ALU.subtract).then_inc(gate_g, 1)
                pool.wait_ge(gate_g, L + 1)
                pool.dma_start(O["new_m_prompt"][L].rearrange("a h -> h a"), rows[:, R_M, SEQ - 1:SEQ]).then_inc(m_out, 16)
                pool.dma_start(O["new_m_sample"][L].rearrange("b h -> h b"), rows[:, R_M, SEQ:TOK]).then_inc(m_out, 16)
                pool.wait_ge(pool_e, 2 * L + 2)
                pool.dma_start(O["new_pool_sample"][L, :, PST - 1, :], us[0:NB, :, :].rearrange("p a b -> p (a b)")).then_inc(out_st, 16)
                pool.dma_start(O["new_pool_prompt"][L, 0], us[32:32 + PST, :, :].rearrange("p a b -> p (a b)")).then_inc(out_st, 16)
                pool.wait_ge(g_ev, 3 * L + 3)
                pool.dma_start(O["new_gmlp_v_sample"][L, :, 0, :], gvo[0:NB, :]).then_inc(out_st, 16)
                for b in range(NB):
                    pool.wait_ge(cn_ready, NB * L + b + 1)
                    pool.dma_start(O["new_C_sample"][L, b].rearrange("h k v -> k h v"), Cb[:, b % 3]).then_inc(C_st, 16)
                    if b + 3 < NB:
                        pool.wait_ge(C_st, 16 * (NB * L + b + 1))
                        pool.wait_ge(cq_done, NB * L + b + 1)
                        pool.dma_start(Cb[:, b % 3], A["state_mlstm_C"][L, b + 3].rearrange("h k v -> k h v")).then_inc(C_in[b % 3], 16)
                pool.wait_ge(st_de, 2 * L + 2)
                pool.dma_start(O["new_n_sample"][L].rearrange("b h k -> (b h) k"), nout[0:NB * H, :]).then_inc(out_st, 16)
                for h in range(H):
                    hn = H * L + h
                    for i in range(TT):
                        n = TT * hn + i
                        w = SEQ - P * i
                        pool.wait_ge(e_ready, n + 1)
                        pool.affine_select(out=E[:, i % 2, 0:P], in_=E[:, i % 2, 0:P], compare_op=ALU.is_ge, fill=0.0,
                                           base=0, pattern=[[1, P]], channel_multiplier=-1).then_inc(e_mask, 1)
                        pool.wait_ge(kv_ev, hn + 1)
                        if i == 3:
                            pool.wait_ge(e_mask, n + 1)
                        if i == 0 and h:
                            pool.wait_ge(c_ready, hn)
                        pool.tensor_scalar(kw[:, i], ktok[:, i], E[:, i % 2, w - 1:w], None, ALU.mult).then_inc(kw_ready, 1)
                    pool.wait_ge(c_ev, hn + 1)
                    pool.dma_start(O["new_C_prompt"][L, 0, h], Cout[:, 0:P]).then_inc(c_out, 16)
                    pool.dma_start(O["new_n_prompt"][L, 0, h].rearrange("(k a) -> k a", a=1), Cout[:, P:P + 1]).then_inc(c_out, 16)
                for h in range(H):
                    hn = H * L + h
                    if h == 0:
                        pool.wait_ge(st_dd, L + 1)
                        pool.wait_ge(nd_max, H * (L + 1))
                    pool.tensor_tensor(D[:, h], D[:, h], D[:, h], ALU.mult).then_inc(hd2, 1)
                pool.wait_ge(sig_o, L + 1)
                for h in range(H):
                    hn = H * L + h
                    pool.wait_ge(hy, hn + 1)
                    pool.tensor_tensor(z[:, Z_O + h], num[:, h], z[:, Z_O + h], ALU.mult).then_inc(hy2, 1)
                pool.wait_ge(y_ok, L + 1)
                pool.dma_start(p_tok[:, 0:TT, :], A["p_prompt"][L, 0].rearrange("(t p) c -> p t c", p=P)).then_inc(p_in, 16)
                pool.dma_start(p_tok[0:NB, TT, :], A["p_sample"][L, :, 0, :]).then_inc(p_in, 16)
                add_x(2 * L)
                pool.wait_ge(r_ready, 5 * L + 3)
                if L:
                    pool.memset(ytb[:, :, :], 0.0)
                pool.memset(acc[:, :, :], 0.0).then_inc(acc0, 1)
                if L:
                    pool.wait_ge(hx_ok, DC)
                    pool.wait_ge(rt_idx, 1)
                    for t in range(5):
                        n = P if t < TT else NB
                        for k in range(2):
                            pool.indirect_dma_start(out=xslot[:, :], out_offset=bass.IndirectOffsetOnAxis(ap=idxu[0:n, t, k:k + 1], axis=0),
                                                    in_=htok[0:n, t, :], in_offset=None, bounds_check=NSLOT - 1,
                                                    oob_is_err=False).then_inc(xs_scat, 16)
                    pool.wait_ge(xs_scat, 16 * 10)

                    def load_slots(at):
                        pool.dma_start(xs[:, 0, :], xslot[bass.ds(at, P), :]).then_inc(xs_in, 16)
                        pool.dma_start(xs[0:CAP2, 1, :], xslot[bass.ds(at + P, CAP2), :]).then_inc(xs_in, 16)
                    load_slots(0)
                    with pool.Fori(0, NE) as e:
                        pool.wait_ge(xg_t, e * DC + DC)
                        load_slots(e * CAP + CAP)
                        pool.wait_ge(ys_ok, e * DC + DC)
                        pool.dma_start(yslot[bass.ds(e * CAP, P), :], ys[:, 0, :]).then_inc(y_stored, 16)
                        pool.dma_start(yslot[bass.ds(e * CAP + P, CAP2), :], ys[0:CAP2, 1, :]).then_inc(y_stored, 16)
                    pool.wait_ge(y_stored, 32 * (NE + 1))
                    for t in range(5):
                        n = P if t < TT else NB
                        if t >= 2:
                            pool.wait_ge(cb_b, t - 1)
                        for k in range(2):
                            pool.indirect_dma_start(out=yrow[0:n, t % 2, k, :], out_offset=None, in_=yslot[:, :],
                                                    in_offset=bass.IndirectOffsetOnAxis(ap=idxu[0:n, t, k:k + 1], axis=0),
                                                    bounds_check=NSLOT, oob_is_err=False).then_inc(y_back[t % 2], 16)
                add_x(2 * L + 1)
            pool.wait_ge(out_st, 16 * 5 * DEPTH)
            pool.wait_ge(m_out, 16 * 2 * DEPTH)
            pool.wait_ge(c_out, 16 * 2 * H * DEPTH)
            pool.wait_ge(C_st, 16 * NB * DEPTH)

        @block.tensor
        def _(pe):
            def mm(out, lhsT, rhs, start=True, stop=True):
                return nc.tensor.matmul(out, lhsT, rhs, start=start, stop=stop)

            pe.wait_ge(c_in, 16 * 9)
            nc.tensor.transpose(aux[:, 3, 0:96], colrows[0:96, :], ident[0:96, 0:96]).then_inc(cols_t, 1)
            pe.wait_ge(x_in, 16 * 5)
            for c in range(DC):
                if c >= 3:
                    pe.wait_ge(x_ok, c - 2)
                for t in range(TT):
                    last = nc.tensor.transpose(aux[:, c % 3, t * P:(t + 1) * P], x_tok[:, t, c * P:(c + 1) * P], ident)
                last.then_inc(x_t, 1)
            for c in range(DC):
                last = nc.tensor.transpose(lin[:, 0, c * NB:(c + 1) * NB], x_tok[0:NB, TT, c * P:(c + 1) * P], ident[0:NB, 0:NB])
            last.then_inc(xs_t, 1)

            def norm(N):
                for c in range(DC):
                    pe.wait_ge(sq_ready, N * DC + c + 1)
                    for a in range(2):
                        last = mm(aux[:, a, 0:HALF], bcol(C_MEAN), two(sq[:, c % 4])[:, a], c == 0, c == DC - 1)
                    last.then_inc(sq_used, 1)

            def slab(q, s, kc, rhs_hi, rhs_lo):
                pe.wait_ge(lo_done, q * 2 + (s + 1))
                if not (isinstance(q, int) and q == 0):
                    pe.wait_ge(pair_free[s], q)
                for k in range(kc):
                    whk, wlk = whi[:, s, k * P:(k + 1) * P], wlo[:, s, k * P:(k + 1) * P]
                    st, en = k == 0, k == kc - 1
                    for a in range(2):
                        o = lin[:, 2 * s + a, 0:HALF]
                        mm(o, whk, two(rhs_hi[:, k])[:, a], st, False)
                        mm(o, whk, two(rhs_lo[:, k])[:, a], False, False)
                    for a in range(2):
                        last = mm(lin[:, 2 * s + a, 0:HALF], wlk, two(rhs_hi[:, k])[:, a], False, en)
                last.then_inc(pe_slab, 1)

            def stream(base, pairs, kc, rhs):
                first = 1 if isinstance(base, int) and base == 0 else 0
                for q in range(first):
                    for s in range(2):
                        slab(0, s, kc[s], *rhs[s])
                with pe.Fori(first, pairs) as i:
                    for s in range(2):
                        slab(i + base, s, kc[s], *rhs[s])

            hh, yy, gg, pp = (h_hi, h_lo), (y_hi, y_lo), (gu_hi, gu_lo), (p_hi, p_lo)
            for L in range(DEPTH):
                norm(5 * L)
                pe.wait_ge(gw_lo, L + 1)
                for k in range(DC):
                    pe.wait_ge(h_ready, DC * 3 * L + k + 1)
                    gk = slice(k * GW, k * GW + P)
                    for a in range(2):
                        o = aux[:, 2 + a, 0:HALF]
                        mm(o, gwh[:, gk], two(h_hi[:, k])[:, a], k == 0, False)
                        mm(o, gwh[:, gk], two(h_lo[:, k])[:, a], False, False)
                        last = mm(o, gwl[:, gk], two(h_hi[:, k])[:, a], False, k == DC - 1)
                last.then_inc(gates, 1)
                stream(win_base(L), WIN_P, kcs("win"), (hh, hh))

                pe.wait_ge(pair_free[1], win_base(L) + WIN_P)
                pe.wait_ge(lay_in, 16 * 7 * (L + 1))
                for j in range(2):
                    nc.tensor.transpose(aux[0:NB, 0, j * P:(j + 1) * P], z[:, Z_POOL + j, SEQ:TOK], ident)
                    nc.tensor.transpose(aux[0:PST, 1, j * P:(j + 1) * P], z[:, Z_POOL + j, SEQ - PST:SEQ], ident)
                    last = nc.tensor.transpose(aux[:, 2, j * P:j * P + NB * PST], pst[0:NB * PST, j * P:(j + 1) * P],
                                               ident[0:NB * PST, 0:NB * PST])
                last.then_inc(pool_t, 1)
                for g in range(4):
                    last = nc.tensor.transpose(lin[:, 0, g * P:(g + 1) * P], wsr[:, g, :], ident)
                last.then_inc(g_wt, 1)
                for j in range(2):
                    n = 2 * L + j
                    pe.wait_ge(g_sq, n + 1)
                    for a in range(2):
                        last = mm(lin[:, 2 + a, 0:HALF], blk, two(gr[:, j])[:, a])
                    last.then_inc(g_mean, 1)
                    if j == 0:
                        pe.wait_ge(g_r, n + 1)
                pe.wait_ge(pool_v, L + 1)
                pe.wait_ge(pool_e, 2 * L + 2)
                for j in range(2):
                    for a in range(2):
                        last = mm(aux[:, 2 * j + a, 0:HALF], bdw[:, j, :], two(gsq[:, j])[:, a])
                last.then_inc(pool_mm, 1)
                for j in range(2):
                    pe.wait_ge(g_vn, 2 * L + 2)
                    for i in range(TT):
                        last = nc.tensor.transpose(lin[:, 2 + j, i * P:(i + 1) * P], z[:, Z_GV + j, i * P:(i + 1) * P], ident)
                    last.then_inc(g_t, 1)
                pe.wait_ge(g_wm, L + 1)
                for j in range(2):
                    last = nc.tensor.transpose(lin[0:NB, 0, j * P:(j + 1) * P], z[:, Z_GV + j, SEQ:TOK], ident)
                last.then_inc(g_t, 1)
                pe.wait_ge(pool_y, L + 1)
                pe.wait_ge(g_ev, 3 * L + 2)
                for j in range(2):
                    for i in range(TT):
                        for g in range(2):
                            o = aux[64 * g:64 * g + 64, j, i * P:(i + 1) * P]
                            mm(o, vnt[:, j, i, 64 * g:64 * g + 64], wmT[:, 2 * j + g, :], True, False)
                            last = mm(o, pick(4, 2 * j + g, 64), bsr[:, L, :], False, True)
                    last.then_inc(g_mix, 1)
                pe.wait_ge(gate_em, L + 1)
                pe.wait_ge(g_y, L + 1)
                for i in range(TT):
                    last = nc.tensor.transpose(aux[:, 0, i * H:(i + 1) * H], rows[:, R_A, i * P:(i + 1) * P], ident[0:H, 0:H])
                last.then_inc(acol_t, 1)
                for h in range(H):
                    nc.tensor.transpose(aux[0:NB, 1, h * P:(h + 1) * P], z[:, Z_V + h, SEQ:TOK], ident)
                    for n, r in enumerate((R_EM, R_G, R_A)):
                        mm(aux[:, 2, (3 * h + n) * NB:(3 * h + n + 1) * NB], pick(H, h), rows[:, r, SEQ:TOK])
                nc.tensor.transpose(aux[:, 3, 0:NB * H], nst[0:NB * H, :], ident[0:NB * H, 0:NB * H]).then_inc(st_t, 1)
                pe.wait_ge(st_k, L + 1)
                mm(aux[:, 3, 0:H * NB], bcol(C_ONE), qn.rearrange("p h b -> p (h b)"))
                nc.tensor.transpose(aux[0:NB * H, 2, 0:P], nn.rearrange("p b h -> p (b h)"), ident).then_inc(st_den, 1)
                for b in range(NB):
                    n = NB * L + b
                    if b >= 2:
                        pe.wait_ge(ct_ready, n - 1)
                    elif b == 0:
                        pe.wait_ge(g_ev, 3 * L + 3)
                    mm(lin[:, b % 2, :], pick(NB, b), vs[0:NB].rearrange("p h v -> p (h v)")).then_inc(vb_ready, 1)
                    if b >= 1:
                        pe.wait_ge(cn_ready, n)
                        for h in range(H):
                            last = mm(lin[:, 2, h * NB + b - 1:h * NB + b], Cb[:, (b - 1) % 3, h], z[:, Z_Q + h, SEQ + b - 1:SEQ + b])
                        last.then_inc(cq_done, 1)
                pe.wait_ge(cn_ready, NB * (L + 1))
                for h in range(H):
                    last = mm(lin[:, 2, h * NB + NB - 1:h * NB + NB], Cb[:, (NB - 1) % 3, h], z[:, Z_Q + h, TOK - 1:TOK])
                last.then_inc(cq_done, 1)
                pe.wait_ge(st_num, L + 1)
                for h in range(H):
                    hn = H * L + h
                    if h:
                        pe.wait_ge(nd_max, hn)
                        pe.wait_ge(nd_ev, hn)
                        pe.wait_ge(c_ev, hn)
                    else:
                        pe.wait_ge(st_dd, L + 1)
                        pe.wait_ge(acol_ok, L + 1)
                    for i in range(TT):
                        nc.tensor.transpose(aux[:, 0, i * P:(i + 1) * P], z[:, Z_V + h, i * P:(i + 1) * P], ident)
                        last = nc.tensor.transpose(aux[:, 1, i * P:(i + 1) * P], z[:, Z_K + h, i * P:(i + 1) * P], ident)
                    last.then_inc(kv_t, 1)
                    mm(aux[:, 2, :], pick(H, h), rows[:, R_G, 0:SEQ])
                    mm(aux[:, 3, :], pick(H, h), rows[:, R_EM, 0:SEQ]).then_inc(gb_ready, 1)
                    for i in range(TT):
                        mm(lin[:, i, 0:SEQ - i * P], z[:, Z_K + h, i * P:(i + 1) * P], z[:, Z_Q + h, i * P:SEQ]).then_inc(s_ready, 1)
                    pe.wait_ge(kv_ev, hn + 1)
                    for i in range(TT):
                        n = TT * hn + i
                        pe.wait_ge(w_ready, n + 1)
                        w = SEQ - i * P
                        mm(aux[:, 0, i * P:SEQ], vtok[:, i, 0:P], W[:, i % 2, 0:w], i == 0, i == TT - 1)
                        mm(aux[:, 1, i * P:SEQ], bcol(C_ONE), W[:, i % 2, 0:w], i == 0, i == TT - 1).then_inc(w_used, 1)
                    pe.wait_ge(e_ready, TT * (hn + 1))
                    pe.wait_ge(kw_ready, TT * (hn + 1))
                    for i in range(TT):
                        last = mm(aux[:, 2, 0:P + 1], kw[:, i], vtok[:, i, :], i == 0, i == TT - 1)
                    last.then_inc(c_ready, 1)
                for h in range(H):
                    hn = H * L + h
                    pe.wait_ge(hq, hn + 1)
                    if h == 0:
                        pe.wait_ge(nd_max, H * (L + 1))
                    for a in range(2):
                        last = mm(aux[:, a, 0:HALF], bcol(C_MEANH), two(hs1[:, 0:TOK])[:, a])
                    last.then_inc(hm, 1)
                pe.wait_ge(y_ok, L + 1)
                stream(wout_base(L), WOUT_P, kcs("wout"), (yy, yy))
                pe.wait_ge(p_in, 32 * (L + 1))
                for j in range(2):
                    if j == 1:
                        pe.wait_ge(p_ok, 2 * L + 1)
                    for t in range(TT):
                        nc.tensor.transpose(aux[:, 2, t * P:(t + 1) * P], p_tok[:, t, j * P:(j + 1) * P], ident)
                    nc.tensor.transpose(aux[:, 3, 0:NB], p_tok[0:NB, TT, j * P:(j + 1) * P], ident[0:NB, 0:NB]).then_inc(p_t, 1)
                norm(5 * L + 1)
                norm(5 * L + 2)
                if L:
                    for c in range(DC):
                        pe.wait_ge(ht_ready, DC * (3 * L + 1) + c + 1)
                        if c >= 2:
                            pe.wait_ge(hx_ok, c - 1)
                        else:
                            pe.wait_ge(r_ready, 5 * L + 3)
                        for t in range(TT):
                            nc.tensor.transpose(aux[:, 2 + c % 2, t * P:(t + 1) * P], ht[:, c % 2, t * P:(t + 1) * P], ident)
                        nc.tensor.transpose(aux[0:NB, c % 2, 0:P], ht[:, c % 2, SEQ:TOK], ident).then_inc(hx_t, 1)
                pe.wait_ge(h_ready, DC * (3 * L + 2))
                if L:
                    pe.wait_ge(rw_lo, 1)
                    pe.wait_ge(hx_ok, DC)
                    for t in range(TT):
                        at = slice(t * P, (t + 1) * P)
                        for k in range(DC):
                            o = aux[:, 2, t * NE:(t + 1) * NE]
                            mm(o, h_hi[:, k, at], rwh[:, k], k == 0, False)
                            mm(o, h_lo[:, k, at], rwh[:, k], False, False)
                            mm(o, h_hi[:, k, at], rwl[:, k], False, k == DC - 1)
                    for k in range(DC):
                        o = aux[0:NB, 2, TT * NE:(TT + 1) * NE]
                        mm(o, h_hi[:, k, SEQ:TOK].bitcast(f32), rwf[:, k], k == 0, False)
                        last = mm(o, h_lo[:, k, SEQ:TOK].bitcast(f32), rwf[:, k], False, k == DC - 1)
                    last.then_inc(rt_lg, 1)
                    pe.wait_ge(rt_oh, 1)
                    for t in range(6):
                        o = aux[:, 3, t * NE:(t + 1) * NE]
                        for u in range(min(t, 5)):
                            last = mm(o, bcol(C_ONE), msk[:, u], u == 0, t == 5 and u == 4)
                        if t < 5:
                            last = mm(o, tri, msk[:, t], t == 0, True)
                    last.then_inc(rt_cnt, 1)
                    pe.wait_ge(rt_gate, 1)
                    for t in range(TT):
                        nc.tensor.transpose(aux[0:NE, 3, t * P:(t + 1) * P], gatet[:, t], ident)
                    nc.tensor.transpose(aux[0:NE, 2, 0:P], gatet[:, TT], ident).then_inc(rt_t, 1)
                    pe.wait_ge(rt_row, 1)

                    def slots_in(e, k, first=False):
                        if k == 0:
                            pe.wait_ge(xs_in, e * 32 + 32)
                        if k >= 2:
                            pe.wait_ge(xg_ok, e * DC + (k - 1))
                        nc.tensor.transpose(aux[:, k % 2, 0:P], xs[:, 0, k * P:(k + 1) * P], ident)
                        nc.tensor.transpose(aux[:, k % 2, P:CAP], xs[0:CAP2, 1, k * P:(k + 1) * P],
                                            ident[0:CAP2, 0:CAP2]).then_inc(xg_t, 1)

                    def rows_out(e, d):
                        pe.wait_ge(pair_free[d % 2], e * (GU_P + DOWN_P) + (ffn_base(1) + GU_P + d // 2 + 1))
                        if d >= 2:
                            pe.wait_ge(ys_ok, e * DC + (d - 1))
                        nc.tensor.transpose(aux[:, 2 + d % 2, 0:P], ytb[:, d % 2, 0:P], ident)
                        nc.tensor.transpose(aux[0:CAP2, 2 + d % 2, P:2 * P], ytb[:, d % 2, P:CAP], ident).then_inc(yx_t, 1)

                    def slab_slots(q, s, kc, rhs):
                        pe.wait_ge(lo_done, q * 2 + (s + 1))
                        pe.wait_ge(pair_free[s], q)
                        for k in range(kc):
                            whk, wlk = whi[:, s, k * P:(k + 1) * P], wlo[:, s, k * P:(k + 1) * P]
                            hl = rhs[:, k].rearrange("p a t -> p (a t)")
                            mm(lin[:, 2 * s, 0:2 * CAP], whk, hl, k == 0, False)
                            last = mm(lin[:, 2 * s, 0:NMIN], wlk, hl[:, 0:NMIN], False, k == kc - 1)
                        last.then_inc(pe_slab, 1)

                    def expert(e, slots):
                        b = e * (GU_P + DOWN_P) + ffn_base(1)
                        with pe.Fori(0, GU_P) as i:
                            for s in range(2):
                                if slots:
                                    slab_slots(i + b, s, DC, xg)
                                else:
                                    slab(i + b, s, DC, h_hi, h_lo)
                        pe.wait_ge(gu_ok, e * GU_P + GU_P * (SLICES[0] + 1))
                        for d in range(DC):
                            q = b + (GU_P + d // 2)
                            if slots:
                                slab_slots(q, d % 2, FCH, gs)
                            else:
                                slab(q, d % 2, FCH, gu_hi, gu_lo)
                            if d == 0:
                                pe.wait_ge(gb_ok, e + 1)
                            slots_in(e + 1, d)
                            if d:
                                rows_out(e, d - 1)
                        rows_out(e, DC - 1)

                    for k in range(DC):
                        slots_in(0, k)
                    with pe.Fori(0, NE) as e:
                        fit = pe.value_load(fitu[0:1, bass.ds(e, 1)], min_val=0, max_val=1)
                        pe.wait_ge(xg_ok, e * DC + DC)
                        pe.wait_ge(pk, e + 1)
                        for a in range(2):
                            last = mm(aux[:, a, 0:HALF], pick_e[:, :], two(grow[:, :])[:, a])
                        last.then_inc(gb_mm, 1)
                        with pe.If(fit == 1):
                            expert(e, True)
                        with pe.Else():
                            expert(e, False)
                    pe.wait_ge(pair_free[0], ple_base(1))
                    pe.wait_ge(pair_free[1], ple_base(1))
                    for t in range(5):
                        n = P if t < TT else NB
                        pe.wait_ge(cb_b, t + 1)
                        if t >= 2:
                            pe.wait_ge(cb_acc, t - 1)
                        for c in range(DC):
                            last = nc.tensor.transpose(lin[:, 2 * (t % 2) + c // 4, (c % 4) * P:(c % 4) * P + n],
                                                       ctok[0:n, t % 2, c * P:(c + 1) * P], ident[0:n, 0:n])
                        last.then_inc(cb_t, 1)
                    pe.wait_ge(cb_acc, 5)
                else:
                    for e in range(SLICES[0]):
                        b = ffn_base(0) + e * (GU_P + DOWN_P)
                        stream(b, GU_P, kcs("gu"), (hh, hh))
                        pe.wait_ge(gu_ok, GU_P * (e + 1))
                        stream(b + GU_P, DOWN_P, kcs("down"), (gg, gg))
                norm(5 * L + 3)
                norm(5 * L + 4)
                pe.wait_ge(h_ready, DC * (3 * L + 3))
                stream(ple_base(L), PLE_P, kcs("ple"), (hh, pp))
            pe.wait_ge(pair_free[1], LAST_PAIR + 1)
            pe.wait_ge(ple_x, DC * DEPTH)
            for t in range(TT + 1):
                n = P if t < TT else NB
                if t:
                    pe.wait_ge(yt_ev, t)
                for c in range(DC):
                    last = nc.tensor.transpose(lin[0:n, c // 4, (c % 4) * P:(c % 4 + 1) * P], x[:, c, t * P:t * P + n], ident)
                last.then_inc(yt_t, 1)

        @block.scalar
        def _(act):
            def cp(out, in_, **k):
                return nc.scalar.activation(out, in_, ACT.Copy, **k)

            def split(q, s, kc):
                act.wait_ge(staged[s], q * 16 + 16)
                if not (isinstance(q, int) and q == 0):
                    act.wait_ge(pe_slab, q * 2 + (s - 1))
                cp(whi[:, s, 0:kc * P], wst[:, s, 0:kc * P]).then_inc(hi_done, 1)

            def stream(base, pairs, kc, after, take, table=None):
                if table is not None:
                    nc.scalar.activation(spare[:, :], epsc[:, :], table)
                def pair(q, i, nxt):
                    split(q, 1, kc[1])
                    take(0, q, i)
                    if nxt:
                        split(q + 1, 0, nxt)
                    take(1, q, i)
                first = 1 if isinstance(base, int) and base == 0 else 0
                if first:
                    pair(0, 0, kc[0])
                with act.Fori(first, pairs - 1) as i:
                    pair(i + base, i, kc[0])
                pair(base + pairs - 1, pairs - 1, after)

            act.wait_ge(setup_pool, 1)
            act.wait_ge(cols_t, 1)
            cp(cols[:, :], aux[:, 3, 0:96]).then_inc(cols_ok, 1)
            split(0, 0, DC)
            for c in range(DC):
                act.wait_ge(x_t, c + 1)
                cp(x[:, c, 0:SEQ], aux[:, c % 3, :]).then_inc(x_ok, 1)
            act.wait_ge(xs_t, 1)
            cp(x[:, :, SEQ:TOK], lin[:, 0, 0:DC * NB].rearrange("p (c b) -> p c b", b=NB)).then_inc(x_ok, 1)
            act.wait_ge(x_ok, DC + 1)

            def norm(N, src, ready):
                for c in range(DC):
                    if ready is not None:
                        act.wait_ge(ready[0], ready[1] + c + 1)
                    if N or c >= 4:
                        act.wait_ge(sq_used, N * DC + max(c - 3, 0))
                    nc.scalar.activation(sq[:, c % 4], src[:, c], ACT.Square).then_inc(sq_ready, 1)
                act.wait_ge(sq_used, (N + 1) * DC)
                nc.scalar.activation(two(rn), aux[:, 0:2, 0:HALF], ACT.Ln, bias=epsc[:, :])
                act.drain()
                nc.scalar.activation(rn, rn, ACT.Exp, scale=-0.5).then_inc(r_ready, 1)

            def round_h(N, rows_too=False):
                for c in range(DC):
                    act.wait_ge(ht_ready, N * DC + c + 1)
                    cp(h_hi[:, c], ht[:, c % 2]).then_inc(h_hi_ok, 1)
                    if rows_too:
                        act.wait_ge(hx_t, c + 1)
                        cp(htok[:, 0:TT, c * P:(c + 1) * P], aux[:, 2 + c % 2, :].rearrange("p (t d) -> p t d", d=P))
                        cp(htok[0:NB, TT, c * P:(c + 1) * P], aux[0:NB, c % 2, 0:P]).then_inc(hx_ok, 1)

            def rsqrt(out, in_, eps=True):
                if eps:
                    nc.scalar.activation(out, in_, ACT.Ln, bias=epsc[:, :])
                else:
                    nc.scalar.activation(out, in_, ACT.Ln)
                act.drain()
                return nc.scalar.activation(out, out, ACT.Exp, scale=-0.5)

            for L in range(DEPTH):
                act.wait_ge(gw_in, 32 * (L + 1))
                cp(gwh[:, :], gwf[:, :]).then_inc(gw_ok, 1)
                norm(5 * L, x, (ple_x, DC * (L - 1)) if L else None)
                round_h(3 * L)
                act.wait_ge(gates, L + 1)
                if L == 0:
                    act.wait_ge(w_small, 16 * 23)
                nc.scalar.activation(two(rows[:, R_IG]), aux[0:H, 2:4, 0:HALF], ACT.Identity, bias=gate_b[:, 0, L:L + 1])
                cp(two(rows[:, R_F]), aux[32:32 + H, 2:4, 0:HALF])
                act.drain()
                nc.scalar.activation(rows[:, R_F], rows[:, R_F], ACT.Identity, bias=gate_b[:, 1, L:L + 1])
                act.drain()
                nc.scalar.activation(rows[:, R_EM], rows[:, R_F], ACT.Abs)
                act.drain()
                nc.scalar.activation(rows[:, R_EM], rows[:, R_EM], ACT.Exp, scale=-1.0)
                act.drain()
                nc.scalar.activation(rows[:, R_EM], rows[:, R_EM], ACT.Ln, bias=one[0:H]).then_inc(gate_l1, 1)

                def take_z(s, q, i):
                    act.wait_ge(pe_slab, q * 2 + (s + 1))
                    cp(z[:, bass.ds(i * 2 + s, 1)].rearrange("p a (b c) -> p (a b) c", c=HALF),
                       lin[:, 2 * s:2 * s + 2, 0:HALF]).then_inc(pair_free[s], 1)
                stream(win_base(L), WIN_P, kcs("win"), kcs("wout")[0], take_z)
                act.wait_ge(pair_free[0], wout_base(L))
                act.wait_ge(pair_free[1], wout_base(L))
                nc.scalar.activation(z[:, Z_O:Z_O + H], z[:, Z_O:Z_O + H], ACT.Sigmoid).then_inc(sig_o, 1)
                act.wait_ge(pool_t, L + 1)
                if L:
                    act.wait_ge(out_st, 16 * 5 * L)
                cp(us[0:NB], aux[0:NB, 0, 0:2 * P].rearrange("p (a b) -> p a b", b=P)).then_inc(pool_e, 1)
                cp(us[32:32 + PST], aux[0:PST, 1, 0:2 * P].rearrange("p (a b) -> p a b", b=P)).then_inc(pool_e, 1)
                for j in range(2):
                    nc.scalar.activation(gr[:, j], z[:, Z_GV + j], ACT.Square).then_inc(g_sq, 1)
                for j in range(2):
                    act.wait_ge(g_mean, 2 * L + j + 1)
                    rsqrt(two(gr[:, j]), lin[:, 2:4, 0:HALF]).then_inc(g_r, 1)
                act.wait_ge(pool_mm, L + 1)
                for j in range(2):
                    ins = cp(two(z[:, Z_POOL + j]), aux[:, 2 * j:2 * j + 2, 0:HALF], scale=cols[:, 80 + 2 * L + j:81 + 2 * L + j])
                ins.then_inc(pool_y, 1)
                for j in range(2):
                    act.wait_ge(g_t, 3 * L + j + 1)
                    cp(vnt[:, j], lin[:, 2 + j, :].rearrange("p (i d) -> p i d", d=P)).then_inc(g_ev, 1)
                act.wait_ge(g_t, 3 * L + 3)
                cp(gvo[0:NB, :], lin[0:NB, 0, 0:2 * P]).then_inc(g_ev, 1)
                act.wait_ge(gate_g, L + 1)
                nc.scalar.activation(rows[:, R_EM], rows[:, R_M], ACT.Exp, scale=-1.0)
                nc.scalar.activation(rows[:, R_G, SEQ:TOK], rows[:, R_G, SEQ:TOK], ACT.Exp)
                nc.scalar.activation(rows[:, R_A, SEQ:TOK], rows[:, R_A, SEQ:TOK], ACT.Exp).then_inc(gate_em, 1)
                act.wait_ge(acol_t, L + 1)
                cp(acol[:, :, :], aux[:, 0, 0:TT * H].rearrange("p (i h) -> p i h", h=H)).then_inc(acol_ok, 1)
                act.wait_ge(st_t, L + 1)
                cp(vs[0:NB], aux[0:NB, 1, :].rearrange("p (h v) -> p h v", v=P))
                cp(dcs[:, :, :, :], aux[:, 2, 0:H * 3 * NB].rearrange("p (h n b) -> p h n b", n=3, b=NB))
                cp(nT[:, :, :], aux[:, 3, 0:NB * H].rearrange("p (b h) -> p b h", h=H)).then_inc(st_ev, 1)
                act.wait_ge(st_den, L + 1)
                nc.scalar.activation(D[:, :, SEQ:TOK], aux[:, 3, 0:H * NB].rearrange("p (h b) -> p h b", b=NB), ACT.Abs).then_inc(st_de, 1)
                cp(nout[0:NB * H, :], aux[0:NB * H, 2, 0:P]).then_inc(st_de, 1)
                act.wait_ge(out_st, 16 * (5 * L + 4))
                for b in range(NB):
                    n = NB * L + b
                    act.wait_ge(vb_ready, n + 1)
                    if b:
                        act.wait_ge(cn_ready, n)
                    for h in range(H):
                        ins = cp(Ct[:, h], lin[:, b % 2, h * P:(h + 1) * P], scale=kws[:, h, b:b + 1])
                    ins.then_inc(ct_ready, 1)
                act.wait_ge(cq_done, NB * (L + 1))
                cp(num[:, :, SEQ:TOK], lin[:, 2, 0:H * NB].rearrange("p (h b) -> p h b", b=NB)).then_inc(st_num, 1)
                for h in range(H):
                    hn = H * L + h
                    act.wait_ge(kv_t, hn + 1)
                    if h:
                        act.wait_ge(c_ready, hn)
                        act.wait_ge(kw_ready, TT * hn)
                    cp(vtok[:, :, 0:P], aux[:, 0, :].rearrange("p (i d) -> p i d", d=P))
                    if h == 0:
                        cp(vtok[:, :, P:P + 1], one.to_broadcast([P, TT]).rearrange("p (i a) -> p i a", a=1))
                    cp(ktok[:, :, :], aux[:, 1, :].rearrange("p (i d) -> p i d", d=P), scale=QS).then_inc(kv_ev, 1)
                    act.wait_ge(gb_ready, hn + 1)
                    for i in range(TT):
                        n = TT * hn + i
                        if n >= 2:
                            act.wait_ge(w_ready, n - 1)
                            act.wait_ge(kw_ready, n - 1)
                        nc.scalar.activation(E[:, i % 2, 0:SEQ - i * P], aux[:, 2, i * P:SEQ], ACT.Exp,
                                             bias=acol[:, i, h:h + 1]).then_inc(e_ready, 1)
                    act.wait_ge(w_used, TT * (hn + 1))
                    cp(num[:, h, 0:SEQ], aux[:, 0, :])
                    nc.scalar.activation(D[:, h, 0:SEQ], aux[:, 1, :], ACT.Abs).then_inc(nd_ev, 1)
                    act.wait_ge(c_ready, hn + 1)
                    if h:
                        act.wait_ge(c_out, 32 * hn)
                    elif L:
                        act.wait_ge(c_out, 32 * H * L)
                    cp(Cout[:, :], aux[:, 2, 0:P + 1]).then_inc(c_ev, 1)
                act.wait_ge(st_num, L + 1)
                act.wait_ge(nd_ev, H * (L + 1))
                for h in range(H):
                    hn = H * L + h
                    nc.scalar.activation(hs1[:, 0:TOK], num[:, h], ACT.Square).then_inc(hq, 1)
                    act.wait_ge(ha, hn + 1)
                    if h:
                        act.wait_ge(hy, hn)
                    rsqrt(hs2[:, 0:TOK], hs1[:, 0:TOK], False).then_inc(hr, 1)
                act.wait_ge(hy2, H * (L + 1))
                act.wait_ge(g_y, L + 1)
                cp(y_hi[:, 0:2], z[:, Z_POOL:Z_POOL + 2])
                cp(y_hi[:, 2:6], z[:, Z_O:Z_O + H])
                cp(y_hi[:, 6:8], z[:, Z_GU:Z_GU + 2]).then_inc(y_hi_ok, 1)

                act.wait_ge(y_ok, L + 1)
                stream(wout_base(L), WOUT_P, kcs("wout"), kcs("gu")[0], take_z)
                for j in range(2):
                    act.wait_ge(p_t, 2 * L + j + 1)
                    cp(p_hi[:, j, 0:SEQ], aux[:, 2, :])
                    cp(p_hi[:, j, SEQ:TOK], aux[:, 3, 0:NB]).then_inc(p_hi_ok, 1)
                act.wait_ge(pair_free[0], ffn_base(L))
                act.wait_ge(pair_free[1], ffn_base(L))
                norm(5 * L + 1, acc, None)
                norm(5 * L + 2, x, (x_upd, DC * 2 * L))
                round_h(3 * L + 1, L == 1)
                if L:
                    act.wait_ge(rt_max, 1)
                    nc.scalar.activation(gwt[:, :, 1], gwt[:, :, 1], ACT.Sigmoid).then_inc(rt_e, 1)
                    act.wait_ge(rt_t, 1)
                    cp(grow[:, 0:SEQ], aux[0:NE, 3, :])
                    act.drain()
                    cp(grow[:, SEQ:TOK], aux[0:NE, 2, 0:NB]).then_inc(rt_row, 1)

                    def slots_hi(e, k):
                        act.wait_ge(xg_t, e * DC + (k + 1))
                        cp(xg[:, k, 0], aux[:, k % 2, 0:CAP]).then_inc(xg_hi, 1)

                    def expert(e, slots):
                        b = e * (GU_P + DOWN_P) + ffn_base(1)

                        def take_gu(s, q, i):
                            if s == 0:
                                act.wait_ge(pe_slab, q * 2 + 1)
                                if slots:
                                    act.wait_ge(pair_free[0], q + 1)
                                    ins = nc.scalar.activation(sg[:, 0:CAP], sg[:, 0:CAP], ACT.Silu)
                                else:
                                    ins = nc.scalar.activation(two(sg), lin[:, 0:2, 0:HALF], ACT.Silu)
                                ins.then_inc(silu_ok, 1)
                            else:
                                act.wait_ge(pair_free[1], q + 1)
                                if slots:
                                    ins = cp(gs[:, bass.ds(i, 1), 0].rearrange("p a t -> p (a t)"), gt[:, 0:CAP])
                                else:
                                    ins = cp(gu_hi[:, bass.ds(i, 1)].rearrange("p a t -> p (a t)"), gt)
                                ins.then_inc(gu_hi_ok, 1)
                        stream(b, GU_P, kcs("gu"), FCH, take_gu, ACT.Silu)
                        for d in range(DC):
                            q, s = b + (GU_P + d // 2), d % 2
                            split(q + s, 1 - s, FCH if d < DC - 1 else DC)
                            slots_hi(e + 1, d)
                            if d:
                                rows_b(e, d - 1)
                        rows_b(e, DC - 1)

                    def rows_b(e, d):
                        if d == 0:
                            act.wait_ge(y_stored, e * 32 + 32)
                        act.wait_ge(yx_t, e * DC + (d + 1))
                        cp(ys[:, :, d * P:(d + 1) * P],
                           aux[:, 2 + d % 2, 0:2 * P].rearrange("p (a c) -> p a c", c=P)).then_inc(ys_ok, 1)

                    for k in range(DC):
                        slots_hi(0, k)
                    with act.Fori(0, NE) as e:
                        fit = act.value_load(fitu[0:1, bass.ds(e, 1)], min_val=0, max_val=1)
                        act.wait_ge(gb_mm, e + 1)
                        cp(two(gb), aux[:, 0:2, 0:HALF]).then_inc(gb_ok, 1)
                        with act.If(fit == 1):
                            expert(e, True)
                        with act.Else():
                            expert(e, False)
                    for t in range(5):
                        n = P if t < TT else NB
                        act.wait_ge(y_back[t % 2], 32 * (t // 2 + 1))
                        if t >= 2:
                            act.wait_ge(cb_t, t - 1)
                        cp(ctok[0:n, t % 2, :], yrow[0:n, t % 2, 0, :], scale=gwt[0:n, t, 0:1]).then_inc(cb_a, 1)
                    act.wait_ge(cb_acc, 5)
                else:
                    for e in range(SLICES[0]):
                        b = ffn_base(0) + e * (GU_P + DOWN_P)

                        def take_gu0(s, q, i):
                            if s == 0:
                                act.wait_ge(pe_slab, q * 2 + 1)
                                nc.scalar.activation(two(sg), lin[:, 0:2, 0:HALF], ACT.Silu).then_inc(pair_free[0], 1)
                            else:
                                act.wait_ge(pair_free[1], q + 1)
                                cp(gu_hi[:, bass.ds(i, 1)].rearrange("p a t -> p (a t)"), gt).then_inc(gu_hi_ok, 1)
                        stream(b, GU_P, kcs("gu"), kcs("down")[0], take_gu0, ACT.Silu)
                        stream(b + GU_P, DOWN_P, kcs("down"), DC, lambda s, q, i: None)
                act.wait_ge(pair_free[0], ple_base(L))
                act.wait_ge(pair_free[1], ple_base(L))
                norm(5 * L + 3, acc, None)
                norm(5 * L + 4, x, (x_upd, DC * (2 * L + 1)))
                round_h(3 * L + 2)

                def take_ple(s, q, i):
                    if s == 0:
                        act.wait_ge(pe_slab, q * 2 + 1)
                        if not (isinstance(i, int) and i == 0):
                            act.wait_ge(pair_free[1], q)
                        nc.scalar.activation(two(sg), lin[:, 0:2, 0:HALF], ACT.Sigmoid).then_inc(pair_free[0], 1)
                stream(ple_base(L), PLE_P, kcs("ple"), kcs("win")[0] if L < DEPTH - 1 else 0, take_ple, ACT.Sigmoid)
            for t in range(TT + 1):
                n = P if t < TT else NB
                act.wait_ge(yt_t, t + 1)
                if t >= 2:
                    act.wait_ge(y_st[t % 2], 16 * (t // 2))
                cp(y_tok[0:n, t % 2, :], lin[0:n, 0:2, :].rearrange("p a b -> p (a b)")).then_inc(yt_ev, 1)

        @block.vector
        def _(dve):
            def tt(out, a, b, op):
                return nc.vector.tensor_tensor(out, a, b, op)

            def stt(out, a, s, b, op0, op1):
                return nc.vector.scalar_tensor_tensor(out=out, in0=a, scalar=s, in1=b, op0=op0, op1=op1)

            def split(q, s, kc):
                dve.wait_ge(hi_done, q * 2 + (s + 1))
                tt(wlo[:, s, 0:kc * P], wst[:, s, 0:kc * P], whi[:, s, 0:kc * P].bitcast(f32), ALU.subtract).then_inc(lo_done, 1)

            def stream(base, pairs, kc, after, take):
                def pair(q, i, nxt):
                    split(q, 1, kc[1])
                    take(0, q, i)
                    if nxt:
                        split(q + 1, 0, nxt)
                    take(1, q, i)
                with dve.Fori(0, pairs - 1) as i:
                    pair(i + base, i, kc[0])
                pair(base + pairs - 1, pairs - 1, after)

            def nothing(s, q, i):
                pass

            def make_h(N, w, rows_too=False):
                def scaled(c):
                    stt(ht[:, c % 2], x[:, c], cols[:, w + c:w + c + 1], rn, ALU.mult, ALU.mult).then_inc(ht_ready, 1)
                scaled(0)
                for c in range(DC):
                    if c + 1 < DC:
                        if c:
                            dve.wait_ge(h_ready, N * DC + c)
                            if rows_too:
                                dve.wait_ge(hx_t, c)
                        scaled(c + 1)
                    dve.wait_ge(h_hi_ok, N * DC + c + 1)
                    dve.wait_ge(ht_ready, N * DC + c + 1)
                    tt(h_lo[:, c], ht[:, c % 2], h_hi[:, c].bitcast(f32), ALU.subtract).then_inc(h_ready, 1)

            def normed(N, w):
                for c in range(DC):
                    if N or c >= 2:
                        dve.wait_ge(x_upd, N * DC + max(c - 1, 0))
                    stt(ut[:, c % 2], acc[:, c], cols[:, w + c:w + c + 1], rn, ALU.mult, ALU.mult).then_inc(ut_ready, 1)

            def add_rows(t):
                n = P if t < TT else NB
                dve.wait_ge(cb_t, t + 1)
                o = acc[:, :, t * P:t * P + n].rearrange("p (a c) t -> p a c t", a=2)
                i = lin[:, 2 * (t % 2):2 * (t % 2) + 2, :].rearrange("p a (c t) -> p a c t", t=P)[:, :, :, 0:n]
                tt(o, o, i, ALU.add).then_inc(cb_acc, 1)

            split(0, 0, DC)
            dve.wait_ge(cols_ok, 1)
            dve.wait_ge(x_ok, DC + 1)
            for L in range(DEPTH):
                dve.wait_ge(gw_ok, L + 1)
                tt(gwl[:, :], gwf[:, :], gwh[:, :].bitcast(f32), ALU.subtract).then_inc(gw_lo, 1)
                dve.wait_ge(r_ready, 5 * L + 1)
                make_h(3 * L, 8 * L)
                stream(win_base(L), WIN_P, kcs("win"), kcs("wout")[0], nothing)
                dve.wait_ge(gate_lf, L + 1)
                nc.vector.tensor_tensor_scan(rows[:, R_G, 0:SEQ], rows[:, R_F, 0:SEQ], rows[:, R_A, 0:SEQ], 0.0, ALU.add, ALU.add)
                nc.vector.tensor_tensor_scan(rows[:, R_M, 0:SEQ], rows[:, R_F, 0:SEQ], rows[:, R_IG, 0:SEQ], 0.0, ALU.add, ALU.max)
                tt(rows[:, R_M, SEQ:TOK], tsm[:, :], rows[:, R_IG, SEQ:TOK], ALU.max).then_inc(gate_scan, 1)
                dve.wait_ge(pool_win, L + 1)
                dve.wait_ge(pool_t, L + 1)
                for g, w in enumerate(WINDOWS):
                    lo, j = 64 * (g % 2), g // 2
                    old = aux[lo:lo + 64, 2, j * P:j * P + NB * PST].rearrange("p (b r) -> p b r", r=PST)[:, :, PST - w + 1:PST]
                    nc.vector.tensor_reduce(gsq[lo:lo + 64, j, SEQ:TOK], old, AXX, ALU.add)
                dve.drain()
                tt(gsq[:, :, SEQ:TOK], gsq[:, :, SEQ:TOK], z[:, Z_POOL:Z_POOL + 2, SEQ:TOK], ALU.add)
                dve.drain()
                for j in range(2):
                    last = stt(gsq[:, j, SEQ:TOK], gsq[:, j, SEQ:TOK], const[:, C_INVW + j:C_INVW + j + 1],
                               z[:, Z_POOL + j, SEQ:TOK], ALU.mult, ALU.subtract)
                last.then_inc(pool_v, 1)
                dve.wait_ge(g_wt, L + 1)
                tt(wmT[:, :, :], lin[:, 0, :].rearrange("p (g t) -> p g t", t=P),
                   tri.rearrange("p (a t) -> p a t", a=1).to_broadcast([P, 4, P]), ALU.mult).then_inc(g_wm, 1)
                for j in range(2):
                    dve.wait_ge(g_r, 2 * L + j + 1)
                    stt(z[:, Z_GV + j], z[:, Z_GV + j], cols[:, 92 + 2 * L + j:93 + 2 * L + j], gr[:, j], ALU.mult, ALU.mult).then_inc(g_vn, 1)
                dve.wait_ge(g_vn, 2 * L + 2)
                dve.wait_ge(pool_mm, L + 1)
                for j in range(2):
                    nc.vector.tensor_scalar(gsq[:, j, SEQ:TOK], z[:, Z_GV + j, SEQ:TOK], sg_b[:, 0, L, j:j + 1],
                                            sg_b[:, 1, L, j:j + 1], ALU.mult, ALU.add)
                dve.drain()
                for j in range(2):
                    dve.wait_ge(g_mix, 2 * L + j + 1)
                    tt(z[:, Z_GU + j, 0:SEQ], z[:, Z_GU + j, 0:SEQ], aux[:, j, :], ALU.mult)
                    last = tt(z[:, Z_GU + j, SEQ:TOK], z[:, Z_GU + j, SEQ:TOK], gsq[:, j, SEQ:TOK], ALU.mult)
                last.then_inc(g_y, 1)
                dve.wait_ge(st_ev, L + 1)
                nv = nn.rearrange("p b h -> p h b")
                stt(kws[:, :, :], z[:, Z_K:Z_K + H, SEQ:TOK], QS, dcs[:, :, 2, :], ALU.mult, ALU.mult)
                tt(nv, nT.rearrange("p b h -> p h b"), dcs[:, :, 1, :], ALU.mult)
                dve.drain()
                tt(nv, nv, kws[:, :, :], ALU.add)
                dve.drain()
                tt(qn[:, :, :], z[:, Z_Q:Z_Q + H, SEQ:TOK], nv, ALU.mult).then_inc(st_k, 1)
                dve.wait_ge(st_de, 2 * L + 1)
                tt(D[:, :, SEQ:TOK], D[:, :, SEQ:TOK], dcs[:, :, 0, :], ALU.max).then_inc(st_dd, 1)
                for b in range(NB):
                    dve.wait_ge(C_in[b % 3], 16 * ((3, 3, 2)[b % 3] * L + b // 3 + 1))
                    dve.wait_ge(ct_ready, NB * L + b + 1)
                    for h in range(H):
                        last = stt(Cb[:, b % 3, h], Cb[:, b % 3, h], dcs[:, h, 1, b:b + 1], Ct[:, h], ALU.mult, ALU.add)
                    last.then_inc(cn_ready, 1)
                for h in range(H):
                    hn = H * L + h
                    for i in range(TT):
                        n = TT * hn + i
                        dve.wait_ge(e_mask, n + 1)
                        dve.wait_ge(s_ready, n + 1)
                        if n >= 2:
                            dve.wait_ge(w_used, n - 1)
                        w = SEQ - i * P
                        stt(W[:, i % 2, 0:w], lin[:, i, 0:w], QS, E[:, i % 2, 0:w], ALU.mult, ALU.mult).then_inc(w_ready, 1)
                    dve.wait_ge(nd_ev, hn + 1)
                    tt(D[:, h, 0:SEQ], D[:, h, 0:SEQ], aux[:, 3, :], ALU.max).then_inc(nd_max, 1)
                for h in range(H):
                    hn = H * L + h
                    dve.wait_ge(hm, hn + 1)
                    dve.wait_ge(hd2, hn + 1)
                    stt(two(hs1[:, 0:TOK]), two(D[:, h]), EPS, aux[:, 0:2, 0:HALF], ALU.mult, ALU.add).then_inc(ha, 1)
                    dve.wait_ge(hr, hn + 1)
                    stt(num[:, h], num[:, h], cols[:, 84 + 4 * L + h:85 + 4 * L + h], hs2[:, 0:TOK], ALU.mult, ALU.mult).then_inc(hy, 1)
                dve.wait_ge(y_hi_ok, L + 1)
                tt(y_lo[:, 0:2], z[:, Z_POOL:Z_POOL + 2], y_hi[:, 0:2].bitcast(f32), ALU.subtract)
                tt(y_lo[:, 2:6], z[:, Z_O:Z_O + H], y_hi[:, 2:6].bitcast(f32), ALU.subtract)
                tt(y_lo[:, 6:8], z[:, Z_GU:Z_GU + 2], y_hi[:, 6:8].bitcast(f32), ALU.subtract).then_inc(y_ok, 1)
                stream(wout_base(L), WOUT_P, kcs("wout"), kcs("gu")[0], nothing)
                for j in range(2):
                    dve.wait_ge(p_hi_ok, 2 * L + j + 1)
                    tt(p_lo[:, j, 0:SEQ], aux[:, 2, :], p_hi[:, j, 0:SEQ].bitcast(f32), ALU.subtract)
                    tt(p_lo[:, j, SEQ:TOK], aux[:, 3, 0:NB], p_hi[:, j, SEQ:TOK].bitcast(f32), ALU.subtract).then_inc(p_ok, 1)
                dve.wait_ge(r_ready, 5 * L + 2)
                normed(2 * L, 16 + 8 * L)
                dve.wait_ge(r_ready, 5 * L + 3)
                make_h(3 * L + 1, 32 + 8 * L, L == 1)
                if L == 0:
                    nc.vector.tensor_copy(rwh[:, :, :], rwf[:, :, :])
                    dve.drain()
                    tt(rwl[:, :, :], rwf[:, :, :], rwh[:, :, :].bitcast(f32), ALU.subtract).then_inc(rw_lo, 1)
                else:
                    dve.wait_ge(rt_lg, 1)
                    rb8 = rbias[:, :].rearrange("p (a e) -> p a e", a=1)
                    tt(lg[:, 0:TT, :], aux[:, 2, 0:TT * NE].rearrange("p (t e) -> p t e", e=NE),
                       rb8.to_broadcast([P, TT, NE]), ALU.add)
                    tt(lg[0:NB, TT, :], aux[0:NB, 2, TT * NE:(TT + 1) * NE], rbias[0:NB, :], ALU.add)
                    dve.drain()
                    for t in range(5):
                        nc.vector.max(top[:, t], lg[:, t])
                    dve.drain()
                    for t in range(5):
                        nc.vector.max_index(topi[:, t], top[:, t], lg[:, t])
                    tt(gwt[:, :, 1], top[:, :, 1], top[:, :, 0], ALU.subtract).then_inc(rt_max, 1)
                    dve.drain()
                    nc.vector.tensor_copy(topf[:, :, :], topi[:, :, :])
                    dve.drain()
                    for t in range(5):
                        for k in range(2):
                            nc.vector.tensor_scalar(oh[:, k, t], iota8[:, :], topf[:, t, k:k + 1],
                                                    const[:, C_VAL + t:C_VAL + t + 1], ALU.is_equal, ALU.mult)
                    dve.drain()
                    tt(msk[:, :, :], oh[:, 0], oh[:, 1], ALU.add).then_inc(rt_oh, 1)
                    dve.wait_ge(rt_e, 1)
                    nc.vector.tensor_scalar(gwt[:, :, 0], gwt[:, :, 1], -1.0, 1.0, ALU.mult, ALU.add)
                    dve.drain()
                    for t in range(5):
                        nc.vector.tensor_scalar(gtmp[:, t], oh[:, 0, t], gwt[:, t, 0:1], None, ALU.mult)
                        nc.vector.tensor_scalar(gatet[:, t], oh[:, 1, t], gwt[:, t, 1:2], None, ALU.mult)
                    dve.drain()
                    tt(gatet[:, :, :], gatet[:, :, :], gtmp[:, :, :], ALU.add)
                    dve.wait_ge(rt_cnt, 1)
                    nc.vector.tensor_scalar(fits[:, :], aux[:, 3, 5 * NE:6 * NE], float(CAP), None, ALU.is_le)
                    nc.vector.tensor_scalar(rbias[:, :], iota8[:, :], float(CAP), float(-1 - NSLOT), ALU.mult, ALU.add)
                    dve.drain()
                    nc.vector.tensor_copy(fitu[:, :], fits[:, :])
                    tt(rel[:, :, :], aux[:, 3, 0:5 * NE].rearrange("p (t e) -> p t e", e=NE),
                       rb8.to_broadcast([P, 5, NE]), ALU.add)
                    dve.drain()
                    tt(rel[:, :, :], rel[:, :, :], fits[:, :].rearrange("p (a e) -> p a e", a=1).to_broadcast([P, 5, NE]), ALU.mult)
                    dve.drain()
                    for k in range(2):
                        tt(oh[:, k], oh[:, k], rel[:, :, :], ALU.mult)
                    dve.drain()
                    for k in range(2):
                        nc.vector.tensor_reduce(idxf[:, :, k], oh[:, k], AXX, ALU.add)
                    dve.drain()
                    nc.vector.tensor_scalar(idxf[:, :, :], idxf[:, :, :], float(NSLOT), None, ALU.add)
                    dve.drain()
                    nc.vector.tensor_copy(idxu[:, :, :], idxf[:, :, :]).then_inc(rt_idx, 1)
                    dve.wait_ge(rt_idx, 1)
                    nc.vector.tensor_copy(gtmp[:, :, :], gatet[:, :, :]).then_inc(rt_gate, 1)
                dve.wait_ge(acc0, L + 1)
                if L:
                    def both(out, s):
                        return nc.vector.tensor_reduce(out, lin[:, 2 * s, 0:2 * CAP].rearrange("p (a t) -> p t a", a=2),
                                                       AXX, ALU.add)

                    def slots_lo(e, k):
                        dve.wait_ge(xg_hi, e * DC + (k + 1))
                        tt(xg[:, k, 1], aux[:, k % 2, 0:CAP], xg[:, k, 0].bitcast(f32), ALU.subtract).then_inc(xg_ok, 1)

                    def expert(e, slots):
                        b = e * (GU_P + DOWN_P) + ffn_base(1)

                        def take_gu(s, q, i):
                            if s == 0:
                                if slots:
                                    dve.wait_ge(pe_slab, q * 2 + 1)
                                    both(sg[:, 0:CAP], 0).then_inc(pair_free[0], 1)
                                return
                            dve.wait_ge(pe_slab, q * 2 + 2)
                            if slots:
                                both(gt[:, CAP:2 * CAP], 1)
                                dve.drain()
                            dve.wait_ge(silu_ok, e * GU_P + (i + 1))
                            if slots:
                                tt(gt[:, 0:CAP], sg[:, 0:CAP], gt[:, CAP:2 * CAP], ALU.mult).then_inc(pair_free[1], 1)
                                src, hi, lo = gt[:, 0:CAP], gs[:, bass.ds(i, 1), 0], gs[:, bass.ds(i, 1), 1]
                            else:
                                dve.wait_ge(gb_ok, e + 1)
                                tt(two(gt), two(sg), lin[:, 2:4, 0:HALF], ALU.mult).then_inc(pair_free[0], 1)
                                dve.drain()
                                tt(gt, gt, gb, ALU.mult).then_inc(pair_free[1], 1)
                                src, hi, lo = gt, gu_hi[:, bass.ds(i, 1)], gu_lo[:, bass.ds(i, 1)]
                            dve.wait_ge(gu_hi_ok, e * GU_P + (i + (GU_P * SLICES[0] + 1)))
                            tt(lo.rearrange("p a t -> p (a t)"), src, hi.rearrange("p a t -> p (a t)").bitcast(f32),
                               ALU.subtract).then_inc(gu_ok, 1)
                        stream(b, GU_P, kcs("gu"), FCH, take_gu)
                        for d in range(DC):
                            q, s = b + (GU_P + d // 2), d % 2
                            split(q + s, 1 - s, FCH if d < DC - 1 else DC)
                            slots_lo(e + 1, d)
                            dve.wait_ge(pe_slab, q * 2 + (s + 1))
                            if slots:
                                if d >= 2:
                                    dve.wait_ge(yx_t, e * DC + (d - 1))
                                both(ytb[:, s], s).then_inc(pair_free[s], 1)
                            else:
                                tt(two(acc[:, d]), two(acc[:, d]), lin[:, 2 * s:2 * s + 2, 0:HALF], ALU.add).then_inc(pair_free[s], 1)

                    for k in range(DC):
                        slots_lo(0, k)
                    with dve.Fori(0, NE) as e:
                        fit = dve.value_load(fitu[0:1, bass.ds(e, 1)], min_val=0, max_val=1)
                        nc.vector.tensor_copy(pick_e[:, :], ident[0:NE, bass.ds(e, 1)].to_broadcast([NE, P])).then_inc(pk, 1)
                        with dve.If(fit == 1):
                            expert(e, True)
                        with dve.Else():
                            expert(e, False)
                    for t in range(5):
                        n = P if t < TT else NB
                        dve.wait_ge(cb_a, t + 1)
                        stt(ctok[0:n, t % 2, :], yrow[0:n, t % 2, 1, :], gwt[0:n, t, 1:2], ctok[0:n, t % 2, :], ALU.mult, ALU.add).then_inc(cb_b, 1)
                        if t:
                            add_rows(t - 1)
                    add_rows(4)
                else:
                    for e in range(SLICES[0]):
                        b = ffn_base(0) + e * (GU_P + DOWN_P)

                        def take_gu0(s, q, i):
                            if s == 0:
                                return
                            dve.wait_ge(pe_slab, q * 2 + 2)
                            dve.wait_ge(pair_free[0], q + 1)
                            tt(two(gt), two(sg), lin[:, 2:4, 0:HALF], ALU.mult).then_inc(pair_free[1], 1)
                            dve.wait_ge(gu_hi_ok, i + (GU_P * e + 1))
                            tt(gu_lo[:, bass.ds(i, 1)].rearrange("p a t -> p (a t)"), gt,
                               gu_hi[:, bass.ds(i, 1)].rearrange("p a t -> p (a t)").bitcast(f32), ALU.subtract).then_inc(gu_ok, 1)

                        def take_down0(s, q, i):
                            dve.wait_ge(pe_slab, q * 2 + (s + 1))
                            o = acc[:, bass.ds(i * 2 + s, 1)].rearrange("p a (b c) -> p (a b) c", c=HALF)
                            tt(o, o, lin[:, 2 * s:2 * s + 2, 0:HALF], ALU.add).then_inc(pair_free[s], 1)
                        stream(b, GU_P, kcs("gu"), kcs("down")[0], take_gu0)
                        stream(b + GU_P, DOWN_P, kcs("down"), DC, take_down0)
                dve.wait_ge(r_ready, 5 * L + 4)
                normed(2 * L + 1, 48 + 8 * L)
                dve.wait_ge(r_ready, 5 * L + 5)
                make_h(3 * L + 2, 64 + 8 * L)

                def take_ple(s, q, i):
                    if s == 0:
                        return
                    dve.wait_ge(pe_slab, q * 2 + 2)
                    dve.wait_ge(pair_free[0], q + 1)
                    tt(two(gt), two(sg), lin[:, 2:4, 0:HALF], ALU.mult).then_inc(pair_free[1], 1)
                    dve.drain()
                    xd = x[:, bass.ds(i, 1)].rearrange("p a t -> p (a t)")
                    tt(xd, xd, gt, ALU.add).then_inc(ple_x, 1)
                stream(ple_base(L), PLE_P, kcs("ple"), kcs("win")[0] if L < DEPTH - 1 else 0, take_ple)


_INS = ["x_prompt", "x_sample", "state_pool", "state_mlstm_C", "state_mlstm_n", "state_mlstm_m", "p_prompt", "p_sample",
        "norm_mix_pre", "norm_mix_post", "norm_ffn_pre", "norm_ffn_post", "norm_ple", "w_in", "pool_w", "pool_scale",
        "mlstm_b_i", "mlstm_b_f", "mlstm_norm_w", "gmlp_norm_w", "gmlp_ws", "gmlp_bs", "w_out", "ffn_w_gate",
        "ffn_w_up", "ffn_w_down", "moe_router_w", "moe_router_b", "moe_w_gate", "moe_w_up", "moe_w_down",
        "ple_w_gate", "ple_w_proj"]
_OUTS = [("y_prompt", (1, SEQ, DM)), ("y_sample", (NB, 1, DM)),
         ("new_pool_prompt", (DEPTH, 1, PST, 256)), ("new_C_prompt", (DEPTH, 1, H, DH, DH)),
         ("new_n_prompt", (DEPTH, 1, H, DH)), ("new_m_prompt", (DEPTH, 1, H)),
         ("new_pool_sample", (DEPTH, NB, PST, 256)), ("new_C_sample", (DEPTH, NB, H, DH, DH)),
         ("new_n_sample", (DEPTH, NB, H, DH)), ("new_m_sample", (DEPTH, NB, H)),
         ("new_gmlp_v_sample", (DEPTH, NB, 1, 256))]


def kernel(**inputs):
    import numpy as np
    import concourse.bacc as bacc
    from concourse import mybir as mb
    from concourse.bass_utils import run_bass_kernel_spmd

    const = np.zeros((P, NCONST), np.float32)
    const[:, C_ID:C_ID + P] = np.eye(P)
    const[:64, C_BLK:C_BLK + 64] = 1 / 64
    const[64:, C_BLK + 64:C_BLK + P] = 1 / 64
    const[:, C_TRI:C_TRI + P] = np.triu(np.ones((P, P)))
    const[:, C_ONE], const[:, C_MEAN], const[:, C_MEANH] = 1, 1 / DM, 1 / DH
    const[:, C_VAL:C_VAL + TT], const[:NB, C_VAL + TT] = 1, 1
    for g, w in enumerate(WINDOWS):
        rows, j = slice(64 * (g % 2), 64 * (g % 2) + 64), g // 2
        const[rows, C_INVW + j] = 1 / w
        const[rows, C_RC + 16 * j:C_RC + 16 * j + 16] = 1 / np.minimum(w, np.arange(16) + 1)

    nc = bacc.Bacc("TRN2", target_bir_lowering=False, num_devices=1)
    arrays, A, O = {}, {}, {}
    for name in _INS + ["shape_constants"]:
        a = np.ascontiguousarray(const if name == "shape_constants" else inputs[name])
        arrays[f"in_{name}"] = a
        A[name] = nc.dram_tensor(f"in_{name}", a.shape, mb.dt.from_np(a.dtype), kind="ExternalInput").ap()
    for name, shape in _OUTS:
        O[name] = nc.dram_tensor(f"out_{name}", shape, mb.dt.float32, kind="ExternalOutput").ap()
    build(nc, A, O)
    r = run_bass_kernel_spmd(nc, [arrays], core_ids=[0])
    return tuple(r.results[0][f"out_{name}"] for name, _ in _OUTS)
```

```python
import concourse.bass as bass
from concourse import mybir
from contextlib import ExitStack

f32 = mybir.dt.float32
f32r = mybir.dt.float32r
u32 = mybir.dt.uint32
ACT = mybir.ActivationFunctionType
ALU = mybir.AluOpType
AXX = mybir.AxisListType.X

P = 128
DEPTH, DM, SEQ, NB = 2, 1024, 512, 8
TOK = SEQ + NB
HALF = TOK // 2
DC = DM // P
TT = SEQ // P
H, DH = 4, 128
NE, FS = 8, 1408
FCH = FS // P
KMAX = FCH
EPS = 1e-6
QS = float(DH) ** -0.5
PLE = 256
WINDOWS = (2, 4, 8, 16)
PST = 15
D_IN = 2824
GATE_COL = 2304
GW = 36
Z_POOL, Z_Q, Z_K, Z_V, Z_O, Z_GU, Z_GV = 0, 2, 6, 10, 14, 18, 20
WIN_P, WOUT_P, GU_P, DOWN_P, PLE_P = 11, 4, 11, 4, 8
LN_EXP_SET = 6
Y_ORDER, Y_PARTS = (0, 1, 6, 7, 2, 3, 4, 5), 6
P_AFTER = (4, 6)
CAP = 160
CAP2 = CAP - P
NMIN = 192
NSLOT = NE * CAP
SLICES = (2, NE)


def win_base(L):
    return 0 if L == 0 else ple_base(0) + PLE_P


def wout_base(L):
    return win_base(L) + WIN_P


def ffn_base(L):
    return wout_base(L) + WOUT_P


def ple_base(L):
    return ffn_base(L) + SLICES[L] * (GU_P + DOWN_P)


LAST_PAIR = ple_base(DEPTH - 1) + PLE_P - 1
MIX_PRE, MIX_POST, FFN_PRE, FFN_POST, PLE_PRE = range(5)
R_F, R_IG, R_EM, R_G, R_M, R_A = range(6)
C_ID, C_BLK, C_TRI, C_ONE, C_MEAN, C_MEANH, C_INVW, C_RC, C_VAL = 0, 128, 256, 384, 385, 386, 387, 389, 421
NCONST = C_VAL + 5


def build(nc, A, O):
    ctx = ExitStack()
    with ctx:
        def sb(name, shape, dt=f32):
            return ctx.enter_context(nc.sbuf_tensor(name, shape, dt))

        def sem(name):
            return ctx.enter_context(nc.semaphore(name))

        x = sb("x", [P, DC, TOK])
        with nc.sbuf_tensor("z_before_xg", [P, 8 * TOK], f32), \
                nc.sbuf_tensor("xg", [P, DC, 2, CAP], f32r) as xg:
            pass
        zreg = sb("zreg", [P, 23 * TOK])
        z = zreg[:, :].rearrange("p (c t) -> p c t", t=TOK)
        acc = z[:, 0:8]
        sq = z[:, 8:12]
        ht = z[:, 12:14]
        rn = z[:, 14]
        sg = z[:, 15]
        gt = z[:, 16]
        ut = z[:, 17:19]
        p_tok = zreg[:, 19 * TOK:19 * TOK + 5 * PLE].rearrange("p (t c) -> p t c", c=PLE)
        gb = z[:, 22]
        xs = zreg[:, 17 * TOK:17 * TOK + 2 * DM].rearrange("p (a c) -> p a c", c=DM)
        ys0 = zreg[:, 8 * TOK + 2 * DC * CAP:8 * TOK + 2 * DC * CAP + DM]
        x_tok = zreg[:, 0:5 * DM].rearrange("p (t c) -> p t c", c=DM)
        y_tok = zreg[:, 0:2 * DM].rearrange("p (t c) -> p t c", c=DM)
        with nc.sbuf_tensor("h_hi", [P, DC, TOK], f32r) as h_hi, \
                nc.sbuf_tensor("h_lo", [P, DC, TOK], f32r) as h_lo:
            pass
        ra = sb("region_a", [P, 2 * DC * TOK])
        with nc.sbuf_tensor("gs", [P, FCH, 2, CAP], f32r) as gs:
            pass
        with nc.sbuf_tensor("htok", [P, 5, DM], f32) as htok:
            pass
        with nc.sbuf_tensor("rows", [H, 6, TOK], f32) as rows:
            pass
        with nc.sbuf_tensor("yrow", [P, 2, 2, DM], f32) as yrow, nc.sbuf_tensor("ctok", [P, 2, DM], f32) as ctok:
            pass
        with nc.sbuf_tensor("gu_hi", [P, FCH, TOK], f32r) as gu_hi, \
                nc.sbuf_tensor("gu_lo", [P, FCH, TOK], f32r) as gu_lo:
            pass
        y_hi = sb("y_hi", [P, DC, TOK], f32r)
        with nc.sbuf_tensor("gsq", [P, 2, TOK], f32) as gsq:
            pass
        y_lo = sb("y_lo", [P, DC, TOK], f32r)
        rb = sb("region_b", [P, 2 * (FCH - DC) * TOK])
        EXT = PST + SEQ
        with nc.sbuf_tensor("p_hi", [P, 2, TOK], f32r) as p_hi, \
                nc.sbuf_tensor("p_lo", [P, 2, TOK], f32r) as p_lo:
            pass
        rc = sb("region_c", [P, 2, 2, EXT])
        with nc.sbuf_tensor("wlo", [P, 4, KMAX * P], f32r) as wlo:
            pass
        wst = sb("wst", [P, 4, KMAX * P])
        whi = sb("whi", [P, 4, KMAX * P], f32r)
        ytb = sb("ytb", [P, 2, CAP])
        const = sb("const", [P, NCONST])
        cols = sb("cols", [P, 96])
        colrows = ra[0:96, 0:P]
        with nc.sbuf_tensor("ys1", [P, DM], f32) as ys1:
            pass
        gwf = sb("gwf", [P, DC * GW + 92])
        gwh = sb("gwh", [P, DC * GW + 92], f32r)
        gwl = sb("gwl", [P, DC * GW + 92], f32r)
        bdw = sb("bdw", [P, 2, P])
        gate_b = sb("gate_b", [H, 2, DEPTH])
        sg_b = sb("sg_b", [P, 2, DEPTH, 2])
        bsr = sb("bsr", [4, DEPTH, P])
        m0 = sb("m0", [H, DEPTH, NB])
        tsm = sb("tsm", [H, NB])
        epsc = sb("epsc", [P, 1])
        spare = sb("spare", [P, 1])
        rwf = sb("rwf", [P, DC, NE])
        rwh = sb("rwh", [P, DC, NE], f32r)
        rwl = sb("rwl", [P, DC, NE], f32r)
        rbias = sb("rbias", [P, NE])
        lg = sb("lg", [P, 5, NE])
        top = sb("top", [P, 5, 8])
        topi = sb("topi", [P, 5, 8], u32)
        topf = sb("topf", [P, 5, 8])
        gwt = sb("gwt", [P, 5, 2])
        oh = sb("oh", [P, 2, 5, NE])
        msk = sb("msk", [P, 5, NE])
        rel = sb("rel", [P, 5, NE])
        fits = sb("fits", [P, NE])
        fitu = sb("fitu", [P, NE], u32)
        idxf = sb("idxf", [P, 5, 2])
        idxu = sb("idxu", [P, 5, 2], u32)
        pick_e = sb("pick_e", [NE, P])
        gatet = sb("gatet", [P, 5, NE])
        gtmp = sb("gtmp", [P, 5, NE])
        iota8 = sb("iota8", [P, NE])
        grow = sb("grow", [NE, TOK])

        def view(region, at, *shape):
            n = 1
            for s in shape:
                n *= s
            v = region[:, at:at + n]
            if len(shape) == 2:
                v = v.rearrange("p (a b) -> p a b", b=shape[1])
            if len(shape) == 3:
                v = v.rearrange("p (a b c) -> p a b c", b=shape[1], c=shape[2])
            return v, at + n

        vtok, a = view(ra, 0, TT, 129)
        ktok, a = view(ra, a, TT, P)
        kw, a = view(ra, a, TT, P)
        E, a = view(ra, a, 2, SEQ)
        W, a = view(ra, a, 2, SEQ)
        a_nd = a
        num, a = view(ra, a, H, TOK)
        D, a = view(ra, a, H, TOK)
        Cout, a = view(ra, a, 129)
        acol, a = view(ra, a, TT, H)
        kws, a = view(ra, a, H, NB)
        dcs, a = view(ra, a, H, 3, NB)
        nT, a = view(ra, a, NB, H)
        nn, a = view(ra, a, NB, H)
        qn, a = view(ra, a, H, NB)
        assert a <= 2 * DC * TOK
        wsr, a = view(ra, a_nd, 4, P)
        wmT, a = view(ra, a, 4, P)
        vnt, a = view(ra, a, 2, TT, P)
        assert a <= a_nd + H * TOK
        gr, a = view(ra, a_nd + H * TOK, 2, TOK)
        Cb, a = view(rb, 0, 3, H, P)
        Ct, a = view(rb, a, H, P)
        vs, a = view(rb, a, H, P)
        us, a = view(rb, a, 2, P)
        nst, a = view(rb, a, P)
        nout, a = view(rb, a, P)
        assert a <= 2 * (FCH - DC) * TOK
        pst = Ct[:, :, :].rearrange("p a b -> p (a b)")[:, 0:256]
        gvo = Ct[:, :, :].rearrange("p a b -> p (a b)")[:, 256:512]
        hs1 = [E[:, :, :].rearrange("p a b -> p (a b)")[:, 0:TOK], W[:, :, :].rearrange("p a b -> p (a b)")[:, 0:TOK]]
        hs2 = [ra[:, 0:TOK], ra[:, TOK:2 * TOK]]

        ident = const[:, C_ID:C_ID + P]
        blk = const[:, C_BLK:C_BLK + P]
        tri = const[:, C_TRI:C_TRI + P]
        one = const[:, C_ONE:C_ONE + 1]

        def bcol(c):
            return const[:, c:c + 1].to_broadcast([P, P])

        def pick(k, n, m=P):
            return const[0:k, n:n + 1].to_broadcast([k, m])

        def two(ap):
            return ap.rearrange("p (a b) -> p a b", b=HALF)

        xslot = nc.dram_tensor("xslot", ((NE + 1) * CAP, DM), f32).ap()
        yslot = nc.dram_tensor("yslot", (NSLOT + 1, DM), f32).ap()
        lin = ctx.enter_context(nc.psum_tensor("lin", [P, 4, 512], f32))
        aux = ctx.enter_context(nc.psum_tensor("aux", [P, 4, 512], f32))

        staged = [sem(f"staged{n}") for n in range(4)]
        filled = sem("filled")
        hi_done, lo_done = sem("hi_done"), sem("lo_done")
        pe_slab = sem("pe_slab")
        pair_free = [sem("pair_free0"), sem("pair_free1")]
        x_in, c_in, w_small = sem("x_in"), sem("c_in"), sem("w_small")
        setup_pool = sem("setup_pool")
        cols_t, cols_ok = sem("cols_t"), sem("cols_ok")
        x_t, x_ok, xs_t = sem("x_t"), sem("x_ok"), sem("xs_t")
        sq_ready, sq_used = sem("sq_ready"), sem("sq_used")
        r_ready = sem("r_ready")
        ht_ready, h_hi_ok, h_ready = sem("ht_ready"), sem("h_hi_ok"), sem("h_ready")
        ut_ready, x_dve, x_pool, ple_x = sem("ut_ready"), sem("x_dve"), sem("x_pool"), sem("ple_x")
        gw_in, gw_ok, gw_lo = sem("gw_in"), sem("gw_ok"), sem("gw_lo")
        gates = sem("gates")
        gate_l1, gate_lf, gate_scan, gate_g, gate_em = (sem(s) for s in
                                                        ("gate_l1", "gate_lf", "gate_scan", "gate_g", "gate_em"))
        lay_in = sem("lay_in")
        m_out = sem("m_out")
        pool_win, pool_t, pool_v, pool_y = sem("pool_win"), sem("pool_t"), sem("pool_v"), sem("pool_y")
        pool_mm, pool_e = sem("pool_mm"), sem("pool_e")
        g_sq, g_mean, g_r, g_vn, g_t, g_ev, g_wm, g_wt, g_mix, g_y = (
            sem(s) for s in ("g_sq", "g_mean", "g_r", "g_vn", "g_t", "g_ev", "g_wm", "g_wt", "g_mix", "g_y"))
        acol_t, acol_ok = sem("acol_t"), sem("acol_ok")
        st_t, st_ev, st_k, st_den, st_de, st_dd = (sem(s) for s in ("st_t", "st_ev", "st_k", "st_den", "st_de", "st_dd"))
        C_in = [sem(f"C_in{i}") for i in range(3)]
        C_st = sem("C_st")
        vb_ready, ct_ready, cn_ready, cq_done = sem("vb_ready"), sem("ct_ready"), sem("cn_ready"), sem("cq_done")
        st_num = sem("st_num")
        kv_t, kv_ev, gb_ready, e_ready, e_mask, s_ready, w_ready, w_used = (
            sem(s) for s in ("kv_t", "kv_ev", "gb_ready", "e_ready", "e_mask", "s_ready", "w_ready", "w_used"))
        nd_ev, nd_max, kw_ready, c_ready, c_ev, c_out = (
            sem(s) for s in ("nd_ev", "nd_max", "kw_ready", "c_ready", "c_ev", "c_out"))
        hq, hm, hd2, ha, hr, hy, hy2 = (sem(s) for s in ("hq", "hm", "hd2", "ha", "hr", "hy", "hy2"))
        sig_o, y_hi_ok, y_ok = sem("sig_o"), sem("y_hi_ok"), sem("y_ok")
        p_in, p_t, p_hi_ok, p_ok = sem("p_in"), sem("p_t"), sem("p_hi_ok"), sem("p_ok")
        gu_hi_ok, gu_ok = sem("gu_hi_ok"), sem("gu_ok")
        acc0 = sem("acc0")
        hx_t, hx_ok, x_zero, rt_oh, rt_cnt, rt_idx, xs_scat, xs_in, xg_t, xg_hi, xg_ok, pk = (
            sem(s) for s in ("hx_t", "hx_ok", "x_zero", "rt_oh", "rt_cnt", "rt_idx", "xs_scat", "xs_in", "xg_t", "xg_hi",
                             "xg_ok", "pk"))
        silu_ok = sem("silu_ok")
        yx_t, ys_ok, y_stored, cb_a, cb_b, cb_t, cb_acc = (
            sem(s) for s in ("yx_t", "ys_ok", "y_stored", "cb_a", "cb_b", "cb_t", "cb_acc"))
        y_back = [sem("y_back0"), sem("y_back1")]
        rw_lo, rt_lg, rt_max, rt_e, rt_gate, rt_t, rt_row, gb_mm, gb_ok = (
            sem(s) for s in ("rw_lo", "rt_lg", "rt_max", "rt_e", "rt_gate", "rt_t", "rt_row", "gb_mm", "gb_ok"))
        yt_t, yt_ev, out_st = sem("yt_t"), sem("yt_ev"), sem("out_st")
        y_st = [sem("y_st0"), sem("y_st1")]
        ctx.enter_context(nc.allow_non_contiguous_dma(reason="per-head rows and state columns are a few words each"))
        block = ctx.enter_context(nc.Block())

        def pair_loop(eng, base, pairs, par, body, peel=False):
            turns = (pairs - 1) // 2
            if peel or isinstance(base, int) and base == 0:
                for i in range(2):
                    body(base + i, i, (par + i) % 2)
                first = 1
            else:
                first = 0
            if turns - first > 1:
                with eng.Fori(2 * first, 2 * turns, 2) as i:
                    for a in range(2):
                        body(i + (base + a), i + a, (par + a) % 2)
                done = 2 * turns
            else:
                done = 2 * first
            for i in range(done, pairs):
                body(base + i, i, (par + i) % 2)

        def expert_par(a):
            return (ffn_base(1) + a * (GU_P + DOWN_P)) % 2

        def kcs(phase):
            return {"win": (8, 8), "wout": (8, 8), "gu": (8, 8), "down": (11, 11), "ple": (8, 2)}[phase]

        @block.sync
        def _(sp):
            tokp = A["x_prompt"][0].rearrange("(t p) c -> p t c", p=P)
            for t in range(TT):
                sp.dma_start(x_tok[:, t, :], tokp[:, t, :]).then_inc(x_in, 16)
            sp.dma_start(x_tok[0:NB, TT, :], A["x_sample"][:, 0, :]).then_inc(x_in, 16)

            def load(q, par, s, src, kc):
                slot = 2 * par + s
                if not (isinstance(q, int) and q < 2):
                    sp.wait_ge(pe_slab, q * 2 + (s - 3))
                sp.dma_start(wst[:, slot, 0:kc * P].rearrange("p (k n) -> p k n", n=P), src).then_inc(staged[slot], 16)

            def cut(w, c):
                return w.rearrange("(k p) n -> p k n", p=P)[:, :, bass.ds(c, P)]

            def loads(base, pairs, par, srcs, kc):
                def body(q, i, par):
                    for s in range(2):
                        load(q, par, s, srcs(s, i), kc[s])
                pair_loop(sp, base, pairs, par, body)

            for L in range(DEPTH):
                b, n_low = win_base(L), Z_GU // 2
                loads(b, n_low, b % 2, lambda s, i: cut(A["w_in"][L], i * 2 * P + s * P), kcs("win"))
                loads(b + n_low, WIN_P - n_low, (b + n_low) % 2,
                      lambda s, i: cut(A["w_in"][L], i * 2 * P + (s * P + Z_GU * P + 2 * H)), kcs("win"))
                b = wout_base(L)
                loads(b, WOUT_P, b % 2, lambda s, i: cut(A["w_out"][L], i * 2 * P + s * P), kcs("wout"))
                if L == 0:
                    for e in range(SLICES[0]):
                        b = ffn_base(0) + e * (GU_P + DOWN_P)
                        loads(b, GU_P, b % 2,
                              lambda s, i: cut(A[("ffn_w_gate", "ffn_w_up")[s]][0], i * P + e * FS), kcs("gu"))
                        loads(b + GU_P, DOWN_P, (b + GU_P) % 2,
                              lambda s, i: cut(A["ffn_w_down"][0, e * FS:(e + 1) * FS], i * 2 * P + s * P), kcs("down"))
                else:
                    def expert(e, par):
                        def w(name):
                            k = A[name].shape[2] // P
                            return A[name][0].rearrange("e (k p) n -> p (e k) n", p=P)[:, bass.ds(e * k, k), :]
                        b = e * (GU_P + DOWN_P) + ffn_base(1)
                        loads(b, GU_P, par,
                              lambda s, i: w(("moe_w_gate", "moe_w_up")[s])[:, :, bass.ds(i * P, P)], kcs("gu"))
                        loads(b + GU_P, DOWN_P, (par + GU_P) % 2,
                              lambda s, i: w("moe_w_down")[:, :, bass.ds(i * 2 * P + s * P, P)], kcs("down"))
                    with sp.Fori(0, NE // 2) as j:
                        for a in range(2):
                            expert(j * 2 + a, expert_par(a))
                b = ple_base(L)
                if L:
                    slot = 2 * (b % 2) + 1
                    sp.wait_ge(pe_slab, b * 2 - 2)
                    sp.dma_start(wst[:, slot, 0:DC * P].rearrange("p (k n) -> p k n", n=P),
                                 cut(A["ple_w_gate"][L], 0)).then_inc(filled, 16)
                    sp.wait_ge(filled, 16)
                loads(b, PLE_P, b % 2, lambda s, i: cut(A[("ple_w_gate", "ple_w_proj")[s]][L], i * P), kcs("ple"))
            for t in range(TT + 1):
                sp.wait_ge(yt_ev, t + 1)
                if t < TT:
                    sp.dma_start(O["y_prompt"][0, t * P:(t + 1) * P, :], y_tok[:, t % 2, :]).then_inc(y_st[t % 2], 16)
                else:
                    sp.dma_start(O["y_sample"][:, 0, :], y_tok[0:NB, t % 2, :]).then_inc(y_st[t % 2], 16)
            sp.wait_ge(y_st[0], 16 * 3)
            sp.wait_ge(y_st[1], 16 * 2)

        @block.gpsimd
        def _(pool):
            pool.dma_start(const[:, :], A["shape_constants"]).then_inc(c_in, 16)
            for n, w in enumerate(("norm_mix_pre", "norm_mix_post", "norm_ffn_pre", "norm_ffn_post", "norm_ple")):
                pool.dma_start(colrows[16 * n:16 * n + 16, :],
                               A[w].rearrange("l (c p) -> (l c) p", p=P)).then_inc(c_in, 16)
            pool.dma_start(colrows[80:84, :], A["pool_scale"].rearrange("l (c p) -> (l c) p", p=P)).then_inc(c_in, 16)
            pool.dma_start(colrows[84:92, :], A["mlstm_norm_w"].rearrange("l (c p) -> (l c) p", p=P)).then_inc(c_in, 16)
            pool.dma_start(colrows[92:96, :], A["gmlp_norm_w"].rearrange("l (c p) -> (l c) p", p=P)).then_inc(c_in, 16)
            small = [(gate_b[:, 0, :], A["mlstm_b_i"].rearrange("l h -> h l")),
                     (gate_b[:, 1, :], A["mlstm_b_f"].rearrange("l h -> h l")),
                     (rbias[:, :], A["moe_router_b"][0].partition_broadcast(P)),
                     (bsr[:, :, :], A["gmlp_bs"].rearrange("l g t -> g l t")),
                     (rwf[:, :, :], A["moe_router_w"][0].rearrange("(k p) n -> p k n", p=P))]
            for L in range(DEPTH):
                small.append((m0[:, L, :], A["state_mlstm_m"][L].rearrange("b h -> h b")))
                for g in range(4):
                    at = slice(64 * (g % 2), 64 * (g % 2) + 64)
                    small.append((sg_b[at, 0, L, g // 2:g // 2 + 1], A["gmlp_ws"][L, g, 0, 0:1].partition_broadcast(64)))
                    small.append((sg_b[at, 1, L, g // 2:g // 2 + 1], A["gmlp_bs"][L, g, 0:1].partition_broadcast(64)))
            pool.memset(gwf[:, :], 0.0)
            pool.memset(epsc[:, :], EPS)
            pool.memset(bdw[:, :, :], 0.0)
            pool.iota(topi[:, 0, :], pattern=[[1, NE]], base=0, channel_multiplier=0)
            pool.drain()
            pool.tensor_copy(iota8[:, :], topi[:, 0, :]).then_inc(setup_pool, 1)
            pool.memset(ytb[:, :, :], 0.0)
            pool.memset(lg[:, :, :], 0.0)

            def add_x(N):
                for c in range(1, DC, 2):
                    pool.wait_ge(ut_ready, N * DC + c + 1)
                    pool.tensor_tensor(x[:, c], x[:, c], ut[:, 1], ALU.add).then_inc(x_pool, 1)

            for L in range(DEPTH):
                if L:
                    pool.wait_ge(h_ready, DC * 3 * L)
                pool.wait_ge(setup_pool, 1)
                gsrc = A["w_in"][L].rearrange("(k p) n -> p k n", p=P)
                gdst = gwf[:, 0:DC * GW].rearrange("p (k n) -> p k n", n=GW)
                pool.dma_start(gdst[:, :, 0:H], gsrc[:, :, GATE_COL:GATE_COL + H]).then_inc(gw_in, 16)
                pool.dma_start(gdst[:, :, 32:32 + H], gsrc[:, :, GATE_COL + H:GATE_COL + 2 * H]).then_inc(gw_in, 16)
                for g in range(4):
                    o = 64 * (g % 2)
                    pool.dma_start(bdw[o:o + 64, g // 2, o:o + 64], A["pool_w"][L, g]).then_inc(lay_in, 16)
                if L:
                    pool.wait_ge(pair_free[1], ple_base(0) + 1)
                pool.dma_start(pst[0:NB * PST, :], A["state_pool"][L].rearrange("b r c -> (b r) c")).then_inc(lay_in, 16)
                pool.dma_start(nst[0:NB * H, :], A["state_mlstm_n"][L].rearrange("b h k -> (b h) k")).then_inc(lay_in, 16)
                pool.dma_start(O["new_pool_sample"][L, :, 0:PST - 1, :], A["state_pool"][L, :, 1:PST, :]).then_inc(out_st, 16)
                if L == 0:
                    for dst, src in small:
                        pool.dma_start(dst, src).then_inc(w_small, 16)
                    pool.wait_ge(w_small, 16 * len(small))
                pool.wait_ge(gate_l1, L + 1)
                pool.tensor_scalar(rows[:, R_F], rows[:, R_F], 0.0, None, ALU.min)
                pool.drain()
                pool.tensor_tensor(rows[:, R_F], rows[:, R_F], rows[:, R_EM], ALU.subtract)
                pool.drain()
                pool.memset(rows[:, R_A], 0.0)
                pool.tensor_tensor(tsm[:, :], rows[:, R_F, SEQ:TOK], m0[:, L, :], ALU.add).then_inc(gate_lf, 1)
                pool.wait_ge(pair_free[0], win_base(L) + 1)
                pool.wait_ge(pair_free[1], win_base(L) + 1)
                pool.memset(rc[:, :, :, 0:PST], 0.0)
                pool.tensor_copy(rc[:, 0, :, PST:EXT], z[:, Z_POOL:Z_POOL + 2, 0:SEQ])
                pool.drain()
                src = 0
                for g, w in enumerate(WINDOWS):
                    sh = w // 2
                    lo = 64 if g % 2 else 0
                    j = g // 2
                    pool.tensor_tensor(rc[:, 1 - src, :, PST:EXT], rc[:, src, :, PST:EXT],
                                       rc[:, src, :, PST - sh:EXT - sh], ALU.add)
                    pool.drain()
                    src = 1 - src
                    s_ = rc[lo:lo + 64, src, j, PST:EXT]
                    zz = z[lo:lo + 64, Z_POOL + j, 0:SEQ]
                    pool.tensor_tensor(gsq[lo:lo + 64, j, 0:16], s_[:, 0:16],
                                       const[lo:lo + 64, C_RC + 16 * j:C_RC + 16 * j + 16], ALU.mult)
                    pool.tensor_scalar(gsq[lo:lo + 64, j, 16:SEQ], s_[:, 16:SEQ],
                                       const[lo:lo + 64, C_INVW + j:C_INVW + j + 1], None, ALU.mult)
                    pool.drain()
                    ins = pool.tensor_tensor(gsq[lo:lo + 64, j, 0:SEQ], gsq[lo:lo + 64, j, 0:SEQ], zz, ALU.subtract)
                    if g < 3:
                        pool.drain()
                ins.then_inc(pool_win, 1)
                pool.wait_ge(gate_scan, L + 1)
                pool.tensor_tensor(rows[:, R_A, 0:SEQ], rows[:, R_IG, 0:SEQ], rows[:, R_G, 0:SEQ], ALU.subtract)
                pool.tensor_tensor(rows[:, R_A, SEQ:TOK], rows[:, R_IG, SEQ:TOK], rows[:, R_M, SEQ:TOK], ALU.subtract)
                pool.drain()
                pool.tensor_tensor(rows[:, R_G, 0:SEQ], rows[:, R_G, 0:SEQ], rows[:, R_M, 0:SEQ], ALU.subtract)
                pool.tensor_tensor(rows[:, R_G, SEQ:TOK], tsm[:, :], rows[:, R_M, SEQ:TOK],
                                   ALU.subtract).then_inc(gate_g, 1)
                if L == 0:
                    xflat = xslot.rearrange("(p r) c -> p r c", r=12)
                    zeros = ytb[:, :, 0:P].rearrange("p a (b c) -> p a b c", b=1)[:, 0].to_broadcast([P, DM // P, P])
                    for n in range(12):
                        pool.dma_start(xflat[:, n].rearrange("p (a c) -> p a c", c=P),
                                       zeros[0:(NE + 1) * CAP // 12]).then_inc(x_zero, 16)
                    for n in range(2):
                        half = yslot[NSLOT:NSLOT + 1, n * (DM // 2):(n + 1) * (DM // 2)]
                        pool.dma_start(half.rearrange("p (a c) -> p a c", c=P), zeros[0:1, 0:DM // 2 // P]).then_inc(y_stored, 16)
                pool.wait_ge(pair_free[1], win_base(L) + WIN_P)
                pool.dma_start(wsr[:, :, :], A["gmlp_ws"][L].rearrange("g t s -> t g s")).then_inc(lay_in, 16)
                for b in range(3):
                    pool.dma_start(Cb[:, b], A["state_mlstm_C"][L, b].rearrange("h k v -> k h v")).then_inc(C_in[b], 16)
                pool.wait_ge(gate_g, L + 1)
                pool.dma_start(O["new_m_prompt"][L].rearrange("a h -> h a"), rows[:, R_M, SEQ - 1:SEQ]).then_inc(m_out, 16)
                pool.dma_start(O["new_m_sample"][L].rearrange("b h -> h b"), rows[:, R_M, SEQ:TOK]).then_inc(m_out, 16)
                pool.wait_ge(pool_e, 2 * L + 2)
                pool.dma_start(O["new_pool_sample"][L, :, PST - 1, :], us[0:NB, :, :].rearrange("p a b -> p (a b)")).then_inc(out_st, 16)
                pool.dma_start(O["new_pool_prompt"][L, 0], us[32:32 + PST, :, :].rearrange("p a b -> p (a b)")).then_inc(out_st, 16)
                pool.wait_ge(g_ev, 3 * L + 3)
                pool.dma_start(O["new_gmlp_v_sample"][L, :, 0, :], gvo[0:NB, :]).then_inc(out_st, 16)
                for b in range(NB):
                    pool.wait_ge(cn_ready, NB * L + b + 1)
                    pool.dma_start(O["new_C_sample"][L, b].rearrange("h k v -> k h v"), Cb[:, b % 3]).then_inc(C_st, 16)
                    if b + 3 < NB:
                        pool.wait_ge(C_st, 16 * (NB * L + b + 1))
                        pool.wait_ge(cq_done, NB * L + b + 1)
                        pool.dma_start(Cb[:, b % 3], A["state_mlstm_C"][L, b + 3].rearrange("h k v -> k h v")).then_inc(C_in[b % 3], 16)
                pool.wait_ge(st_de, 2 * L + 2)
                pool.dma_start(O["new_n_sample"][L].rearrange("b h k -> (b h) k"), nout[0:NB * H, :]).then_inc(out_st, 16)
                for h in range(H):
                    hn = H * L + h
                    for i in range(TT):
                        n = TT * hn + i
                        w = SEQ - P * i
                        pool.wait_ge(e_ready, n + 1)
                        pool.affine_select(out=E[:, i % 2, 0:P], in_=E[:, i % 2, 0:P], compare_op=ALU.is_ge, fill=0.0,
                                           base=0, pattern=[[1, P]], channel_multiplier=-1).then_inc(e_mask, 1)
                        pool.wait_ge(kv_ev, hn + 1)
                        if i == 3:
                            pool.wait_ge(e_mask, n + 1)
                        if i == 0 and h:
                            pool.wait_ge(c_ready, hn)
                        pool.tensor_scalar(kw[:, i], ktok[:, i], E[:, i % 2, w - 1:w], None, ALU.mult).then_inc(kw_ready, 1)
                    pool.wait_ge(c_ev, hn + 1)
                    pool.dma_start(O["new_C_prompt"][L, 0, h], Cout[:, 0:P]).then_inc(c_out, 16)
                    pool.dma_start(O["new_n_prompt"][L, 0, h].rearrange("(k a) -> k a", a=1), Cout[:, P:P + 1]).then_inc(c_out, 16)
                for h in range(H):
                    hn = H * L + h
                    if h == 0:
                        pool.wait_ge(st_dd, L + 1)
                        pool.wait_ge(nd_max, H * (L + 1))
                    pool.tensor_tensor(D[:, h], D[:, h], D[:, h], ALU.mult).then_inc(hd2, 1)
                pool.wait_ge(sig_o, L + 1)
                for h in range(H):
                    hn = H * L + h
                    pool.wait_ge(hy, hn + 1)
                    pool.tensor_tensor(z[:, Z_O + h], num[:, h], z[:, Z_O + h], ALU.mult).then_inc(hy2, 1)
                pool.wait_ge(y_ok, Y_PARTS * (L + 1))
                pool.dma_start(p_tok[:, 0:TT, :], A["p_prompt"][L, 0].rearrange("(t p) c -> p t c", p=P)).then_inc(p_in, 16)
                pool.dma_start(p_tok[0:NB, TT, :], A["p_sample"][L, :, 0, :]).then_inc(p_in, 16)
                add_x(2 * L)
                pool.wait_ge(r_ready, 5 * L + 3)
                if L:
                    pool.memset(ytb[:, :, :], 0.0)
                pool.memset(acc[:, :, :], 0.0).then_inc(acc0, 1)
                if L:
                    pool.wait_ge(hx_ok, DC)
                    pool.wait_ge(rt_idx, 1)
                    pool.wait_ge(x_zero, 16 * 12)
                    for t in range(5):
                        n = P if t < TT else NB
                        for k in range(2):
                            pool.indirect_dma_start(out=xslot[:, :], out_offset=bass.IndirectOffsetOnAxis(ap=idxu[0:n, t, k:k + 1], axis=0),
                                                    in_=htok[0:n, t, :], in_offset=None, bounds_check=NSLOT - 1,
                                                    oob_is_err=False).then_inc(xs_scat, 16)
                    pool.wait_ge(xs_scat, 16 * 10)

                    def load_slots(at):
                        pool.dma_start(xs[:, 0, :], xslot[bass.ds(at, P), :]).then_inc(xs_in, 16)
                        pool.dma_start(xs[0:CAP2, 1, :], xslot[bass.ds(at + P, CAP2), :]).then_inc(xs_in, 16)
                    load_slots(0)
                    with pool.Fori(0, NE) as e:
                        pool.wait_ge(xg_t, e * DC + DC)
                        load_slots(e * CAP + CAP)
                        pool.wait_ge(ys_ok, e * DC + DC)
                        pool.dma_start(yslot[bass.ds(e * CAP, P), :], ys0).then_inc(y_stored, 16)
                        pool.dma_start(yslot[bass.ds(e * CAP + P, CAP2), :], ys1[0:CAP2, :]).then_inc(y_stored, 16)
                    pool.wait_ge(y_stored, 32 * (NE + 1))
                    for t in range(5):
                        n = P if t < TT else NB
                        if t >= 2:
                            pool.wait_ge(cb_b, t - 1)
                        for k in range(2):
                            pool.indirect_dma_start(out=yrow[0:n, t % 2, k, :], out_offset=None, in_=yslot[:, :],
                                                    in_offset=bass.IndirectOffsetOnAxis(ap=idxu[0:n, t, k:k + 1], axis=0),
                                                    bounds_check=NSLOT, oob_is_err=False).then_inc(y_back[t % 2], 16)
                add_x(2 * L + 1)
            pool.wait_ge(out_st, 16 * 5 * DEPTH)
            pool.wait_ge(m_out, 16 * 2 * DEPTH)
            pool.wait_ge(c_out, 16 * 2 * H * DEPTH)
            pool.wait_ge(C_st, 16 * NB * DEPTH)

        @block.tensor
        def _(pe):
            def mm(out, lhsT, rhs, start=True, stop=True):
                return nc.tensor.matmul(out, lhsT, rhs, start=start, stop=stop)

            pe.wait_ge(c_in, 16 * 9)
            nc.tensor.transpose(aux[:, 3, 0:96], colrows[0:96, :], ident[0:96, 0:96]).then_inc(cols_t, 1)
            pe.wait_ge(x_in, 16 * 5)
            for c in range(DC):
                if c >= 3:
                    pe.wait_ge(x_ok, c - 2)
                for t in range(TT):
                    last = nc.tensor.transpose(aux[:, c % 3, t * P:(t + 1) * P], x_tok[:, t, c * P:(c + 1) * P], ident)
                last.then_inc(x_t, 1)
            for c in range(DC):
                last = nc.tensor.transpose(lin[:, 0, c * NB:(c + 1) * NB], x_tok[0:NB, TT, c * P:(c + 1) * P], ident[0:NB, 0:NB])
            last.then_inc(xs_t, 1)

            def mean(N, c):
                pe.wait_ge(sq_ready, N * DC + c + 1)
                for a in range(2):
                    last = mm(aux[:, a, 0:HALF], bcol(C_MEAN), two(sq[:, c % 4])[:, a], c == 0, c == DC - 1)
                last.then_inc(sq_used, 1)

            def norm(N):
                for c in range(DC):
                    mean(N, c)

            def slab(q, par, s, kc, rhs_hi, rhs_lo, order=None, ready=None):
                ks = range(kc) if order is None else order
                w = 2 * par + s
                pe.wait_ge(lo_done, q * 2 + (s + 1))
                if not (isinstance(q, int) and q == 0):
                    pe.wait_ge(pair_free[s], q)
                for k in ks:
                    whk, wlk = whi[:, w, k * P:(k + 1) * P], wlo[:, w, k * P:(k + 1) * P]
                    st, en = k == ks[0], k == ks[-1]
                    if ready is not None:
                        ready(k)
                    for a in range(2):
                        o = lin[:, 2 * s + a, 0:HALF]
                        mm(o, whk, two(rhs_hi[:, k])[:, a], st, False)
                        mm(o, whk, two(rhs_lo[:, k])[:, a], False, False)
                    for a in range(2):
                        last = mm(lin[:, 2 * s + a, 0:HALF], wlk, two(rhs_hi[:, k])[:, a], False, en)
                last.then_inc(pe_slab, 1)

            def stream(base, pairs, kc, rhs, ready=None, after_slab=None, order=None):
                def body(q, i, par):
                    for s in range(2):
                        slab(q, par, s, kc[s], *rhs[s], order, ready if isinstance(i, int) and i == 0 and s == 0 else None)
                        if after_slab is not None:
                            after_slab(2 * i + s)
                pair_loop(pe, base, pairs, base % 2, body, peel=ready is not None)

            hh, yy, gg, pp = (h_hi, h_lo), (y_hi, y_lo), (gu_hi, gu_lo), (p_hi, p_lo)
            for L in range(DEPTH):
                norm(5 * L)
                pe.wait_ge(gw_lo, L + 1)
                for k in range(DC):
                    pe.wait_ge(h_ready, DC * 3 * L + k + 1)
                    gk = slice(k * GW, k * GW + P)
                    for a in range(2):
                        o = aux[:, 2 + a, 0:HALF]
                        mm(o, gwh[:, gk], two(h_hi[:, k])[:, a], k == 0, False)
                        mm(o, gwh[:, gk], two(h_lo[:, k])[:, a], False, False)
                        last = mm(o, gwl[:, gk], two(h_hi[:, k])[:, a], False, k == DC - 1)
                last.then_inc(gates, 1)
                stream(win_base(L), WIN_P, kcs("win"), (hh, hh))

                pe.wait_ge(pair_free[1], win_base(L) + WIN_P)
                pe.wait_ge(lay_in, 16 * 7 * (L + 1))
                for j in range(2):
                    nc.tensor.transpose(aux[0:NB, 0, j * P:(j + 1) * P], z[:, Z_POOL + j, SEQ:TOK], ident)
                    nc.tensor.transpose(aux[0:PST, 1, j * P:(j + 1) * P], z[:, Z_POOL + j, SEQ - PST:SEQ], ident)
                    last = nc.tensor.transpose(aux[:, 2, j * P:j * P + NB * PST], pst[0:NB * PST, j * P:(j + 1) * P],
                                               ident[0:NB * PST, 0:NB * PST])
                last.then_inc(pool_t, 1)
                for g in range(4):
                    last = nc.tensor.transpose(lin[:, 0, g * P:(g + 1) * P], wsr[:, g, :], ident)
                last.then_inc(g_wt, 1)
                for j in range(2):
                    n = 2 * L + j
                    pe.wait_ge(g_sq, n + 1)
                    for a in range(2):
                        last = mm(lin[:, 2 + a, 0:HALF], blk, two(gr[:, j])[:, a])
                    last.then_inc(g_mean, 1)
                    if j == 0:
                        pe.wait_ge(g_r, n + 1)
                pe.wait_ge(pool_v, L + 1)
                pe.wait_ge(pool_e, 2 * L + 2)
                for j in range(2):
                    for a in range(2):
                        last = mm(aux[:, 2 * j + a, 0:HALF], bdw[:, j, :], two(gsq[:, j])[:, a])
                last.then_inc(pool_mm, 1)
                for j in range(2):
                    pe.wait_ge(g_vn, 2 * L + 2)
                    for i in range(TT):
                        last = nc.tensor.transpose(lin[:, 2 + j, i * P:(i + 1) * P], z[:, Z_GV + j, i * P:(i + 1) * P], ident)
                    last.then_inc(g_t, 1)
                pe.wait_ge(g_wm, L + 1)
                for j in range(2):
                    last = nc.tensor.transpose(lin[0:NB, 0, j * P:(j + 1) * P], z[:, Z_GV + j, SEQ:TOK], ident)
                last.then_inc(g_t, 1)
                pe.wait_ge(pool_y, L + 1)
                pe.wait_ge(g_ev, 3 * L + 2)
                for j in range(2):
                    for i in range(TT):
                        for g in range(2):
                            o = aux[64 * g:64 * g + 64, j, i * P:(i + 1) * P]
                            mm(o, vnt[:, j, i, 64 * g:64 * g + 64], wmT[:, 2 * j + g, :], True, False)
                            last = mm(o, pick(4, 2 * j + g, 64), bsr[:, L, :], False, True)
                    last.then_inc(g_mix, 1)
                pe.wait_ge(gate_em, L + 1)
                pe.wait_ge(g_y, L + 1)
                for i in range(TT):
                    last = nc.tensor.transpose(aux[:, 0, i * H:(i + 1) * H], rows[:, R_A, i * P:(i + 1) * P], ident[0:H, 0:H])
                last.then_inc(acol_t, 1)
                for h in range(H):
                    nc.tensor.transpose(aux[0:NB, 1, h * P:(h + 1) * P], z[:, Z_V + h, SEQ:TOK], ident)
                    for n, r in enumerate((R_EM, R_G, R_A)):
                        mm(aux[:, 2, (3 * h + n) * NB:(3 * h + n + 1) * NB], pick(H, h), rows[:, r, SEQ:TOK])
                nc.tensor.transpose(aux[:, 3, 0:NB * H], nst[0:NB * H, :], ident[0:NB * H, 0:NB * H]).then_inc(st_t, 1)
                pe.wait_ge(st_k, L + 1)
                mm(aux[:, 3, 0:H * NB], bcol(C_ONE), qn.rearrange("p h b -> p (h b)"))
                nc.tensor.transpose(aux[0:NB * H, 2, 0:P], nn.rearrange("p b h -> p (b h)"), ident).then_inc(st_den, 1)
                for b in range(NB):
                    n = NB * L + b
                    if b >= 2:
                        pe.wait_ge(ct_ready, n - 1)
                    elif b == 0:
                        pe.wait_ge(g_ev, 3 * L + 3)
                    mm(lin[:, b % 2, :], pick(NB, b), vs[0:NB].rearrange("p h v -> p (h v)")).then_inc(vb_ready, 1)
                    if b >= 1:
                        pe.wait_ge(cn_ready, n)
                        for h in range(H):
                            last = mm(lin[:, 2, h * NB + b - 1:h * NB + b], Cb[:, (b - 1) % 3, h], z[:, Z_Q + h, SEQ + b - 1:SEQ + b])
                        last.then_inc(cq_done, 1)
                pe.wait_ge(cn_ready, NB * (L + 1))
                for h in range(H):
                    last = mm(lin[:, 2, h * NB + NB - 1:h * NB + NB], Cb[:, (NB - 1) % 3, h], z[:, Z_Q + h, TOK - 1:TOK])
                last.then_inc(cq_done, 1)
                pe.wait_ge(st_num, L + 1)
                for h in range(H):
                    hn = H * L + h
                    if h:
                        pe.wait_ge(nd_max, hn)
                        pe.wait_ge(nd_ev, hn)
                        pe.wait_ge(c_ev, hn)
                    else:
                        pe.wait_ge(st_dd, L + 1)
                        pe.wait_ge(acol_ok, L + 1)
                    for i in range(TT):
                        nc.tensor.transpose(aux[:, 0, i * P:(i + 1) * P], z[:, Z_V + h, i * P:(i + 1) * P], ident)
                        last = nc.tensor.transpose(aux[:, 1, i * P:(i + 1) * P], z[:, Z_K + h, i * P:(i + 1) * P], ident)
                    last.then_inc(kv_t, 1)
                    mm(aux[:, 2, :], pick(H, h), rows[:, R_G, 0:SEQ])
                    mm(aux[:, 3, :], pick(H, h), rows[:, R_EM, 0:SEQ]).then_inc(gb_ready, 1)
                    for i in range(TT):
                        mm(lin[:, i, 0:SEQ - i * P], z[:, Z_K + h, i * P:(i + 1) * P], z[:, Z_Q + h, i * P:SEQ]).then_inc(s_ready, 1)
                    pe.wait_ge(kv_ev, hn + 1)
                    for i in range(TT):
                        n = TT * hn + i
                        pe.wait_ge(w_ready, n + 1)
                        w = SEQ - i * P
                        mm(aux[:, 0, i * P:SEQ], vtok[:, i, 0:P], W[:, i % 2, 0:w], i == 0, i == TT - 1)
                        mm(aux[:, 1, i * P:SEQ], bcol(C_ONE), W[:, i % 2, 0:w], i == 0, i == TT - 1).then_inc(w_used, 1)
                    pe.wait_ge(e_ready, TT * (hn + 1))
                    pe.wait_ge(kw_ready, TT * (hn + 1))
                    for i in range(TT):
                        last = mm(aux[:, 2, 0:P + 1], kw[:, i], vtok[:, i, :], i == 0, i == TT - 1)
                    last.then_inc(c_ready, 1)
                for h in range(H):
                    hn = H * L + h
                    pe.wait_ge(hq, hn + 1)
                    if h == 0:
                        pe.wait_ge(nd_max, H * (L + 1))
                    if h == 1:
                        pe.wait_ge(c_ev, H * (L + 1))
                    if h >= 2:
                        pe.wait_ge(ha, hn - 1)
                    for a in range(2):
                        last = mm(aux[:, 2 * (h % 2) + a, 0:HALF], bcol(C_MEANH), two(hs1[h % 2])[:, a])
                    last.then_inc(hm, 1)

                def with_wout(n):
                    if n:
                        mean(5 * L + 1, n - 1)
                    if n + 1 in P_AFTER:
                        j = P_AFTER.index(n + 1)
                        if j == 0:
                            pe.wait_ge(p_in, 32 * (L + 1))
                        else:
                            pe.wait_ge(p_ok, 2 * L + 1)
                        for t in range(TT):
                            nc.tensor.transpose(aux[:, 2, t * P:(t + 1) * P], p_tok[:, t, j * P:(j + 1) * P], ident)
                        nc.tensor.transpose(aux[:, 3, 0:NB], p_tok[0:NB, TT, j * P:(j + 1) * P], ident[0:NB, 0:NB]).then_inc(p_t, 1)
                pe.wait_ge(ha, H * (L + 1))
                stream(wout_base(L), WOUT_P, kcs("wout"), (yy, yy), after_slab=with_wout, order=Y_ORDER,
                       ready=lambda k: pe.wait_ge(y_ok, Y_PARTS * L + (1, 1, 3, 4, 5, 6, 2, 2)[k]))
                mean(5 * L + 1, DC - 1)
                norm(5 * L + 2)
                if L:
                    for c in range(DC):
                        pe.wait_ge(ht_ready, DC * (3 * L + 1) + c + 1)
                        if c >= 2:
                            pe.wait_ge(hx_ok, c - 1)
                        else:
                            pe.wait_ge(r_ready, 5 * L + 3)
                        for t in range(TT):
                            nc.tensor.transpose(aux[:, 2 + c % 2, t * P:(t + 1) * P], ht[:, c % 2, t * P:(t + 1) * P], ident)
                        nc.tensor.transpose(aux[0:NB, c % 2, 0:P], ht[:, c % 2, SEQ:TOK], ident).then_inc(hx_t, 1)
                if L:
                    pe.wait_ge(h_ready, DC * (3 * L + 2))
                    pe.wait_ge(rw_lo, 1)
                    pe.wait_ge(hx_ok, DC)
                    for t in range(TT):
                        at = slice(t * P, (t + 1) * P)
                        for k in range(DC):
                            o = aux[:, 2, t * NE:(t + 1) * NE]
                            mm(o, h_hi[:, k, at], rwh[:, k], k == 0, False)
                            mm(o, h_lo[:, k, at], rwh[:, k], False, False)
                            mm(o, h_hi[:, k, at], rwl[:, k], False, k == DC - 1)
                    for k in range(DC):
                        o = aux[0:NB, 2, TT * NE:(TT + 1) * NE]
                        mm(o, h_hi[:, k, SEQ:TOK].bitcast(f32), rwf[:, k], k == 0, False)
                        last = mm(o, h_lo[:, k, SEQ:TOK].bitcast(f32), rwf[:, k], False, k == DC - 1)
                    last.then_inc(rt_lg, 1)
                    pe.wait_ge(rt_oh, 1)
                    for t in range(6):
                        o = aux[:, 3, t * NE:(t + 1) * NE]
                        for u in range(min(t, 5)):
                            last = mm(o, bcol(C_ONE), msk[:, u], u == 0, t == 5 and u == 4)
                        if t < 5:
                            last = mm(o, tri, msk[:, t], t == 0, True)
                    last.then_inc(rt_cnt, 1)
                    pe.wait_ge(rt_gate, 1)
                    for t in range(TT):
                        nc.tensor.transpose(aux[0:NE, 3, t * P:(t + 1) * P], gatet[:, t], ident)
                    nc.tensor.transpose(aux[0:NE, 2, 0:P], gatet[:, TT], ident).then_inc(rt_t, 1)
                    pe.wait_ge(rt_row, 1)

                    def slots_in(e, k, first=False):
                        if k == 0:
                            pe.wait_ge(xs_in, e * 32 + 32)
                        if k >= 2:
                            pe.wait_ge(xg_ok, e * DC + (k - 1))
                        nc.tensor.transpose(aux[:, k % 2, 0:P], xs[:, 0, k * P:(k + 1) * P], ident)
                        nc.tensor.transpose(aux[:, k % 2, P:CAP], xs[0:CAP2, 1, k * P:(k + 1) * P],
                                            ident[0:CAP2, 0:CAP2]).then_inc(xg_t, 1)

                    def rows_out(e, d):
                        pe.wait_ge(pair_free[d % 2], e * (GU_P + DOWN_P) + (ffn_base(1) + GU_P + d // 2 + 1))
                        if d >= 2:
                            pe.wait_ge(ys_ok, e * DC + (d - 1))
                        nc.tensor.transpose(aux[:, 2 + d % 2, 0:P], ytb[:, d % 2, 0:P], ident)
                        nc.tensor.transpose(aux[0:CAP2, 2 + d % 2, P:2 * P], ytb[:, d % 2, P:CAP], ident).then_inc(yx_t, 1)

                    def slab_slots(q, par, s, kc, rhs):
                        w = 2 * par + s
                        pe.wait_ge(lo_done, q * 2 + (s + 1))
                        pe.wait_ge(pair_free[s], q)
                        for k in range(kc):
                            whk, wlk = whi[:, w, k * P:(k + 1) * P], wlo[:, w, k * P:(k + 1) * P]
                            hl = rhs[:, k].rearrange("p a t -> p (a t)")
                            mm(lin[:, 2 * s, 0:2 * CAP], whk, hl, k == 0, False)
                            last = mm(lin[:, 2 * s, 0:NMIN], wlk, hl[:, 0:NMIN], False, k == kc - 1)
                        last.then_inc(pe_slab, 1)

                    def expert(e, par, slots):
                        b = e * (GU_P + DOWN_P) + ffn_base(1)

                        def gu(q, i, par):
                            for s in range(2):
                                if slots:
                                    slab_slots(q, par, s, DC, xg)
                                else:
                                    slab(q, par, s, DC, h_hi, h_lo)
                        pair_loop(pe, b, GU_P, par, gu)
                        pe.wait_ge(gu_ok, e * GU_P + GU_P * (SLICES[0] + 1))
                        for d in range(DC):
                            q, dpar = b + (GU_P + d // 2), (par + GU_P + d // 2) % 2
                            if slots:
                                slab_slots(q, dpar, d % 2, FCH, gs)
                            else:
                                slab(q, dpar, d % 2, FCH, gu_hi, gu_lo)
                            slots_in(e + 1, d)
                            if d == 0:
                                gate_row(e + 1)
                            else:
                                if d == 1:
                                    pe.wait_ge(gb_ok, e + 2)
                                rows_out(e, d - 1)
                        rows_out(e, DC - 1)

                    def gate_row(e):
                        pe.wait_ge(pk, e + 1)
                        for a in range(2):
                            last = mm(aux[:, 2 + a, 0:HALF], pick_e[:, :], two(grow[:, :])[:, a])
                        last.then_inc(gb_mm, 1)

                    gate_row(0)
                    for k in range(DC):
                        slots_in(0, k)

                    def run(e, par):
                        fit = pe.value_load(fitu[0:1, bass.ds(e, 1)], min_val=0, max_val=1)
                        pe.wait_ge(xg_ok, e * DC + DC)
                        with pe.If(fit == 1):
                            expert(e, par, True)
                        with pe.Else():
                            expert(e, par, False)

                    with pe.Fori(0, NE // 2) as j:
                        for a in range(2):
                            run(j * 2 + a, expert_par(a))
                    pe.wait_ge(pair_free[0], ple_base(1))
                    pe.wait_ge(pair_free[1], ple_base(1))
                    for t in range(5):
                        n = P if t < TT else NB
                        pe.wait_ge(cb_b, t + 1)
                        if t >= 2:
                            pe.wait_ge(cb_acc, t - 1)
                        for c in range(DC):
                            last = nc.tensor.transpose(lin[:, 2 * (t % 2) + c // 4, (c % 4) * P:(c % 4) * P + n],
                                                       ctok[0:n, t % 2, c * P:(c + 1) * P], ident[0:n, 0:n])
                        last.then_inc(cb_t, 1)
                    pe.wait_ge(cb_acc, 5)
                else:
                    for e in range(SLICES[0]):
                        b = ffn_base(0) + e * (GU_P + DOWN_P)
                        stream(b, GU_P, kcs("gu"), (hh, hh), ready=(lambda k: pe.wait_ge(h_ready, DC + k + 1)) if e == 0 else None)
                        pe.wait_ge(gu_ok, GU_P * (e + 1))
                        if e == 0:
                            stream(b + GU_P, DOWN_P, kcs("down"), (gg, gg))
                        else:
                            stream(b + GU_P, DOWN_P, kcs("down"), (gg, gg),
                                   after_slab=lambda n: mean(5 * L + 3, n - 1) if n else None)
                            mean(5 * L + 3, DC - 1)
                if L:
                    norm(5 * L + 3)
                norm(5 * L + 4)
                stream(ple_base(L), PLE_P, kcs("ple"), (hh, pp), ready=lambda k: pe.wait_ge(h_ready, DC * (3 * L + 2) + k + 1))
            pe.wait_ge(pair_free[1], LAST_PAIR + 1)
            pe.wait_ge(ple_x, DC * DEPTH)
            for t in range(TT + 1):
                n = P if t < TT else NB
                if t:
                    pe.wait_ge(yt_ev, t)
                for c in range(DC):
                    last = nc.tensor.transpose(lin[0:n, c // 4, (c % 4) * P:(c % 4 + 1) * P], x[:, c, t * P:t * P + n], ident)
                last.then_inc(yt_t, 1)

        @block.scalar
        def _(act):
            def cp(out, in_, **k):
                return nc.scalar.activation(out, in_, ACT.Copy, **k)

            def split(q, par, s, kc):
                slot = 2 * par + s
                act.wait_ge(staged[slot], (q + (2 - par)) * 8)
                cp(whi[:, slot, 0:kc * P], wst[:, slot, 0:kc * P]).then_inc(hi_done, 1)

            def stream(base, pairs, kc, after, take, table=None, par=None):
                if table == ACT.Ln:
                    log_exp_table()
                elif table is not None:
                    nc.scalar.activation(spare[:, :], epsc[:, :], table)
                par = base % 2 if par is None else par
                def pair(q, i, par, nxt):
                    for s in range(2):
                        if nxt:
                            split(q + 1, 1 - par, s, nxt[s])
                        take(s, q, i)
                pair_loop(act, base, pairs - 1, par, lambda q, i, par: pair(q, i, par, kc))
                pair(base + (pairs - 1), pairs - 1, (par + pairs - 1) % 2, after)

            act.wait_ge(setup_pool, 1)
            act.wait_ge(cols_t, 1)
            cp(cols[:, :], aux[:, 3, 0:96]).then_inc(cols_ok, 1)
            for s in range(2):
                split(0, 0, s, DC)
            for c in range(DC):
                act.wait_ge(x_t, c + 1)
                cp(x[:, c, 0:SEQ], aux[:, c % 3, :]).then_inc(x_ok, 1)
            act.wait_ge(xs_t, 1)
            cp(x[:, :, SEQ:TOK], lin[:, 0, 0:DC * NB].rearrange("p (c b) -> p c b", b=NB)).then_inc(x_ok, 1)
            act.wait_ge(x_ok, DC + 1)

            def square(N, c, src):
                if N or c >= 4:
                    act.wait_ge(sq_used, N * DC + max(c - 3, 0))
                nc.scalar.activation(two(sq[:, c % 4]), src, ACT.Square).then_inc(sq_ready, 1)

            def root(N):
                act.wait_ge(sq_used, (N + 1) * DC)
                nc.scalar.activation(two(rn), aux[:, 0:2, 0:HALF], ACT.Ln, bias=epsc[:, :])
                act.drain()
                nc.scalar.activation(rn, rn, ACT.Exp, scale=-0.5).then_inc(r_ready, 1)

            def log_exp_table():
                act.add_instruction(mybir.InstLoadActFuncSet(name=nc.get_next_instruction_name(), act_func_set_id=LN_EXP_SET,
                                                             engine=mybir.EngineType.Activation, ins=[], outs=[]))

            def norm_x(N, ready=None):
                for c in range(DC):
                    if ready is not None:
                        ready(c)
                    square(N, c, two(x[:, c]))
                root(N)

            def added(N):
                def wait(c):
                    act.wait_ge((x_dve, x_pool)[c % 2], N * DC // 2 + c // 2 + 1)
                return wait

            def round_h(N, rows_too=False):
                for c in range(DC):
                    act.wait_ge(ht_ready, N * DC + c + 1)
                    cp(h_hi[:, c], ht[:, c % 2]).then_inc(h_hi_ok, 1)
                    if rows_too:
                        act.wait_ge(hx_t, c + 1)
                        cp(htok[:, 0:TT, c * P:(c + 1) * P], aux[:, 2 + c % 2, :].rearrange("p (t d) -> p t d", d=P))
                        cp(htok[0:NB, TT, c * P:(c + 1) * P], aux[0:NB, c % 2, 0:P]).then_inc(hx_ok, 1)

            def rsqrt(out, in_, eps=True):
                if eps:
                    nc.scalar.activation(out, in_, ACT.Ln, bias=epsc[:, :])
                else:
                    nc.scalar.activation(out, in_, ACT.Ln)
                act.drain()
                return nc.scalar.activation(out, out, ACT.Exp, scale=-0.5)

            for L in range(DEPTH):
                act.wait_ge(gw_in, 32 * (L + 1))
                cp(gwh[:, :], gwf[:, :]).then_inc(gw_ok, 1)
                log_exp_table()
                norm_x(5 * L, (lambda c: act.wait_ge(ple_x, DC * (L - 1) + c + 1)) if L else None)
                round_h(3 * L)
                act.wait_ge(gates, L + 1)
                if L == 0:
                    act.wait_ge(w_small, 16 * 23)
                nc.scalar.activation(two(rows[:, R_IG]), aux[0:H, 2:4, 0:HALF], ACT.Identity, bias=gate_b[:, 0, L:L + 1])
                cp(two(rows[:, R_F]), aux[32:32 + H, 2:4, 0:HALF])
                act.drain()
                nc.scalar.activation(rows[:, R_F], rows[:, R_F], ACT.Identity, bias=gate_b[:, 1, L:L + 1])
                act.drain()
                nc.scalar.activation(rows[:, R_EM], rows[:, R_F], ACT.Abs)
                act.drain()
                nc.scalar.activation(rows[:, R_EM], rows[:, R_EM], ACT.Exp, scale=-1.0)
                act.drain()
                nc.scalar.activation(rows[:, R_EM], rows[:, R_EM], ACT.Ln, bias=one[0:H]).then_inc(gate_l1, 1)

                def take_z(s, q, i):
                    act.wait_ge(pe_slab, q * 2 + (s + 1))
                    cp(z[:, bass.ds(i * 2 + s, 1)].rearrange("p a (b c) -> p (a b) c", c=HALF),
                       lin[:, 2 * s:2 * s + 2, 0:HALF]).then_inc(pair_free[s], 1)
                stream(win_base(L), WIN_P, kcs("win"), kcs("wout"), take_z)
                act.wait_ge(pair_free[0], wout_base(L))
                act.wait_ge(pair_free[1], wout_base(L))
                nc.scalar.activation(z[:, Z_O:Z_O + H], z[:, Z_O:Z_O + H], ACT.Sigmoid).then_inc(sig_o, 1)
                log_exp_table()
                act.wait_ge(pool_t, L + 1)
                if L:
                    act.wait_ge(out_st, 16 * 5 * L)
                cp(us[0:NB], aux[0:NB, 0, 0:2 * P].rearrange("p (a b) -> p a b", b=P)).then_inc(pool_e, 1)
                cp(us[32:32 + PST], aux[0:PST, 1, 0:2 * P].rearrange("p (a b) -> p a b", b=P)).then_inc(pool_e, 1)
                for j in range(2):
                    nc.scalar.activation(gr[:, j], z[:, Z_GV + j], ACT.Square).then_inc(g_sq, 1)
                for j in range(2):
                    act.wait_ge(g_mean, 2 * L + j + 1)
                    rsqrt(two(gr[:, j]), lin[:, 2:4, 0:HALF]).then_inc(g_r, 1)
                act.wait_ge(pool_mm, L + 1)
                for j in range(2):
                    ins = cp(two(z[:, Z_POOL + j]), aux[:, 2 * j:2 * j + 2, 0:HALF], scale=cols[:, 80 + 2 * L + j:81 + 2 * L + j])
                ins.then_inc(pool_y, 1)
                for j in range(2):
                    act.wait_ge(g_t, 3 * L + j + 1)
                    cp(vnt[:, j], lin[:, 2 + j, :].rearrange("p (i d) -> p i d", d=P)).then_inc(g_ev, 1)
                act.wait_ge(g_t, 3 * L + 3)
                cp(gvo[0:NB, :], lin[0:NB, 0, 0:2 * P]).then_inc(g_ev, 1)
                act.wait_ge(gate_g, L + 1)
                nc.scalar.activation(rows[:, R_EM], rows[:, R_M], ACT.Exp, scale=-1.0)
                nc.scalar.activation(rows[:, R_G, SEQ:TOK], rows[:, R_G, SEQ:TOK], ACT.Exp)
                nc.scalar.activation(rows[:, R_A, SEQ:TOK], rows[:, R_A, SEQ:TOK], ACT.Exp).then_inc(gate_em, 1)
                act.wait_ge(acol_t, L + 1)
                cp(acol[:, :, :], aux[:, 0, 0:TT * H].rearrange("p (i h) -> p i h", h=H)).then_inc(acol_ok, 1)
                act.wait_ge(st_t, L + 1)
                cp(vs[0:NB], aux[0:NB, 1, :].rearrange("p (h v) -> p h v", v=P))
                cp(dcs[:, :, :, :], aux[:, 2, 0:H * 3 * NB].rearrange("p (h n b) -> p h n b", n=3, b=NB))
                cp(nT[:, :, :], aux[:, 3, 0:NB * H].rearrange("p (b h) -> p b h", h=H)).then_inc(st_ev, 1)
                act.wait_ge(st_den, L + 1)
                nc.scalar.activation(D[:, :, SEQ:TOK], aux[:, 3, 0:H * NB].rearrange("p (h b) -> p h b", b=NB), ACT.Abs).then_inc(st_de, 1)
                cp(nout[0:NB * H, :], aux[0:NB * H, 2, 0:P]).then_inc(st_de, 1)
                act.wait_ge(out_st, 16 * (5 * L + 4))
                for b in range(NB):
                    n = NB * L + b
                    act.wait_ge(vb_ready, n + 1)
                    if b:
                        act.wait_ge(cn_ready, n)
                    for h in range(H):
                        ins = cp(Ct[:, h], lin[:, b % 2, h * P:(h + 1) * P], scale=kws[:, h, b:b + 1])
                    ins.then_inc(ct_ready, 1)
                act.wait_ge(cq_done, NB * (L + 1))
                cp(num[:, :, SEQ:TOK], lin[:, 2, 0:H * NB].rearrange("p (h b) -> p h b", b=NB)).then_inc(st_num, 1)
                for h in range(H):
                    hn = H * L + h
                    act.wait_ge(kv_t, hn + 1)
                    if h:
                        act.wait_ge(c_ready, hn)
                        act.wait_ge(kw_ready, TT * hn)
                    cp(vtok[:, :, 0:P], aux[:, 0, :].rearrange("p (i d) -> p i d", d=P))
                    if h == 0:
                        cp(vtok[:, :, P:P + 1], one.to_broadcast([P, TT]).rearrange("p (i a) -> p i a", a=1))
                    cp(ktok[:, :, :], aux[:, 1, :].rearrange("p (i d) -> p i d", d=P), scale=QS).then_inc(kv_ev, 1)
                    act.wait_ge(gb_ready, hn + 1)
                    for i in range(TT):
                        n = TT * hn + i
                        if n >= 2:
                            act.wait_ge(w_ready, n - 1)
                            act.wait_ge(kw_ready, n - 1)
                        nc.scalar.activation(E[:, i % 2, 0:SEQ - i * P], aux[:, 2, i * P:SEQ], ACT.Exp,
                                             bias=acol[:, i, h:h + 1]).then_inc(e_ready, 1)
                    act.wait_ge(w_used, TT * (hn + 1))
                    cp(num[:, h, 0:SEQ], aux[:, 0, :])
                    nc.scalar.activation(D[:, h, 0:SEQ], aux[:, 1, :], ACT.Abs).then_inc(nd_ev, 1)
                    act.wait_ge(c_ready, hn + 1)
                    if h:
                        act.wait_ge(c_out, 32 * hn)
                    elif L:
                        act.wait_ge(c_out, 32 * H * L)
                    cp(Cout[:, :], aux[:, 2, 0:P + 1]).then_inc(c_ev, 1)
                act.wait_ge(st_num, L + 1)
                act.wait_ge(nd_ev, H * (L + 1))
                for t in range(H + 2):
                    if t < H:
                        if t >= 2:
                            act.wait_ge(hr, H * L + t - 1)
                        nc.scalar.activation(hs1[t % 2], num[:, t], ACT.Square).then_inc(hq, 1)
                    if 1 <= t <= H:
                        h = t - 1
                        act.wait_ge(ha, H * L + h + 1)
                        if h >= 2:
                            act.wait_ge(hy, H * L + h - 1)
                        rsqrt(hs2[h % 2], hs1[h % 2], False).then_inc(hr, 1)
                    if t == 1:
                        act.wait_ge(g_y, L + 1)
                        act.wait_ge(m_out, 32 * (L + 1))
                        cp(y_hi[:, 0:2], z[:, Z_POOL:Z_POOL + 2]).then_inc(y_hi_ok, 1)
                        cp(y_hi[:, 6:8], z[:, Z_GU:Z_GU + 2]).then_inc(y_hi_ok, 1)
                    if t >= 2:
                        h = t - 2
                        act.wait_ge(hy2, H * L + h + 1)
                        cp(y_hi[:, 2 + h], z[:, Z_O + h]).then_inc(y_hi_ok, 1)

                def take_wout(s, q, i):
                    n = 2 * i + s
                    act.wait_ge(pe_slab, q * 2 + (s + 1))
                    square(5 * L + 1, n, lin[:, 2 * s:2 * s + 2, 0:HALF])
                    cp(two(acc[:, n]), lin[:, 2 * s:2 * s + 2, 0:HALF]).then_inc(pair_free[s], 1)
                    if n in P_AFTER:
                        j = P_AFTER.index(n)
                        act.wait_ge(p_t, 2 * L + j + 1)
                        cp(p_hi[:, j, 0:SEQ], aux[:, 2, :])
                        cp(p_hi[:, j, SEQ:TOK], aux[:, 3, 0:NB]).then_inc(p_hi_ok, 1)
                stream(wout_base(L), WOUT_P, kcs("wout"), kcs("gu"), take_wout)
                root(5 * L + 1)
                norm_x(5 * L + 2, added(2 * L))
                round_h(3 * L + 1, L == 1)
                if L:
                    act.wait_ge(rt_max, 1)
                    nc.scalar.activation(gwt[:, :, 1], gwt[:, :, 1], ACT.Sigmoid).then_inc(rt_e, 1)
                    act.wait_ge(rt_t, 1)
                    cp(grow[:, 0:SEQ], aux[0:NE, 3, :])
                    act.drain()
                    cp(grow[:, SEQ:TOK], aux[0:NE, 2, 0:NB]).then_inc(rt_row, 1)

                    def slots_hi(e, k):
                        act.wait_ge(xg_t, e * DC + (k + 1))
                        cp(xg[:, k, 0], aux[:, k % 2, 0:CAP]).then_inc(xg_hi, 1)

                    def expert(e, par, slots):
                        b = e * (GU_P + DOWN_P) + ffn_base(1)

                        def take_gu(s, q, i):
                            if s == 0:
                                act.wait_ge(pe_slab, q * 2 + 1)
                                if slots:
                                    act.wait_ge(pair_free[0], q + 1)
                                    ins = nc.scalar.activation(sg[:, 0:CAP], sg[:, 0:CAP], ACT.Silu)
                                else:
                                    ins = nc.scalar.activation(two(sg), lin[:, 0:2, 0:HALF], ACT.Silu)
                                ins.then_inc(silu_ok, 1)
                            else:
                                act.wait_ge(pair_free[1], q + 1)
                                if slots:
                                    ins = cp(gs[:, bass.ds(i, 1), 0].rearrange("p a t -> p (a t)"), gt[:, 0:CAP])
                                else:
                                    ins = cp(gu_hi[:, bass.ds(i, 1)].rearrange("p a t -> p (a t)"), gt)
                                ins.then_inc(gu_hi_ok, 1)
                        stream(b, GU_P, kcs("gu"), kcs("down"), take_gu, ACT.Silu, par)
                        for d in range(DC):
                            q, s = b + (GU_P + d // 2), d % 2
                            split(q + 1, (par + GU_P + d // 2 + 1) % 2, s, FCH if d < DC - 2 else DC)
                            slots_hi(e + 1, d)
                            if d == 0:
                                gate_row(e + 1)
                            if d:
                                rows_b(e, d - 1)
                        rows_b(e, DC - 1)

                    def rows_b(e, d):
                        if d == 0:
                            act.wait_ge(y_stored, e * 32 + 32)
                        act.wait_ge(yx_t, e * DC + (d + 1))
                        cp(ys0[:, d * P:(d + 1) * P], aux[:, 2 + d % 2, 0:P])
                        cp(ys1[0:CAP2, d * P:(d + 1) * P], aux[0:CAP2, 2 + d % 2, P:2 * P]).then_inc(ys_ok, 1)

                    def gate_row(e):
                        act.wait_ge(gb_mm, e + 1)
                        cp(two(gb), aux[:, 2:4, 0:HALF]).then_inc(gb_ok, 1)

                    gate_row(0)
                    for k in range(DC):
                        slots_hi(0, k)

                    def run(e, par):
                        fit = act.value_load(fitu[0:1, bass.ds(e, 1)], min_val=0, max_val=1)
                        with act.If(fit == 1):
                            expert(e, par, True)
                        with act.Else():
                            expert(e, par, False)

                    with act.Fori(0, NE // 2) as j:
                        for a in range(2):
                            run(j * 2 + a, expert_par(a))
                    for t in range(5):
                        n = P if t < TT else NB
                        act.wait_ge(y_back[t % 2], 32 * (t // 2 + 1))
                        if t >= 2:
                            act.wait_ge(cb_t, t - 1)
                        cp(ctok[0:n, t % 2, :], yrow[0:n, t % 2, 0, :], scale=gwt[0:n, t, 0:1]).then_inc(cb_a, 1)
                    act.wait_ge(cb_acc, 5)
                else:
                    for e in range(SLICES[0]):
                        b = ffn_base(0) + e * (GU_P + DOWN_P)

                        def take_gu0(s, q, i):
                            if s == 0:
                                act.wait_ge(pe_slab, q * 2 + 1)
                                nc.scalar.activation(two(sg), lin[:, 0:2, 0:HALF], ACT.Silu).then_inc(pair_free[0], 1)
                            else:
                                act.wait_ge(pair_free[1], q + 1)
                                cp(gu_hi[:, bass.ds(i, 1)].rearrange("p a t -> p (a t)"), gt).then_inc(gu_hi_ok, 1)
                        stream(b, GU_P, kcs("gu"), kcs("down"), take_gu0, ACT.Silu)

                        def square_acc(s, q, i):
                            act.wait_ge(pair_free[s], q + 1)
                            square(5 * L + 3, 2 * i + s, two(acc[:, 2 * i + s]))
                        if e == 0:
                            stream(b + GU_P, DOWN_P, kcs("down"), kcs("gu"), lambda s, q, i: None)
                        else:
                            stream(b + GU_P, DOWN_P, kcs("down"), kcs("ple"), square_acc, ACT.Ln)
                if L:
                    log_exp_table()
                    for c in range(DC):
                        square(5 * L + 3, c, two(acc[:, c]))
                root(5 * L + 3)
                norm_x(5 * L + 4, added(2 * L + 1))
                round_h(3 * L + 2)

                def take_ple(s, q, i):
                    if s == 0:
                        act.wait_ge(pe_slab, q * 2 + 1)
                        if not (isinstance(i, int) and i == 0):
                            act.wait_ge(pair_free[1], q)
                        nc.scalar.activation(two(sg), lin[:, 0:2, 0:HALF], ACT.Sigmoid).then_inc(pair_free[0], 1)
                stream(ple_base(L), PLE_P, kcs("ple"), kcs("win") if L < DEPTH - 1 else None, take_ple, ACT.Sigmoid)
            for t in range(TT + 1):
                n = P if t < TT else NB
                act.wait_ge(yt_t, t + 1)
                if t >= 2:
                    act.wait_ge(y_st[t % 2], 16 * (t // 2))
                cp(y_tok[0:n, t % 2, :], lin[0:n, 0:2, :].rearrange("p a b -> p (a b)")).then_inc(yt_ev, 1)

        @block.vector
        def _(dve):
            def tt(out, a, b, op):
                return nc.vector.tensor_tensor(out, a, b, op)

            def stt(out, a, s, b, op0, op1):
                return nc.vector.scalar_tensor_tensor(out=out, in0=a, scalar=s, in1=b, op0=op0, op1=op1)

            def split(q, par, s, kc):
                slot = 2 * par + s
                dve.wait_ge(hi_done, q * 2 + (s + 1))
                tt(wlo[:, slot, 0:kc * P], wst[:, slot, 0:kc * P], whi[:, slot, 0:kc * P].bitcast(f32),
                   ALU.subtract).then_inc(lo_done, 1)

            def stream(base, pairs, kc, after, take, par=None):
                par = base % 2 if par is None else par
                def pair(q, i, par, nxt, last=False):
                    for s in range(2):
                        rest = take(s, q, i)
                        if rest and last:
                            rest()
                        if nxt:
                            split(q + 1, 1 - par, s, nxt[s])
                        if rest and not last:
                            rest()
                pair_loop(dve, base, pairs - 1, par, lambda q, i, par: pair(q, i, par, kc))
                pair(base + (pairs - 1), pairs - 1, (par + pairs - 1) % 2, after, True)

            def nothing(s, q, i):
                pass

            def make_h(N, w, rows_too=False):
                def scaled(c):
                    stt(ht[:, c % 2], x[:, c], cols[:, w + c:w + c + 1], rn, ALU.mult, ALU.mult).then_inc(ht_ready, 1)
                scaled(0)
                for c in range(DC):
                    if c + 1 < DC:
                        if c:
                            dve.wait_ge(h_ready, N * DC + c)
                            if rows_too:
                                dve.wait_ge(hx_t, c)
                        scaled(c + 1)
                    dve.wait_ge(h_hi_ok, N * DC + c + 1)
                    dve.wait_ge(ht_ready, N * DC + c + 1)
                    tt(h_lo[:, c], ht[:, c % 2], h_hi[:, c].bitcast(f32), ALU.subtract).then_inc(h_ready, 1)

            def normed(N, w):
                for c in range(DC + 1):
                    if c < DC:
                        if N or c >= 2:
                            dve.wait_ge((x_dve, x_pool)[c % 2], N * DC // 2 + c // 2)
                        stt(ut[:, c % 2], acc[:, c], cols[:, w + c:w + c + 1], rn, ALU.mult, ALU.mult).then_inc(ut_ready, 1)
                    if c % 2:
                        dve.wait_ge(ut_ready, N * DC + c)
                        tt(x[:, c - 1], x[:, c - 1], ut[:, 0], ALU.add).then_inc(x_dve, 1)

            def add_rows(t):
                n = P if t < TT else NB
                dve.wait_ge(cb_t, t + 1)
                o = acc[:, :, t * P:t * P + n].rearrange("p (a c) t -> p a c t", a=2)
                i = lin[:, 2 * (t % 2):2 * (t % 2) + 2, :].rearrange("p a (c t) -> p a c t", t=P)[:, :, :, 0:n]
                tt(o, o, i, ALU.add).then_inc(cb_acc, 1)

            for s in range(2):
                split(0, 0, s, DC)
            dve.wait_ge(cols_ok, 1)
            dve.wait_ge(x_ok, DC + 1)
            for L in range(DEPTH):
                dve.wait_ge(gw_ok, L + 1)
                tt(gwl[:, :], gwf[:, :], gwh[:, :].bitcast(f32), ALU.subtract).then_inc(gw_lo, 1)
                dve.wait_ge(r_ready, 1 + 5 * L)
                make_h(3 * L, 8 * L)

                def scans(s, q, i):
                    if not (isinstance(i, int) and i == WIN_P - 3 and s == 0):
                        return
                    dve.wait_ge(gate_lf, L + 1)
                    nc.vector.tensor_tensor_scan(rows[:, R_G, 0:SEQ], rows[:, R_F, 0:SEQ], rows[:, R_A, 0:SEQ], 0.0, ALU.add, ALU.add)
                    nc.vector.tensor_tensor_scan(rows[:, R_M, 0:SEQ], rows[:, R_F, 0:SEQ], rows[:, R_IG, 0:SEQ], 0.0, ALU.add, ALU.max)
                    tt(rows[:, R_M, SEQ:TOK], tsm[:, :], rows[:, R_IG, SEQ:TOK], ALU.max).then_inc(gate_scan, 1)
                stream(win_base(L), WIN_P, kcs("win"), kcs("wout"), scans)
                dve.wait_ge(pool_win, L + 1)
                dve.wait_ge(pool_t, L + 1)
                for g, w in enumerate(WINDOWS):
                    lo, j = 64 * (g % 2), g // 2
                    old = aux[lo:lo + 64, 2, j * P:j * P + NB * PST].rearrange("p (b r) -> p b r", r=PST)[:, :, PST - w + 1:PST]
                    nc.vector.tensor_reduce(gsq[lo:lo + 64, j, SEQ:TOK], old, AXX, ALU.add)
                dve.drain()
                tt(gsq[:, :, SEQ:TOK], gsq[:, :, SEQ:TOK], z[:, Z_POOL:Z_POOL + 2, SEQ:TOK], ALU.add)
                dve.drain()
                for j in range(2):
                    last = stt(gsq[:, j, SEQ:TOK], gsq[:, j, SEQ:TOK], const[:, C_INVW + j:C_INVW + j + 1],
                               z[:, Z_POOL + j, SEQ:TOK], ALU.mult, ALU.subtract)
                last.then_inc(pool_v, 1)
                dve.wait_ge(g_wt, L + 1)
                tt(wmT[:, :, :], lin[:, 0, :].rearrange("p (g t) -> p g t", t=P),
                   tri.rearrange("p (a t) -> p a t", a=1).to_broadcast([P, 4, P]), ALU.mult).then_inc(g_wm, 1)
                for j in range(2):
                    dve.wait_ge(g_r, 2 * L + j + 1)
                    stt(z[:, Z_GV + j], z[:, Z_GV + j], cols[:, 92 + 2 * L + j:93 + 2 * L + j], gr[:, j], ALU.mult, ALU.mult).then_inc(g_vn, 1)
                dve.wait_ge(g_vn, 2 * L + 2)
                dve.wait_ge(pool_mm, L + 1)
                for j in range(2):
                    nc.vector.tensor_scalar(gsq[:, j, SEQ:TOK], z[:, Z_GV + j, SEQ:TOK], sg_b[:, 0, L, j:j + 1],
                                            sg_b[:, 1, L, j:j + 1], ALU.mult, ALU.add)
                dve.drain()
                for j in range(2):
                    dve.wait_ge(g_mix, 2 * L + j + 1)
                    tt(z[:, Z_GU + j, 0:SEQ], z[:, Z_GU + j, 0:SEQ], aux[:, j, :], ALU.mult)
                    last = tt(z[:, Z_GU + j, SEQ:TOK], z[:, Z_GU + j, SEQ:TOK], gsq[:, j, SEQ:TOK], ALU.mult)
                last.then_inc(g_y, 1)
                dve.wait_ge(st_ev, L + 1)
                nv = nn.rearrange("p b h -> p h b")
                stt(kws[:, :, :], z[:, Z_K:Z_K + H, SEQ:TOK], QS, dcs[:, :, 2, :], ALU.mult, ALU.mult)
                tt(nv, nT.rearrange("p b h -> p h b"), dcs[:, :, 1, :], ALU.mult)
                dve.drain()
                tt(nv, nv, kws[:, :, :], ALU.add)
                dve.drain()
                tt(qn[:, :, :], z[:, Z_Q:Z_Q + H, SEQ:TOK], nv, ALU.mult).then_inc(st_k, 1)
                dve.wait_ge(st_de, 2 * L + 1)
                tt(D[:, :, SEQ:TOK], D[:, :, SEQ:TOK], dcs[:, :, 0, :], ALU.max).then_inc(st_dd, 1)
                for b in range(NB):
                    dve.wait_ge(C_in[b % 3], 16 * ((3, 3, 2)[b % 3] * L + b // 3 + 1))
                    dve.wait_ge(ct_ready, NB * L + b + 1)
                    for h in range(H):
                        last = stt(Cb[:, b % 3, h], Cb[:, b % 3, h], dcs[:, h, 1, b:b + 1], Ct[:, h], ALU.mult, ALU.add)
                    last.then_inc(cn_ready, 1)
                for h in range(H):
                    hn = H * L + h
                    for i in range(TT):
                        n = TT * hn + i
                        dve.wait_ge(e_mask, n + 1)
                        dve.wait_ge(s_ready, n + 1)
                        if n >= 2:
                            dve.wait_ge(w_used, n - 1)
                        w = SEQ - i * P
                        stt(W[:, i % 2, 0:w], lin[:, i, 0:w], QS, E[:, i % 2, 0:w], ALU.mult, ALU.mult).then_inc(w_ready, 1)
                    dve.wait_ge(nd_ev, hn + 1)
                    tt(D[:, h, 0:SEQ], D[:, h, 0:SEQ], aux[:, 3, :], ALU.max).then_inc(nd_max, 1)
                for t in range(H + 2):
                    if t < H:
                        dve.wait_ge(hm, H * L + t + 1)
                        dve.wait_ge(hd2, H * L + t + 1)
                        stt(two(hs1[t % 2]), two(D[:, t]), EPS, aux[:, 2 * (t % 2):2 * (t % 2) + 2, 0:HALF], ALU.mult, ALU.add).then_inc(ha, 1)
                    if 1 <= t <= H:
                        h = t - 1
                        dve.wait_ge(hr, H * L + h + 1)
                        stt(num[:, h], num[:, h], cols[:, 84 + 4 * L + h:85 + 4 * L + h], hs2[h % 2], ALU.mult, ALU.mult).then_inc(hy, 1)
                    if t == 1:
                        for n, (at, src) in enumerate(((0, Z_POOL), (6, Z_GU))):
                            dve.wait_ge(y_hi_ok, Y_PARTS * L + n + 1)
                            tt(y_lo[:, at:at + 2], z[:, src:src + 2], y_hi[:, at:at + 2].bitcast(f32), ALU.subtract).then_inc(y_ok, 1)
                    if t >= 2:
                        h = t - 2
                        dve.wait_ge(y_hi_ok, Y_PARTS * L + h + 3)
                        tt(y_lo[:, 2 + h], z[:, Z_O + h], y_hi[:, 2 + h].bitcast(f32), ALU.subtract).then_inc(y_ok, 1)

                def lo_of_p(s, q, i):
                    n = 2 * i + s
                    if n in P_AFTER:
                        j = P_AFTER.index(n)
                        dve.wait_ge(p_hi_ok, 2 * L + j + 1)
                        tt(p_lo[:, j, 0:SEQ], aux[:, 2, :], p_hi[:, j, 0:SEQ].bitcast(f32), ALU.subtract)
                        tt(p_lo[:, j, SEQ:TOK], aux[:, 3, 0:NB], p_hi[:, j, SEQ:TOK].bitcast(f32), ALU.subtract).then_inc(p_ok, 1)
                stream(wout_base(L), WOUT_P, kcs("wout"), kcs("gu"), lo_of_p)
                dve.wait_ge(r_ready, 1 + 5 * L + 1)
                normed(2 * L, 16 + 8 * L)
                dve.wait_ge(r_ready, 1 + 5 * L + 2)
                make_h(3 * L + 1, 32 + 8 * L, L == 1)
                if L == 0:
                    nc.vector.tensor_copy(rwh[:, :, :], rwf[:, :, :])
                    dve.drain()
                    tt(rwl[:, :, :], rwf[:, :, :], rwh[:, :, :].bitcast(f32), ALU.subtract).then_inc(rw_lo, 1)
                else:
                    dve.wait_ge(rt_lg, 1)
                    rb8 = rbias[:, :].rearrange("p (a e) -> p a e", a=1)
                    tt(lg[:, 0:TT, :], aux[:, 2, 0:TT * NE].rearrange("p (t e) -> p t e", e=NE),
                       rb8.to_broadcast([P, TT, NE]), ALU.add)
                    tt(lg[0:NB, TT, :], aux[0:NB, 2, TT * NE:(TT + 1) * NE], rbias[0:NB, :], ALU.add)
                    dve.drain()
                    for t in range(5):
                        nc.vector.max(top[:, t], lg[:, t])
                    dve.drain()
                    for t in range(5):
                        nc.vector.max_index(topi[:, t], top[:, t], lg[:, t])
                    tt(gwt[:, :, 1], top[:, :, 1], top[:, :, 0], ALU.subtract).then_inc(rt_max, 1)
                    dve.drain()
                    nc.vector.tensor_copy(topf[:, :, :], topi[:, :, :])
                    dve.drain()
                    for t in range(5):
                        for k in range(2):
                            nc.vector.tensor_scalar(oh[:, k, t], iota8[:, :], topf[:, t, k:k + 1],
                                                    const[:, C_VAL + t:C_VAL + t + 1], ALU.is_equal, ALU.mult)
                    dve.drain()
                    tt(msk[:, :, :], oh[:, 0], oh[:, 1], ALU.add).then_inc(rt_oh, 1)
                    dve.wait_ge(rt_e, 1)
                    nc.vector.tensor_scalar(gwt[:, :, 0], gwt[:, :, 1], -1.0, 1.0, ALU.mult, ALU.add)
                    dve.drain()
                    for t in range(5):
                        nc.vector.tensor_scalar(gtmp[:, t], oh[:, 0, t], gwt[:, t, 0:1], None, ALU.mult)
                        nc.vector.tensor_scalar(gatet[:, t], oh[:, 1, t], gwt[:, t, 1:2], None, ALU.mult)
                    dve.drain()
                    tt(gatet[:, :, :], gatet[:, :, :], gtmp[:, :, :], ALU.add)
                    dve.wait_ge(rt_cnt, 1)
                    nc.vector.tensor_scalar(fits[:, :], aux[:, 3, 5 * NE:6 * NE], float(CAP), None, ALU.is_le)
                    nc.vector.tensor_scalar(rbias[:, :], iota8[:, :], float(CAP), float(-1 - NSLOT), ALU.mult, ALU.add)
                    dve.drain()
                    nc.vector.tensor_copy(fitu[:, :], fits[:, :])
                    tt(rel[:, :, :], aux[:, 3, 0:5 * NE].rearrange("p (t e) -> p t e", e=NE),
                       rb8.to_broadcast([P, 5, NE]), ALU.add)
                    dve.drain()
                    tt(rel[:, :, :], rel[:, :, :], fits[:, :].rearrange("p (a e) -> p a e", a=1).to_broadcast([P, 5, NE]), ALU.mult)
                    dve.drain()
                    for k in range(2):
                        tt(oh[:, k], oh[:, k], rel[:, :, :], ALU.mult)
                    dve.drain()
                    for k in range(2):
                        nc.vector.tensor_reduce(idxf[:, :, k], oh[:, k], AXX, ALU.add)
                    dve.drain()
                    nc.vector.tensor_scalar(idxf[:, :, :], idxf[:, :, :], float(NSLOT), None, ALU.add)
                    dve.drain()
                    nc.vector.tensor_copy(idxu[:, :, :], idxf[:, :, :]).then_inc(rt_idx, 1)
                    dve.wait_ge(rt_idx, 1)
                    nc.vector.tensor_copy(gtmp[:, :, :], gatet[:, :, :]).then_inc(rt_gate, 1)
                dve.wait_ge(acc0, L + 1)
                if L:
                    def both(out, s):
                        return nc.vector.tensor_reduce(out, lin[:, 2 * s, 0:2 * CAP].rearrange("p (a t) -> p t a", a=2),
                                                       AXX, ALU.add)

                    def slots_lo(e, k):
                        dve.wait_ge(xg_hi, e * DC + (k + 1))
                        tt(xg[:, k, 1], aux[:, k % 2, 0:CAP], xg[:, k, 0].bitcast(f32), ALU.subtract).then_inc(xg_ok, 1)

                    def expert(e, par, slots):
                        b = e * (GU_P + DOWN_P) + ffn_base(1)

                        def take_gu(s, q, i):
                            if s == 0:
                                if slots:
                                    dve.wait_ge(pe_slab, q * 2 + 1)
                                    both(sg[:, 0:CAP], 0).then_inc(pair_free[0], 1)
                                return
                            if not slots:
                                dve.drain()
                            dve.wait_ge(pe_slab, q * 2 + 2)
                            if slots:
                                both(gt[:, CAP:2 * CAP], 1)
                                dve.drain()
                            dve.wait_ge(silu_ok, e * GU_P + (i + 1))
                            if slots:
                                tt(gt[:, 0:CAP], sg[:, 0:CAP], gt[:, CAP:2 * CAP], ALU.mult).then_inc(pair_free[1], 1)
                                src, hi, lo = gt[:, 0:CAP], gs[:, bass.ds(i, 1), 0], gs[:, bass.ds(i, 1), 1]
                            else:
                                dve.wait_ge(gb_ok, e + 1)
                                tt(two(gt), two(sg), lin[:, 2:4, 0:HALF], ALU.mult).then_inc(pair_free[0], 1)
                                dve.drain()
                                tt(gt, gt, gb, ALU.mult).then_inc(pair_free[1], 1)
                                src, hi, lo = gt, gu_hi[:, bass.ds(i, 1)], gu_lo[:, bass.ds(i, 1)]

                            def rest():
                                dve.wait_ge(gu_hi_ok, e * GU_P + (i + (GU_P * SLICES[0] + 1)))
                                tt(lo.rearrange("p a t -> p (a t)"), src, hi.rearrange("p a t -> p (a t)").bitcast(f32),
                                   ALU.subtract).then_inc(gu_ok, 1)
                            return rest
                        stream(b, GU_P, kcs("gu"), kcs("down"), take_gu, par)
                        for d in range(DC):
                            q, s = b + (GU_P + d // 2), d % 2
                            split(q + 1, (par + GU_P + d // 2 + 1) % 2, s, FCH if d < DC - 2 else DC)
                            if d == 0:
                                pick_row(e + 1)
                            slots_lo(e + 1, d)
                            dve.wait_ge(pe_slab, q * 2 + (s + 1))
                            if slots:
                                if d >= 2:
                                    dve.wait_ge(yx_t, e * DC + (d - 1))
                                both(ytb[:, s], s).then_inc(pair_free[s], 1)
                            else:
                                tt(two(acc[:, d]), two(acc[:, d]), lin[:, 2 * s:2 * s + 2, 0:HALF], ALU.add).then_inc(pair_free[s], 1)

                    def pick_row(e):
                        nc.vector.tensor_copy(pick_e[:, :], ident[0:NE, bass.ds(e, 1)].to_broadcast([NE, P])).then_inc(pk, 1)

                    pick_row(0)
                    for k in range(DC):
                        slots_lo(0, k)

                    def run(e, par):
                        fit = dve.value_load(fitu[0:1, bass.ds(e, 1)], min_val=0, max_val=1)
                        with dve.If(fit == 1):
                            expert(e, par, True)
                        with dve.Else():
                            expert(e, par, False)

                    with dve.Fori(0, NE // 2) as j:
                        for a in range(2):
                            run(j * 2 + a, expert_par(a))
                    for t in range(5):
                        n = P if t < TT else NB
                        dve.wait_ge(cb_a, t + 1)
                        stt(ctok[0:n, t % 2, :], yrow[0:n, t % 2, 1, :], gwt[0:n, t, 1:2], ctok[0:n, t % 2, :], ALU.mult, ALU.add).then_inc(cb_b, 1)
                        if t:
                            add_rows(t - 1)
                    add_rows(4)
                else:
                    for e in range(SLICES[0]):
                        b = ffn_base(0) + e * (GU_P + DOWN_P)

                        def take_gu0(s, q, i):
                            if s == 0:
                                return
                            dve.drain()
                            dve.wait_ge(pe_slab, q * 2 + 2)
                            dve.wait_ge(pair_free[0], q + 1)
                            tt(two(gt), two(sg), lin[:, 2:4, 0:HALF], ALU.mult).then_inc(pair_free[1], 1)

                            def rest():
                                dve.wait_ge(gu_hi_ok, i + (GU_P * e + 1))
                                tt(gu_lo[:, bass.ds(i, 1)].rearrange("p a t -> p (a t)"), gt,
                                   gu_hi[:, bass.ds(i, 1)].rearrange("p a t -> p (a t)").bitcast(f32), ALU.subtract).then_inc(gu_ok, 1)
                            return rest

                        def take_down0(s, q, i):
                            dve.wait_ge(pe_slab, q * 2 + (s + 1))
                            o = acc[:, bass.ds(i * 2 + s, 1)].rearrange("p a (b c) -> p (a b) c", c=HALF)
                            tt(o, o, lin[:, 2 * s:2 * s + 2, 0:HALF], ALU.add).then_inc(pair_free[s], 1)
                        stream(b, GU_P, kcs("gu"), kcs("down"), take_gu0)
                        stream(b + GU_P, DOWN_P, kcs("down"), kcs("gu") if e == 0 else kcs("ple"), take_down0)
                dve.wait_ge(r_ready, 1 + 5 * L + 3)
                normed(2 * L + 1, 48 + 8 * L)
                dve.wait_ge(r_ready, 1 + 5 * L + 4)
                make_h(3 * L + 2, 64 + 8 * L)

                def take_ple(s, q, i):
                    if s == 0:
                        return
                    dve.drain()
                    dve.wait_ge(pe_slab, q * 2 + 2)
                    dve.wait_ge(pair_free[0], q + 1)
                    tt(two(gt), two(sg), lin[:, 2:4, 0:HALF], ALU.mult).then_inc(pair_free[1], 1)
                    dve.drain()
                    xd = x[:, bass.ds(i, 1)].rearrange("p a t -> p (a t)")
                    tt(xd, xd, gt, ALU.add).then_inc(ple_x, 1)
                stream(ple_base(L), PLE_P, kcs("ple"), kcs("win") if L < DEPTH - 1 else None, take_ple)


_INS = ["x_prompt", "x_sample", "state_pool", "state_mlstm_C", "state_mlstm_n", "state_mlstm_m", "p_prompt", "p_sample",
        "norm_mix_pre", "norm_mix_post", "norm_ffn_pre", "norm_ffn_post", "norm_ple", "w_in", "pool_w", "pool_scale",
        "mlstm_b_i", "mlstm_b_f", "mlstm_norm_w", "gmlp_norm_w", "gmlp_ws", "gmlp_bs", "w_out", "ffn_w_gate",
        "ffn_w_up", "ffn_w_down", "moe_router_w", "moe_router_b", "moe_w_gate", "moe_w_up", "moe_w_down",
        "ple_w_gate", "ple_w_proj"]
_OUTS = [("y_prompt", (1, SEQ, DM)), ("y_sample", (NB, 1, DM)),
         ("new_pool_prompt", (DEPTH, 1, PST, 256)), ("new_C_prompt", (DEPTH, 1, H, DH, DH)),
         ("new_n_prompt", (DEPTH, 1, H, DH)), ("new_m_prompt", (DEPTH, 1, H)),
         ("new_pool_sample", (DEPTH, NB, PST, 256)), ("new_C_sample", (DEPTH, NB, H, DH, DH)),
         ("new_n_sample", (DEPTH, NB, H, DH)), ("new_m_sample", (DEPTH, NB, H)),
         ("new_gmlp_v_sample", (DEPTH, NB, 1, 256))]


def kernel(**inputs):
    import numpy as np
    import concourse.bacc as bacc
    from concourse import mybir as mb
    from concourse.bass_utils import run_bass_kernel_spmd

    const = np.zeros((P, NCONST), np.float32)
    const[:, C_ID:C_ID + P] = np.eye(P)
    const[:64, C_BLK:C_BLK + 64] = 1 / 64
    const[64:, C_BLK + 64:C_BLK + P] = 1 / 64
    const[:, C_TRI:C_TRI + P] = np.triu(np.ones((P, P)))
    const[:, C_ONE], const[:, C_MEAN], const[:, C_MEANH] = 1, 1 / DM, 1 / DH
    const[:, C_VAL:C_VAL + TT], const[:NB, C_VAL + TT] = 1, 1
    for g, w in enumerate(WINDOWS):
        rows, j = slice(64 * (g % 2), 64 * (g % 2) + 64), g // 2
        const[rows, C_INVW + j] = 1 / w
        const[rows, C_RC + 16 * j:C_RC + 16 * j + 16] = 1 / np.minimum(w, np.arange(16) + 1)

    nc = bacc.Bacc("TRN2", target_bir_lowering=False, num_devices=1)
    arrays, A, O = {}, {}, {}
    for name in _INS + ["shape_constants"]:
        a = np.ascontiguousarray(const if name == "shape_constants" else inputs[name])
        arrays[f"in_{name}"] = a
        A[name] = nc.dram_tensor(f"in_{name}", a.shape, mb.dt.from_np(a.dtype), kind="ExternalInput").ap()
    for name, shape in _OUTS:
        O[name] = nc.dram_tensor(f"out_{name}", shape, mb.dt.float32, kind="ExternalOutput").ap()
    build(nc, A, O)
    r = run_bass_kernel_spmd(nc, [arrays], core_ids=[0])
    return tuple(r.results[0][f"out_{name}"] for name, _ in _OUTS)
```
